# Optimizing a Trainium2 kernel written in Bass

```python
import math
import jax, jax.numpy as jnp
from jax import lax
import numpy as np

D_MODEL = 1024
BATCH = 1
SEQ = 256
DEPTH = 2

N_A = DEPTH // 2
N_B = DEPTH - N_A
CONV_W = 3
HEAD_DIM = 64
N_HEADS = D_MODEL // HEAD_DIM
N_KV_HEADS = 4
GROUP = N_HEADS // N_KV_HEADS
WINDOW = 128
BLOCK = 128
ROT_DIM = HEAD_DIM // 4
ROPE_THETA = 500000.0
D_FF = ((8 * D_MODEL // 3 + 255) // 256) * 256
EPS = 1e-6
NEG = -1e30


def rmsnorm(x, g):
    xf = x.astype(jnp.float32)
    r = lax.rsqrt(jnp.mean(xf * xf, axis=-1, keepdims=True) + EPS)
    return (xf * r).astype(x.dtype) * g

def rope_tables(seq_len, dtype):
    inv_freq = ROPE_THETA ** (-jnp.arange(0, ROT_DIM, 2, dtype=jnp.float32) / ROT_DIM)
    ang = jnp.arange(seq_len, dtype=jnp.float32)[:, None] * inv_freq[None, :]
    return jnp.cos(ang)[:, None, :].astype(dtype), jnp.sin(ang)[:, None, :].astype(dtype)

def partial_rotary(t, cos, sin):
    half = ROT_DIM // 2
    t1, t2, rest = t[..., :half], t[..., half:ROT_DIM], t[..., ROT_DIM:]
    return jnp.concatenate([t1 * cos - t2 * sin, t2 * cos + t1 * sin, rest], axis=-1)

def causal_depthwise_conv3(u, w):
    s = u.shape[1]
    up = jnp.pad(u, ((0, 0), (CONV_W - 1, 0), (0, 0)))
    return up[:, 0:s] * w[0] + up[:, 1:s + 1] * w[1] + up[:, 2:s + 2] * w[2]

def short_conv_mixer(h, w_in, conv_w, w_out):
    bcx = h @ w_in
    b_gate, c_gate, u = jnp.split(bcx, 3, axis=-1)
    y = b_gate * causal_depthwise_conv3(c_gate * u, conv_w)
    return y @ w_out

def swiglu(h, w_gate_up, w_down):
    g, u = jnp.split(h @ w_gate_up, 2, axis=-1)
    return (jax.nn.silu(g) * u) @ w_down

def sliding_window_sink_attention(q, k, v, sinks):
    bsz, s = q.shape[0], q.shape[1]
    nb = s // BLOCK
    qb = q.reshape(bsz, nb, BLOCK, N_KV_HEADS, GROUP, HEAD_DIM)

    def with_prev(t):
        tb = t.reshape(bsz, nb, BLOCK, N_KV_HEADS, HEAD_DIM)
        prev = jnp.concatenate([jnp.zeros_like(tb[:, :1]), tb[:, :-1]], axis=1)
        return jnp.concatenate([prev, tb], axis=2)

    kk, vv = with_prev(k), with_prev(v)
    scale = 1.0 / math.sqrt(HEAD_DIM)
    scores = jnp.einsum('bnqhgd,bnkhd->bnhgqk', qb, kk).astype(jnp.float32) * scale

    qi = jnp.arange(BLOCK)[:, None]
    kj = jnp.arange(2 * BLOCK)[None, :]
    diff = BLOCK + qi - kj
    band = (diff >= 0) & (diff < WINDOW)
    not_pad = (jnp.arange(nb)[:, None, None] > 0) | (kj[None] >= BLOCK)
    valid = band[None] & not_pad
    scores = jnp.where(valid[None, :, None, None], scores, NEG)

    sink = jnp.broadcast_to(
        sinks.astype(jnp.float32).reshape(N_KV_HEADS, GROUP)[None, None, :, :, None, None],
        scores.shape[:-1] + (1,))
    probs = jax.nn.softmax(jnp.concatenate([scores, sink], axis=-1), axis=-1)[..., :-1]
    out = jnp.einsum('bnhgqk,bnkhd->bnqhgd', probs.astype(v.dtype), vv)
    return out.reshape(bsz, s, N_HEADS * HEAD_DIM)

def first_inputs(seed: int = 0) -> dict:
    key = jax.random.key(seed)
    ks = jax.random.split(key, 24)
    f32 = jnp.float32
    D, F = D_MODEL, D_FF
    QD = N_HEADS * HEAD_DIM
    KVD = N_KV_HEADS * HEAD_DIM

    def nrm(k, shape, fan_in):
        return jax.random.normal(k, shape, f32) * (fan_in ** -0.5)

    def gain(k, shape):
        return 1.0 + 0.05 * jax.random.normal(k, shape, f32)

    return {
        "x": jax.random.normal(ks[0], (BATCH, SEQ, D), f32),
        "a_pre_norm": gain(ks[1], (N_A, D)),
        "a_w_in": nrm(ks[2], (N_A, D, 3 * D), D),
        "a_conv_w": nrm(ks[3], (N_A, CONV_W, D), CONV_W),
        "a_w_out": nrm(ks[4], (N_A, D, D), D),
        "a_post_norm": gain(ks[5], (N_A, D)),
        "ffn_pre_norm": gain(ks[6], (DEPTH, D)),
        "ffn_w_gate_up": nrm(ks[7], (DEPTH, D, 2 * F), D),
        "ffn_w_down": nrm(ks[8], (DEPTH, F, D), F),
        "ffn_post_norm": gain(ks[9], (DEPTH, D)),
        "kv_norm": gain(ks[10], (D,)),
        "w_kv": nrm(ks[11], (D, 2 * KVD), D),
        "b_pre_norm": gain(ks[12], (N_B, D)),
        "b_w_q": nrm(ks[13], (N_B, D, QD), D),
        "b_sinks": 0.5 * jax.random.normal(ks[14], (N_B, N_HEADS), f32),
        "b_w_o": nrm(ks[15], (N_B, QD, D), QD),
        "b_post_norm": gain(ks[16], (N_B, D)),
    }

def first_block(x, a_pre_norm, a_w_in, a_conv_w, a_w_out, a_post_norm,
              ffn_pre_norm, ffn_w_gate_up, ffn_w_down, ffn_post_norm,
              kv_norm, w_kv,
              b_pre_norm, b_w_q, b_sinks, b_w_o, b_post_norm):
    bsz, s, _ = x.shape
    cos, sin = rope_tables(s, x.dtype)
    h = x
    for l in range(DEPTH):
        if l < N_A:
            mix = short_conv_mixer(rmsnorm(h, a_pre_norm[l]), a_w_in[l], a_conv_w[l], a_w_out[l])
            h = h + rmsnorm(mix, a_post_norm[l])
        else:
            j = l - N_A
            if j == 0:
                kv = rmsnorm(h, kv_norm) @ w_kv
                k_sh, v_sh = jnp.split(kv, 2, axis=-1)
                k_sh = partial_rotary(k_sh.reshape(bsz, s, N_KV_HEADS, HEAD_DIM), cos, sin)
                v_sh = v_sh.reshape(bsz, s, N_KV_HEADS, HEAD_DIM)
            q = (rmsnorm(h, b_pre_norm[j]) @ b_w_q[j]).reshape(bsz, s, N_HEADS, HEAD_DIM)
            q = partial_rotary(q, cos, sin)
            attn = sliding_window_sink_attention(q, k_sh, v_sh, b_sinks[j]) @ b_w_o[j]
            h = h + rmsnorm(attn, b_post_norm[j])
        ff = swiglu(rmsnorm(h, ffn_pre_norm[l]), ffn_w_gate_up[l], ffn_w_down[l])
        h = h + rmsnorm(ff, ffn_post_norm[l])
    return h


N_MIXERS = 2
DN_HEADS = 8
DN_HEAD_DIM = 128
DN_DIM = DN_HEADS * DN_HEAD_DIM
DN_CONV = 4
DN_CHUNK = 64
DN_IN = 4 * DN_DIM + 2 * DN_HEADS
MB_HEADS = 8
MB_HEAD_DIM = D_MODEL // MB_HEADS
MB_DIM = MB_HEADS * MB_HEAD_DIM
MB_BLOCK = 256
MB_TOPK = 3
MB_QCHUNK = 16
D_FF_2 = 4 * D_MODEL
RMS_EPS = 1e-6
N_DN_LAYERS = (DEPTH + 1) // 2
N_MB_LAYERS = DEPTH // 2


def rmsnorm_2(x, g):
    xf = x.astype(jnp.float32)
    y = xf * lax.rsqrt(jnp.mean(xf * xf, axis=-1, keepdims=True) + RMS_EPS)
    return (y * g.astype(jnp.float32)).astype(x.dtype)

def l2norm(x):
    xf = x.astype(jnp.float32)
    return xf * lax.rsqrt(jnp.sum(xf * xf, axis=-1, keepdims=True) + 1e-6)

def causal_depthwise_conv(x, w):
    k_w = w.shape[0]
    t = x.shape[1]
    xp = jnp.pad(x, ((0, 0), (k_w - 1, 0), (0, 0)))
    y = xp[:, 0:t] * w[0]
    for j in range(1, k_w):
        y = y + xp[:, j:j + t] * w[j]
    return y

def alibi_slopes(n_heads):
    return jnp.exp2(-8.0 * jnp.arange(1, n_heads + 1, dtype=jnp.float32) / n_heads)

def chunk_gated_delta_rule(q, k, v, g, beta):
    b, h, t, dk = q.shape
    dv = v.shape[-1]
    c = DN_CHUNK
    n = t // c
    q = q.astype(jnp.float32).reshape(b, h, n, c, dk)
    k = k.astype(jnp.float32).reshape(b, h, n, c, dk)
    v = v.astype(jnp.float32).reshape(b, h, n, c, dv)
    g = g.astype(jnp.float32).reshape(b, h, n, c)
    beta = beta.astype(jnp.float32).reshape(b, h, n, c)

    gc = jnp.cumsum(g, axis=-1)
    idx = jnp.arange(c)
    tri_incl = idx[:, None] >= idx[None, :]
    tri_strict = idx[:, None] > idx[None, :]
    decay = jnp.exp(jnp.where(tri_incl, gc[..., :, None] - gc[..., None, :], -jnp.inf))

    k_beta = k * beta[..., None]
    a_low = jnp.where(tri_strict, jnp.einsum('bhncd,bhnsd->bhncs', k_beta, k) * decay, 0.0)
    a_mat = a_low + jnp.eye(c, dtype=jnp.float32)
    rhs = jnp.concatenate([v * beta[..., None], k_beta * jnp.exp(gc)[..., None]], axis=-1)
    sol = lax.linalg.triangular_solve(a_mat, rhs, left_side=True, lower=True, unit_diagonal=True)
    u, w = sol[..., :dv], sol[..., dv:]

    attn_intra = jnp.einsum('bhncd,bhnsd->bhncs', q, k) * decay
    q_dec = q * jnp.exp(gc)[..., None]
    k_dec = k * jnp.exp(gc[..., -1:] - gc)[..., None]
    g_tot = jnp.exp(gc[..., -1])

    xs = tuple(jnp.moveaxis(a, 2, 0) for a in (u, w, q_dec, k_dec, attn_intra, g_tot))

    def step(state, inp):
        u_c, w_c, qd_c, kd_c, at_c, gt_c = inp
        v_new = u_c - jnp.einsum('bhcd,bhde->bhce', w_c, state)
        o_c = jnp.einsum('bhcd,bhde->bhce', qd_c, state) + jnp.einsum('bhcs,bhse->bhce', at_c, v_new)
        state = state * gt_c[..., None, None] + jnp.einsum('bhcd,bhce->bhde', kd_c, v_new)
        return state, o_c

    s0 = jnp.zeros((b, h, dk, dv), jnp.float32)
    _, o = lax.scan(step, s0, xs)
    return jnp.moveaxis(o, 0, 2).reshape(b, h, t, dv)

def gated_deltanet(hn, w_in, conv_w, a_log, dt_bias, out_norm_g, w_out):
    b, t, _ = hn.shape
    proj = hn @ w_in
    qkv = jax.nn.silu(causal_depthwise_conv(proj[..., :3 * DN_DIM], conv_w))
    z = proj[..., 3 * DN_DIM:4 * DN_DIM]
    b_raw = proj[..., 4 * DN_DIM:4 * DN_DIM + DN_HEADS].astype(jnp.float32)
    a_raw = proj[..., 4 * DN_DIM + DN_HEADS:].astype(jnp.float32)

    def heads(a):
        return a.reshape(b, t, DN_HEADS, DN_HEAD_DIM).transpose(0, 2, 1, 3)

    q = heads(l2norm(heads(qkv[..., :DN_DIM]).transpose(0, 2, 1, 3)) * DN_HEAD_DIM ** -0.5)
    k = heads(l2norm(heads(qkv[..., DN_DIM:2 * DN_DIM]).transpose(0, 2, 1, 3)))
    v = heads(qkv[..., 2 * DN_DIM:])
    beta = jax.nn.sigmoid(b_raw).transpose(0, 2, 1)
    g = (-jnp.exp(a_log.astype(jnp.float32)) *
         jax.nn.softplus(a_raw + dt_bias.astype(jnp.float32))).transpose(0, 2, 1)
    o = chunk_gated_delta_rule(q, k, v, g, beta)
    o = o.transpose(0, 2, 1, 3).astype(hn.dtype)
    o = rmsnorm_2(o, out_norm_g) * jax.nn.silu(z.reshape(b, t, DN_HEADS, DN_HEAD_DIM))
    return o.reshape(b, t, DN_DIM) @ w_out

def moba_attention(q, k, v):
    b, h, t, dh = q.shape
    nb = -(-t // MB_BLOCK)
    tp = nb * MB_BLOCK
    pad = ((0, 0), (0, 0), (0, tp - t), (0, 0))
    q, k, v = jnp.pad(q, pad), jnp.pad(k, pad), jnp.pad(v, pad)
    kb = k.reshape(b, h, nb, MB_BLOCK, dh)
    vb = v.reshape(b, h, nb, MB_BLOCK, dh)
    top = min(MB_TOPK, nb)
    scale = dh ** -0.5
    slopes = alibi_slopes(h)

    k_mean = jnp.mean(kb.astype(jnp.float32), axis=3)
    gate = jnp.einsum('bhtd,bhnd->bhtn', q.astype(jnp.float32), k_mean)
    q_blk = jnp.arange(tp) // MB_BLOCK
    past = jnp.arange(nb)[None, :] < q_blk[:, None]
    gate = jnp.where(past, gate, -jnp.inf)
    _, sel = lax.top_k(gate, top)
    valid = sel < q_blk[:, None]

    n_qc = tp // MB_QCHUNK

    def to_chunks(a):
        return jnp.moveaxis(a.reshape(b, h, n_qc, MB_QCHUNK, *a.shape[3:]), 2, 0)

    gather_blocks = jax.vmap(jax.vmap(lambda blocks, ids: blocks[ids]))

    def attend_chunk(args):
        qc, selc, validc, ci = args
        t0 = ci * MB_QCHUNK
        blk = t0 // MB_BLOCK
        tpos = (t0 + jnp.arange(MB_QCHUNK)).astype(jnp.float32)
        ks = gather_blocks(kb, selc)
        vs = gather_blocks(vb, selc)
        s_sel = jnp.einsum('bhqd,bhqnld->bhqnl', qc, ks).astype(jnp.float32) * scale
        kpos_sel = (selc[..., None] * MB_BLOCK + jnp.arange(MB_BLOCK)).astype(jnp.float32)
        dist_sel = tpos[:, None, None] - kpos_sel
        s_sel = jnp.where(validc[..., None], s_sel - slopes[:, None, None, None] * dist_sel, -jnp.inf)
        ko = lax.dynamic_index_in_dim(kb, blk, axis=2, keepdims=False)
        vo = lax.dynamic_index_in_dim(vb, blk, axis=2, keepdims=False)
        s_own = jnp.einsum('bhqd,bhld->bhql', qc, ko).astype(jnp.float32) * scale
        dist_own = tpos[:, None] - (blk * MB_BLOCK + jnp.arange(MB_BLOCK)).astype(jnp.float32)
        s_own = jnp.where(dist_own >= 0, s_own - slopes[:, None, None] * dist_own, -jnp.inf)
        logits = jnp.concatenate([s_sel.reshape(b, h, MB_QCHUNK, top * MB_BLOCK), s_own], axis=-1)
        p = jax.nn.softmax(logits, axis=-1).astype(vs.dtype)
        p_sel = p[..., :top * MB_BLOCK].reshape(b, h, MB_QCHUNK, top, MB_BLOCK)
        p_own = p[..., top * MB_BLOCK:]
        return (jnp.einsum('bhqnl,bhqnld->bhqd', p_sel, vs) +
                jnp.einsum('bhql,bhld->bhqd', p_own, vo))

    out = lax.map(attend_chunk, (to_chunks(q), to_chunks(sel), to_chunks(valid), jnp.arange(n_qc)))
    out = jnp.moveaxis(out, 0, 2).reshape(b, h, tp, dh)
    return out[:, :, :t]

def moba_layer(hn, w_in, w_out):
    b, t, _ = hn.shape
    proj = hn @ w_in

    def heads(a):
        return a.reshape(b, t, MB_HEADS, MB_HEAD_DIM).transpose(0, 2, 1, 3)

    q = heads(proj[..., :MB_DIM])
    k = heads(proj[..., MB_DIM:2 * MB_DIM])
    v = heads(proj[..., 2 * MB_DIM:])
    o = moba_attention(q, k, v)
    return o.transpose(0, 2, 1, 3).reshape(b, t, MB_DIM) @ w_out

def squared_relu_mlp(hn, w_up, w_down):
    return jnp.square(jax.nn.relu(hn @ w_up)) @ w_down

def second_inputs(seed: int = 0) -> dict:
    key = jax.random.key(seed)
    ks = jax.random.split(key, 16)
    f32 = jnp.float32
    x = jax.random.normal(ks[0], (BATCH, SEQ, D_MODEL), f32)
    mix_norm_g = 1.0 + 0.02 * jax.random.normal(ks[1], (DEPTH, D_MODEL), f32)
    mlp_norm_g = 1.0 + 0.02 * jax.random.normal(ks[2], (DEPTH, D_MODEL), f32)
    dn_w_in = jax.random.normal(ks[3], (N_DN_LAYERS, D_MODEL, DN_IN), f32) * D_MODEL ** -0.5
    dn_conv_w = jax.random.normal(ks[4], (N_DN_LAYERS, DN_CONV, 3 * DN_DIM), f32) * DN_CONV ** -0.5
    dn_a_log = jnp.log(jax.random.uniform(ks[5], (N_DN_LAYERS, DN_HEADS), f32, 1.0, 16.0))
    dt = jnp.exp(jax.random.uniform(ks[6], (N_DN_LAYERS, DN_HEADS), f32, math.log(1e-3), math.log(1e-1)))
    dn_dt_bias = dt + jnp.log(-jnp.expm1(-dt))
    dn_out_norm_g = 1.0 + 0.02 * jax.random.normal(ks[7], (N_DN_LAYERS, DN_HEAD_DIM), f32)
    dn_w_out = jax.random.normal(ks[8], (N_DN_LAYERS, DN_DIM, D_MODEL), f32) * DN_DIM ** -0.5
    mb_w_in = jax.random.normal(ks[9], (N_MB_LAYERS, D_MODEL, 3 * MB_DIM), f32) * D_MODEL ** -0.5
    mb_w_out = jax.random.normal(ks[10], (N_MB_LAYERS, MB_DIM, D_MODEL), f32) * MB_DIM ** -0.5
    mlp_w_up = jax.random.normal(ks[11], (DEPTH, D_MODEL, D_FF_2), f32) * D_MODEL ** -0.5
    mlp_w_down = jax.random.normal(ks[12], (DEPTH, D_FF_2, D_MODEL), f32) * D_FF_2 ** -0.5
    final_norm_g = 1.0 + 0.02 * jax.random.normal(ks[13], (D_MODEL,), f32)
    return {"x": x, "mix_norm_g": mix_norm_g, "mlp_norm_g": mlp_norm_g,
            "dn_w_in": dn_w_in, "dn_conv_w": dn_conv_w, "dn_a_log": dn_a_log,
            "dn_dt_bias": dn_dt_bias, "dn_out_norm_g": dn_out_norm_g, "dn_w_out": dn_w_out,
            "mb_w_in": mb_w_in, "mb_w_out": mb_w_out,
            "mlp_w_up": mlp_w_up, "mlp_w_down": mlp_w_down, "final_norm_g": final_norm_g}

def second_block(x, mix_norm_g, mlp_norm_g, dn_w_in, dn_conv_w, dn_a_log, dn_dt_bias,
              dn_out_norm_g, dn_w_out, mb_w_in, mb_w_out, mlp_w_up, mlp_w_down, final_norm_g):
    h = x
    for i in range(DEPTH):
        hn = rmsnorm_2(h, mix_norm_g[i])
        j = i // N_MIXERS
        if i % N_MIXERS == 0:
            mix = gated_deltanet(hn, dn_w_in[j], dn_conv_w[j], dn_a_log[j], dn_dt_bias[j],
                                 dn_out_norm_g[j], dn_w_out[j])
        else:
            mix = moba_layer(hn, mb_w_in[j], mb_w_out[j])
        h = h + mix.astype(h.dtype)
        h = h + squared_relu_mlp(rmsnorm_2(h, mlp_norm_g[i]), mlp_w_up[i], mlp_w_down[i])
    return rmsnorm_2(h, final_norm_g)


def setup_inputs(seed=0):
    out = dict(first_inputs(seed))
    for name, value in second_inputs(seed + 1).items():
        if name != "x":
            out[name + "_2"] = value
    return out


def reference(
    x, a_pre_norm, a_w_in, a_conv_w, a_w_out, a_post_norm, ffn_pre_norm, ffn_w_gate_up,
    ffn_w_down, ffn_post_norm, kv_norm, w_kv, b_pre_norm, b_w_q, b_sinks, b_w_o, b_post_norm,
    mix_norm_g_2, mlp_norm_g_2, dn_w_in_2, dn_conv_w_2, dn_a_log_2, dn_dt_bias_2,
    dn_out_norm_g_2, dn_w_out_2, mb_w_in_2, mb_w_out_2, mlp_w_up_2, mlp_w_down_2,
    final_norm_g_2,
):
    x = first_block(
        x, a_pre_norm, a_w_in, a_conv_w, a_w_out, a_post_norm, ffn_pre_norm, ffn_w_gate_up,
        ffn_w_down, ffn_post_norm, kv_norm, w_kv, b_pre_norm, b_w_q, b_sinks, b_w_o,
        b_post_norm,
    )
    return second_block(
        x, mix_norm_g_2, mlp_norm_g_2, dn_w_in_2, dn_conv_w_2, dn_a_log_2, dn_dt_bias_2,
        dn_out_norm_g_2, dn_w_out_2, mb_w_in_2, mb_w_out_2, mlp_w_up_2, mlp_w_down_2,
        final_norm_g_2,
    )


_drawn_inputs = setup_inputs


def setup_inputs(seed=0):
    import zlib

    import numpy as np

    out = dict(_drawn_inputs(seed))
    spreads = {}
    factors = {'b_sinks': 3.48,
     'mix_norm_g_2': 5.634,
     'mlp_norm_g_2': 11.23,
     'dn_out_norm_g_2': 8.0,
     'final_norm_g_2': 7.666}
    for name, (base, spread) in spreads.items():
        noise = np.random.default_rng([zlib.crc32(name.encode()), seed]).standard_normal(out[name].shape)
        drawn = base * np.exp(spread * noise) if base else spread * noise
        out[name] = __import__('jax').numpy.asarray(drawn.astype(out[name].dtype))
    for name, factor in factors.items():
        out[name] = (out[name] * factor).astype(out[name].dtype)
    return out
```

```python
from contextlib import ExitStack

import concourse.bass as bass
from concourse import mybir

ALU = mybir.AluOpType
ACT = mybir.ActivationFunctionType
F32 = mybir.dt.float32
F32R = mybir.dt.float32r
U8 = mybir.dt.uint8
X = mybir.AxisListType.X

P = 128
T = 256
NT = T // P
D = 1024
KC = D // P
FF = 2816
NF = FF // P
FF2 = 4096
NM = FF2 // P
EPS = 1e-6
HD = 64
NH = 16
NKV = 4
ROT = 8
DH = 128
NHD = 8
SW_SCALE = HD ** -0.5
MB_SCALE = DH ** -0.5

RING = 6
RAW = 3
AHEAD = 4
BODY = RING

U_MIX = 0
U_MIXO = U_MIX + 3 * KC
U_FF = [U_MIXO + KC, 0]
U_KV = U_FF[0] + 3 * NF
U_Q = U_KV + 4
U_O = U_Q + KC
U_FF[1] = U_O + KC
U_DN = U_FF[1] + 3 * NF
U_DNO = U_DN + 4 * NHD
U_MLP = [U_DNO + KC, 0]
U_MB = U_MLP[0] + 2 * NM
U_MBV = U_MB + 2 * NHD
U_MBO = U_MBV + KC
U_MLP[1] = U_MBO + KC
N_UNITS = U_MLP[1] + 2 * NM
LAST_UNIT = [u - 1 for u in (U_FF[0], U_KV, U_FF[1], U_DN, U_MLP[0], U_MB, U_MLP[1], N_UNITS)]

G_A, G_F0, G_F1, G_KV, G_B, G_X0, G_X1, G_M0, G_M1 = [KC * n for n in range(9)]
G_CONV = 9 * KC
C_ID, C_INCL, C_STRICT, C_NEG, C_ONE = [P * n for n in range(5)]
C_BAND = 5 * P
C_DIST = C_BAND + 3 * P
C_COS = C_DIST + 3 * P
C_SIN = C_COS + NT * ROT
N_CONST = C_SIN + NT * ROT
LEVELS = 7

W_SG, W_HX = 0, 3 * T
W_CSB, W_CU, W_Y = 6 * T, 8 * T, 10 * T
W_QTOK, W_QT, W_KDUP, W_KT, W_V, W_RT = 0, 2048, 4096, 5120, 6144, 6656
W_S, W_PT = 7168, 7168 + 4 * 384
W_MQK, W_MV = 0, 4096
W_QKV, W_Z, W_GRP = 0, 24 * T, 32 * T
W_SQ, W_CBUF, W_YBUF = W_GRP, W_GRP + 16 * T, W_GRP + 16 * T + 2 * 260
N_WORK = W_GRP + 2 * 9 * 512

CORE = [("pool", "gs"), ("pe", "kvT"), ("pe", "decay"), ("dve", "kscale"), ("act", "dec"),
        ("pool", "decmask"), ("pe", "knT"), ("act", "knT_copy"), ("act", "z_init"), ("pe", "scores"),
        ("dve", "attn"), ("dve", "b"), ("dve", "z1"), ("pe", "zT"), ("act", "x1")]
for _l in range(1, LEVELS):
    CORE += [("pe", f"y{_l}"), ("act", f"y{_l}_copy"), ("pe", f"dxz{_l}"), ("dve", f"xz{_l}")]
CORE += [("pe", "vn0"), ("act", "vn0_copy"), ("pe", "state"), ("act", "state_copy"), ("pe", "o0"),
         ("pe", "kqs"), ("dve", "rhs1"), ("dve", "t1"), ("pe", "vn1"), ("act", "vn1_copy"), ("pe", "o1"),
         ("dve", "o"), ("act", "osq"), ("pool", "omean"), ("pool", "orstd"), ("dve", "on"), ("pe", "oT"),
         ("dve", "y"), ("dve", "yh"), ("dve", "yl")]
CORE_ORDER = [(e, s, g) for half in range(2) for e, s in CORE for g in (2 * half, 2 * half + 1)]


def core_value(engine, step, g):
    mine = [(s, k) for e, s, k in CORE_ORDER if e == engine]
    return mine.index((step, g)) + 1


def val(static, i, per):
    return static if i is None else i * per + static


def turns(eng, first, n, body, step):
    whole = n // body
    if whole > 1:
        with eng.Fori(0, whole) as i:
            for js in range(first, first + body):
                step(js, i)
        first, n = first + whole * body, n - whole * body
    for js in range(first, first + n):
        step(js, None)


def build(nc, a, out):
    ctx = ExitStack()
    with ctx:
        def sb(name, shape, dt=F32):
            return ctx.enter_context(nc.sbuf_tensor(name, shape, dt))

        def sem(name):
            return ctx.enter_context(nc.semaphore(name))

        w_raw = sb("w_raw", [P, RAW, 1024])
        w_hi = sb("w_hi", [P, RING, 1024], F32R)
        w_lo = sb("w_lo", [P, RING, 1024], F32R)
        h = sb("h", [P, NT, D])
        xh, xl = sb("xh", [P, KC, T], F32R), sb("xl", [P, KC, T], F32R)
        yh, yl = sb("yh", [P, KC, T], F32R), sb("yl", [P, KC, T], F32R)
        xn = sb("xn", [P, NT, D])
        xf = sb("xf", [P, 2, 512])
        gpost = sb("gpost", [P, 2, D])
        hh, hl = sb("hh", [P, 3, T], F32R), sb("hl", [P, 3, T], F32R)
        work = sb("work", [P, N_WORK])
        const = sb("const", [P, N_CONST])
        lmask = sb("lmask", [P, 2 * LEVELS, P], U8)
        rows = sb("rows", [96, 2, P])
        gT = sb("gT", [P, 96])
        cT = sb("cT", [P, 96])
        og = sb("og", [P, 1])
        wba = sb("wba", [P, KC, 16])
        sinks = sb("sinks", [P, NH])
        dtb, alog = sb("dtb", [P, NHD]), sb("alog", [P, NHD])
        sums = sb("sums", [P, 40])
        means = sb("means", [P, 40])
        rstd = sb("rstd", [P, 40])
        half_neg = sb("half_neg", [P, 32])
        mx = sb("mx", [P, 24, 2])
        nm = sb("nm", [P, 24, 2])
        dsk = sb("dsk", [P, NH, 2])
        es = sb("es", [P, NH, 2])
        den = sb("den", [P, 24, 2])
        dtot = sb("dtot", [P, 24, 2])
        rinv = sb("rinv", [P, 24, 2])
        ba = sb("ba", [P, NT, 16])
        sp = sb("sp", [P, 8, 16])
        qkss = sb("qkss", [P, 4, 16])
        pair = sb("pair", [P, 12, 16])
        oss = sb("oss", [P, 3, 16])

        acc = ctx.enter_context(nc.psum_tensor("acc", [P, 4, 512], F32))
        hp = ctx.enter_context(nc.psum_tensor("hp", [P, 4, 512], F32))

        ident = const[:, C_ID:C_ID + P]

        landed = [sem(f"landed{s}") for s in range(RAW)]
        hi_ready, lo_ready, unit_used = sem("hi_ready"), sem("lo_ready"), sem("unit_used")
        x_loaded, early_loaded, late_loaded, masks_loaded = (
            sem("x_loaded"), sem("early_loaded"), sem("late_loaded"), sem("masks_loaded"))
        gpost_loaded = [sem(f"gpost_loaded{s}") for s in range(2)]
        rows_T, gains_ready, pool_const = sem("rows_T"), sem("gains_ready"), sem("pool_const")
        pre_sq, pre_mean, pre_rstd = sem("pre_sq"), sem("pre_mean"), sem("pre_rstd")
        xn_ready, xT_ps, xf_ready, xhi_ready, xT_ready = (
            sem("xn_ready"), sem("xT_ps"), sem("xf_ready"), sem("xhi_ready"), sem("xT_ready"))
        acc_first, post_sq, post_mean, post_rstd = (
            sem("acc_first"), sem("post_sq"), sem("post_mean"), sem("post_rstd"))
        post_tmp, h_new, out_ready, stored = (
            sem("post_tmp"), sem("h_new"), sem("out_ready"), sem("stored"))
        c_copied, pad_zero, cu_step, y_ready = (
            sem("c_copied"), sem("pad_zero"), sem("cu_step"), sem("y_ready"))
        act_done, hid_mul, hid_hi, hid_ready = (
            sem("act_done"), sem("hid_mul"), sem("hid_hi"), sem("hid_ready"))
        kv_copied, q_copied = sem("kv_copied"), sem("q_copied")
        rot_mul, rot_done, k_dup = sem("rot_mul"), sem("rot_done"), sem("k_dup")
        kT_ps, kT_copied, qT_ps, qT_copied = sem("kT_ps"), sem("kT_copied"), sem("qT_ps"), sem("qT_copied")
        sc_done, s_made, mx_done, nm_ready = sem("sc_done"), sem("s_made"), sem("mx_done"), sem("nm_ready")
        dsk_ready, p_ready, pt_ps, pt_ready = sem("dsk_ready"), sem("p_ready"), sem("pt_ps"), sem("pt_ready")
        pv_done, den_ready, rinv_ready, o_made = (
            sem("pv_done"), sem("den_ready"), sem("rinv_ready"), sem("o_made"))
        oT_ps, oT_hi, oT_ready = sem("oT_ps"), sem("oT_hi"), sem("oT_ready")
        mb_copied, mbv_copied = sem("mb_copied"), sem("mbv_copied")
        ba_ps, ba_step, ba_act, ba_pool = sem("ba_ps"), sem("ba_step"), sem("ba_act"), sem("ba_pool")
        conv_in, conv_step, conv_silu = sem("conv_in"), sem("conv_step"), sem("conv_silu")
        z_ready, qk_sq, qk_ps = sem("z_ready"), sem("qk_sq"), sem("qk_ps")
        gc_ps = sem("gc_ps")
        core = {"pe": sem("core_tensor"), "act": sem("core_scalar"),
                "dve": sem("core_vector"), "pool": sem("core_pool")}

        def wk(at, n):
            return work[:, at:at + n]

        def small_psum(slot):
            return hp[:, slot, 0:T]

        def mix_psum(js, kind):
            return (acc if js % 2 == 0 else hp)[:, kind, 0:T]

        def core_bank(g, b):
            return (acc if g % 2 == 0 else hp)[:, b, :].rearrange("p (a n) -> p a n", a=4)

        def core_buf(g, name):
            where = {"kn": 0, "X": 0, "kb": 1, "Z": 1, "vb": 2, "kd": 3, "knT": 4, "y": 4,
                     "kbT": 5, "Y": 5, "decS": 6, "SR": 6, "attnT": 7, "B": 8, "t1": 8}
            if name in ("gs", "vn"):
                return xn[:, g % 2, 0:512].rearrange("p (a n) -> p a n", a=4)
            if name in ("decI", "o"):
                return xn[:, g % 2, 512:1024].rearrange("p (a n) -> p a n", a=4)
            at = W_GRP + ((g % 2) * 9 + where[name]) * 512
            return wk(at, 512).rearrange("p (a n) -> p a n", a=4)

        def qkvT(j):
            return work[:, W_QKV + j * T:W_QKV + (j + 1) * T]

        def each(tile, n=4):
            return tile.unsqueeze(1).broadcast_to([P, n, P])

        def per_pair(row, g):
            return pair[:, row, 4 * g:4 * g + 4].unsqueeze(2).broadcast_to([P, 4, P])

        def core_wait(eng, engine, step, g):
            eng.wait_ge(core[engine], core_value(engine, step, g))

        def wait_unit(eng, us, i=None):
            eng.wait_ge(unit_used, val(us + 1, i, BODY))

        def wait_acc(eng, m, t):
            if t == 0:
                eng.wait_ge(acc_first, m + 1)
            else:
                wait_unit(eng, LAST_UNIT[m])

        block = ctx.enter_context(nc.Block())

        @block.sync
        def _(sp_):
            x_t = a["x"].rearrange("b (t p) d -> p (b t) d", p=P)
            sp_.dma_start(h[:, :, :], x_t).then_inc(x_loaded, 16)

            sp_.dma_start(const[:, :], a["consts"]).then_inc(early_loaded, 16)

            def rows_in(at, k, vector):
                sp_.dma_start(rows[at:at + k, 0, :], vector).then_inc(early_loaded, 16)

            for at, name, l in ((G_A, "a_pre_norm", 0), (G_F0, "ffn_pre_norm", 0), (G_F1, "ffn_pre_norm", 1),
                                (G_B, "b_pre_norm", 0), (G_X0, "mix_norm_g_2", 0), (G_X1, "mix_norm_g_2", 1),
                                (G_M0, "mlp_norm_g_2", 0), (G_M1, "mlp_norm_g_2", 1)):
                rows_in(at, KC, a[name][l].rearrange("(k p) -> k p", p=P))
            rows_in(G_KV, KC, a["kv_norm"].rearrange("(k p) -> k p", p=P))
            rows_in(G_CONV, 3 * KC, a["a_conv_w"].rearrange("a w (k p) -> (a w k) p", p=P))
            sp_.dma_start(rows[:, 1, :], a["dn_conv_w_2"].rearrange("a w (k p) -> (a w k) p", p=P)) \
                .then_inc(early_loaded, 16)

            def late_loads():
                sp_.dma_start(og[:, :], a["dn_out_norm_g_2"].rearrange("a d -> d a")).then_inc(late_loaded, 16)
                sp_.dma_start(wba[:, :, :], a["dn_w_in_2"][0].rearrange("(k p) n -> p k n", p=P)[:, :, 4 * D:4 * D + 16]) \
                    .then_inc(late_loaded, 16)
                sp_.dma_start(sinks[:, :], a["b_sinks"].broadcast_to([P, NH])).then_inc(late_loaded, 16)
                sp_.dma_start(dtb[:, :], a["dn_dt_bias_2"].broadcast_to([P, NHD])).then_inc(late_loaded, 16)
                sp_.dma_start(alog[:, :], a["dn_a_log_2"].broadcast_to([P, NHD])).then_inc(late_loaded, 16)

            def load_gpost(p):
                vector = [a["a_post_norm"], a["ffn_post_norm"][0:1], a["b_post_norm"],
                          a["ffn_post_norm"][1:2], a["final_norm_g_2"].rearrange("(a d) -> a d", a=1)][p]
                if p >= 2:
                    sp_.wait_ge(h_new, 2 * (p - 2) + 2)
                sp_.dma_start(gpost[:, p % 2, :], vector.broadcast_to([P, D])).then_inc(gpost_loaded[p % 2], 16)

            def load(us, i, src, k):
                if us >= RAW or i is not None:
                    sp_.wait_ge(lo_ready, val(us - RAW + 1, i, BODY))
                sp_.dma_start(w_raw[:, us % RAW, :].rearrange("p (k n) -> p k n", k=k), src) \
                    .then_inc(landed[us % RAW], 16)

            def columns(w):
                return w.rearrange("(k p) n -> p k n", p=P)

            def col_chunk(w, start):
                return columns(w)[:, :, bass.ds(start, P)]

            def row_chunk(w, start):
                return w[bass.ds(start, P), :].unsqueeze(1)

            w_in = a["a_w_in"][0]

            def mixer(js, i):
                for n, kind in enumerate((1, 2, 0)):
                    us = U_MIX + 3 * js + n
                    src = col_chunk(w_in, val(kind * D + js * P, i, 2 * P))
                    load(us, i, src, KC)
            for js in range(2):
                mixer(js, None)
            load_gpost(0)
            load_gpost(1)
            late_loads()
            turns(sp_, 2, KC - 2, 2, mixer)

            def rows_of(u0, w, n=KC):
                for k in range(n):
                    load(u0 + k, None, row_chunk(w, k * P), 1)

            rows_of(U_MIXO, a["a_w_out"][0])

            def swiglu(layer):
                up, down = a["ffn_w_gate_up"][layer], a["ffn_w_down"][layer]
                u0 = U_FF[layer]
                load(u0, None, col_chunk(up, 0), KC)
                load(u0 + 1, None, col_chunk(up, FF), KC)

                def step(js, i):
                    us = u0 + 2 + 3 * js
                    load(us, i, col_chunk(up, val((js + 1) * P, i, 2 * P)), KC)
                    load(us + 1, i, col_chunk(up, val(FF + (js + 1) * P, i, 2 * P)), KC)
                    load(us + 2, i, row_chunk(down, val(js * P, i, 2 * P)), 1)
                step(0, None)
                turns(sp_, 1, NF - 2, 2, step)
                load(u0 + 3 * NF - 1, None, row_chunk(down, (NF - 1) * P), 1)

            def relu2(layer):
                up, down = a["mlp_w_up_2"][layer], a["mlp_w_down_2"][layer]
                u0 = U_MLP[layer]
                load(u0, None, col_chunk(up, 0), KC)
                load(u0 + 1, None, col_chunk(up, P), KC)

                def step(js, i):
                    us = u0 + 2 + 2 * js
                    load(us, i, col_chunk(up, val((js + 2) * P, i, 3 * P)), KC)
                    load(us + 1, i, row_chunk(down, val(js * P, i, 3 * P)), 1)
                step(0, None)
                turns(sp_, 1, NM - 3, 3, step)
                load(u0 + 2 * NM - 2, None, row_chunk(down, (NM - 2) * P), 1)
                load(u0 + 2 * NM - 1, None, row_chunk(down, (NM - 1) * P), 1)

            swiglu(0)
            load_gpost(2)
            w_kv = a["w_kv"].rearrange("(k p) n -> p k n", p=P)
            for n in range(4):
                load(U_KV + n, None, w_kv[:, 2 * n:2 * n + 2, :], 2)
            rows_of(U_Q, a["b_w_q"][0])
            rows_of(U_O, a["b_w_o"][0])
            load_gpost(3)
            swiglu(1)
            load_gpost(4)

            dn = a["dn_w_in_2"][0]
            turns(sp_, 0, 32, BODY, lambda js, i: load(U_DN + js, i, col_chunk(dn, val(js * P, i, BODY * P)), KC))
            rows_of(U_DNO, a["dn_w_out_2"][0])
            relu2(0)
            mb = a["mb_w_in_2"][0]
            turns(sp_, 0, 16, BODY, lambda js, i: load(U_MB + js, i, col_chunk(mb, val(js * P, i, BODY * P)), KC))
            rows_of(U_MBV, mb[:, 2 * D:3 * D])
            rows_of(U_MBO, a["mb_w_out_2"][0])
            relu2(1)

            for t in range(NT):
                sp_.wait_ge(out_ready, t + 1)
                sp_.dma_start(out[0, t * P:(t + 1) * P, :], xn[:, t, :]).then_inc(stored, 16)
            sp_.wait_ge(stored, 16 * NT)

        @block.gpsimd
        def _(pool):
            nc.gpsimd.memset(half_neg[:, :], -0.5).then_inc(pool_const, 1)
            pool.wait_ge(pool_const, 1)
            pool.dma_start(lmask[:, :, :], a["masks"]).then_inc(masks_loaded, 16)

            def pre(n):
                for t in range(NT):
                    q = 2 * n + t
                    pool.wait_ge(pre_sq, q + 1)
                    nc.gpsimd.tensor_scalar(means[:, q:q + 1], sums[:, q:q + 1], 1.0 / D, EPS, ALU.mult, ALU.add) \
                        .then_inc(pre_mean, 1)
                    pool.wait_ge(pre_mean, q + 1)
                    nc.gpsimd.tensor_tensor(rstd[:, q:q + 1], means[:, q:q + 1], half_neg[:, 0:1], ALU.pow) \
                        .then_inc(pre_rstd, 1)

            def post(m):
                for t in range(NT):
                    e = 2 * m + t
                    c = 20 + e
                    pool.wait_ge(post_sq, e + 1)
                    nc.gpsimd.tensor_scalar(means[:, c:c + 1], sums[:, c:c + 1], 1.0 / D, EPS, ALU.mult, ALU.add) \
                        .then_inc(post_mean, 1)
                    pool.wait_ge(post_mean, e + 1)
                    nc.gpsimd.tensor_tensor(rstd[:, c:c + 1], means[:, c:c + 1], half_neg[:, 0:1], ALU.pow) \
                        .then_inc(post_rstd, 1)

            for n in range(4):
                pre(n)
                post(n)
            pre(4)
            pool.wait_ge(ba_step, 8)
            nc.gpsimd.tensor_scalar(qkss[:, 0:2, :], qkss[:, 2:4, :], 1.0, 1e-6, ALU.mult, ALU.add).then_inc(ba_pool, 1)
            pool.wait_ge(ba_pool, 1)
            nc.gpsimd.tensor_tensor(pair[:, 0:2, :], qkss[:, 0:2, :],
                                    half_neg[:, :].rearrange("p (a n) -> p a n", a=2), ALU.pow).then_inc(ba_pool, 1)
            pool.wait_ge(ba_step, 14)
            for e, step, g in CORE_ORDER:
                if e != "pool":
                    continue
                if step == "gs":
                    if g >= 2:
                        core_wait(pool, "pe", "o1", g - 2)
                    ins = nc.gpsimd.tensor_tensor(core_buf(g, "gs"), each(const[:, C_STRICT:C_STRICT + P]),
                                                  per_pair(3, g), ALU.mult)
                elif step == "decmask":
                    core_wait(pool, "act", "dec", g)
                    nc.gpsimd.tensor_tensor(core_buf(g, "decS"), core_buf(g, "decI"),
                                            each(const[:, C_NEG:C_NEG + P]), ALU.mult)
                    ins = nc.gpsimd.tensor_tensor(core_buf(g, "decI"), core_buf(g, "decI"),
                                                  each(const[:, C_INCL:C_INCL + P]), ALU.mult)
                elif step == "omean":
                    core_wait(pool, "act", "osq", g)
                    ins = nc.gpsimd.tensor_scalar(oss[:, 1, 4 * g:4 * g + 4], oss[:, 0, 4 * g:4 * g + 4],
                                                  1.0 / DH, EPS, ALU.mult, ALU.add)
                else:
                    core_wait(pool, "pool", "omean", g)
                    ins = nc.gpsimd.tensor_tensor(oss[:, 2, 4 * g:4 * g + 4], oss[:, 1, 4 * g:4 * g + 4],
                                                  half_neg[:, 0:4], ALU.pow)
                ins.then_inc(core["pool"], 1)
            for n in range(5, 9):
                pre(n)

        @block.scalar
        def _(act):
            def split(us, i=None):
                if us >= N_UNITS:
                    return
                act.wait_ge(landed[us % RAW], val(16 * (us // RAW + 1), i, 16 * BODY // RAW))
                if us >= RING or i is not None:
                    act.wait_ge(unit_used, val(us - RING + 1, i, BODY))
                nc.scalar.activation(w_hi[:, us % RING, :], w_raw[:, us % RAW, :], ACT.Copy).then_inc(hi_ready, 1)

            def splits(u0, n):
                for u in range(u0, u0 + n):
                    split(u + AHEAD)

            def pre(n):
                for t in range(NT):
                    q = 2 * n + t
                    if n == 0:
                        act.wait_ge(x_loaded, 16)
                    else:
                        act.wait_ge(h_new, 2 * (n - 1) + t + 1)
                    nc.scalar.activation(xn[:, t, :], h[:, t, :], ACT.Square, accum_out=sums[:, q:q + 1]) \
                        .then_inc(pre_sq, 1)
                for t in range(NT):
                    q = 2 * n + t
                    if n < 8:
                        act.wait_ge(pre_rstd, q + 1)
                        nc.scalar.activation(xn[:, t, :], h[:, t, :], ACT.Copy, scale=rstd[:, q:q + 1]) \
                            .then_inc(xn_ready, 1)

            def post(m):
                for t in range(NT):
                    e = 2 * m + t
                    wait_acc(act, m, t)
                    nc.scalar.activation(xn[:, t, :].rearrange("p (a n) -> p a n", a=2), acc[:, 2 * t:2 * t + 2, :],
                                         ACT.Square, accum_out=sums[:, 20 + e:21 + e]).then_inc(post_sq, 1)

            pre(0)
            for u in range(AHEAD):
                split(u)

            def mixer(js, i):
                us = U_MIX + 3 * js
                split(us + AHEAD, i)
                split(us + AHEAD + 1, i)
                wait_unit(act, us, i)
                if js >= 2 or i is not None:
                    act.wait_ge(y_ready, val(js - 1, i, 2))
                nc.scalar.activation(wk(W_CSB + (js % 2) * T, T), mix_psum(js, 0), ACT.Copy).then_inc(c_copied, 1)
                split(us + AHEAD + 2, i)
            for js in range(2):
                mixer(js, None)
            turns(act, 2, KC - 2, 2, mixer)
            splits(U_MIXO, KC)
            post(0)
            pre(1)

            def swiglu(layer):
                u0, fb = U_FF[layer], NF * layer

                def silu(js, i, unit):
                    wait_unit(act, unit, i)
                    if fb + js >= 2 or i is not None:
                        act.wait_ge(hid_mul, val(fb + js - 1, i, 2))
                    nc.scalar.activation(wk(W_SG + (js % 2) * T, T), hp[:, 2 * (js % 2), 0:T], ACT.Silu) \
                        .then_inc(act_done, 1)
                split(u0 + AHEAD)
                split(u0 + AHEAD + 1)
                silu(0, None, u0)

                def step(js, i):
                    us = u0 + 2 + 3 * js
                    split(us + AHEAD, i)
                    split(us + AHEAD + 1, i)
                    silu(js + 1, i, us)
                    split(us + AHEAD + 2, i)
                step(0, None)
                turns(act, 1, NF - 2, 2, step)
                split(u0 + 3 * NF - 1 + AHEAD)

            def relu2(layer):
                u0, cb = U_MLP[layer], 2 * NF + NM * layer

                def relu(js, i, unit):
                    wait_unit(act, unit, i)
                    act.wait_ge(hid_mul, val(cb + js - 2, i, 3))
                    nc.scalar.activation(wk(W_SG + (js % 3) * T, T), hp[:, js % 3, 0:T], ACT.Relu) \
                        .then_inc(act_done, 1)
                split(u0 + AHEAD)
                relu(0, None, u0)
                split(u0 + AHEAD + 1)
                relu(1, None, u0 + 1)

                def step(js, i):
                    us = u0 + 2 + 2 * js
                    split(us + AHEAD, i)
                    split(us + AHEAD + 1, i)
                    relu(js + 2, i, us)
                step(0, None)
                turns(act, 1, NM - 3, 3, step)
                split(u0 + 2 * NM - 2 + AHEAD)
                split(u0 + 2 * NM - 1 + AHEAD)

            def heads(first, n, scale, sink):
                def exp(hd):
                    i = first + hd
                    s = wk(W_S + (i % 4) * 384, 384)
                    act.wait_ge(nm_ready, i + 1)
                    if sink:
                        act.wait_ge(dsk_ready, i + 1)
                        nc.scalar.activation(es[:, i, :], dsk[:, i, :], ACT.Exp)
                    nc.scalar.activation(s[:, 0:P], s[:, 0:P], ACT.Exp, bias=nm[:, i, 0:1], scale=scale,
                                         accum_out=den[:, i, 0:1])
                    nc.scalar.activation(s[:, P:384], s[:, P:384], ACT.Exp, bias=nm[:, i, 1:2], scale=scale,
                                         accum_out=den[:, i, 1:2]).then_inc(p_ready, 1)

                def pt_copy(hd):
                    i = first + hd
                    act.wait_ge(pt_ps, i + 1)
                    if i >= 2:
                        act.wait_ge(pv_done, i - 1)
                    nc.scalar.activation(wk(W_PT + (i % 2) * 384, 384), acc[:, 2 + i % 2, 0:384], ACT.Copy) \
                        .then_inc(pt_ready, 1)
                for k in range(n + 2):
                    if 1 <= k <= n:
                        exp(k - 1)
                    if k >= 2:
                        pt_copy(k - 2)

            swiglu(0)
            post(1)
            pre(2)
            splits(U_KV, 4)
            for t in range(NT):
                wait_unit(act, U_Q - 1)
                nc.scalar.activation(wk(W_KDUP + t * 512, 512).rearrange("p (g c n) -> p g c n", g=4, c=2)[:, :, 0, :],
                                     hp[:, t, 0:256].rearrange("p (g n) -> p g n", g=4), ACT.Copy)
                nc.scalar.activation(wk(W_V + t * 256, 256), hp[:, t, 256:512], ACT.Copy).then_inc(kv_copied, 1)
            splits(U_Q, KC)
            for t in range(NT):
                wait_unit(act, U_O - 1)
                nc.scalar.activation(wk(W_QTOK + t * D, D).rearrange("p (a n) -> p a n", a=2), acc[:, 2 * t:2 * t + 2, :],
                                     ACT.Copy).then_inc(q_copied, 1)
            for t in range(NT):
                act.wait_ge(kT_ps, t + 1)
                nc.scalar.activation(wk(W_KT, 1024).rearrange("p (g n) -> p g n", g=4)[:, :, t * P:(t + 1) * P],
                                     hp[:, 2 + t, :].rearrange("p (g n) -> p g n", g=4), ACT.Copy).then_inc(kT_copied, 1)
            for t in range(NT):
                for half in range(2):
                    act.wait_ge(qT_ps, 2 * t + half + 1)
                    nc.scalar.activation(
                        wk(W_QT + half * 1024, 1024).rearrange("p (g n) -> p g n", g=4)[:, :, t * P:(t + 1) * P],
                        hp[:, 2 * t + half, :].rearrange("p (g n) -> p g n", g=4), ACT.Copy).then_inc(qT_copied, 1)
            heads(0, NH, 1.0, True)
            splits(U_O, KC)
            post(2)
            pre(3)
            swiglu(1)
            post(3)
            pre(4)

            def conv(js, i):
                split(U_DN + js + AHEAD, i)
                if js >= 1 or i is not None:
                    silu(js - 1, i)
                wait_unit(act, U_DN + js, i)
                if js >= 2 or i is not None:
                    act.wait_ge(conv_step, val(4 * (js - 1), i, 4 * BODY))
                nc.scalar.activation(work[:, W_CBUF + (js % 2) * 260 + 3:W_CBUF + (js % 2) * 260 + 3 + T],
                                     small_psum(js % 3), ACT.Copy).then_inc(conv_in, 1)

            def silu(js, i):
                act.wait_ge(conv_step, val(4 * (js + 1), i, 4 * BODY))
                at = val(W_QKV + js * T, i, BODY * T)
                nc.scalar.activation(work[:, bass.ds(at, T)], wk(W_YBUF + (js % 2) * T, T), ACT.Silu) \
                    .then_inc(conv_silu, 1)
            for js in range(BODY):
                conv(js, None)
            turns(act, BODY, 24 - BODY, BODY, conv)
            silu(23, None)
            for j in range(24, 32):
                split(U_DN + j + AHEAD)
                wait_unit(act, U_DN + j)
                nc.scalar.activation(wk(W_Z + (j - 24) * T, T), small_psum(j % 3), ACT.Silu).then_inc(z_ready, 1)
            act.wait_ge(conv_step, 4 * 24)
            act.wait_ge(conv_silu, 24)
            for part in range(4):
                nc.scalar.activation(wk(W_SQ + part * 4 * T, 4 * T), wk(W_QKV + part * 4 * T, 4 * T), ACT.Square) \
                    .then_inc(qk_sq, 1)
            act.wait_ge(ba_step, 3)
            nc.scalar.activation(sp[:, 0, :].rearrange("p (h t) -> p h t", t=2), ba[:, :, 0:8].rearrange("p t h -> p h t"),
                                 ACT.Exp, scale=-1.0)
            nc.scalar.activation(sp[:, 2, :], sp[:, 1, :], ACT.Exp, scale=-1.0)
            nc.scalar.activation(sp[:, 3, 0:8], alog[:, :], ACT.Exp).then_inc(ba_act, 1)
            act.wait_ge(ba_act, 1)
            nc.scalar.activation(sp[:, 4, :], sp[:, 2, :], ACT.Ln, bias=1.0).then_inc(ba_act, 1)
            act.wait_ge(gc_ps, 1)
            nc.scalar.activation(pair[:, 4:6, :], acc[:, 2, 0:32].rearrange("p (a n) -> p a n", a=2), ACT.Exp) \
                .then_inc(ba_act, 1)

            for e, step, g in CORE_ORDER:
                if e != "act":
                    continue
                bank = lambda b: core_bank(g, b)
                buf = lambda name: core_buf(g, name)
                if step == "dec":
                    core_wait(act, "pe", "decay", g)
                    ins = nc.scalar.activation(buf("decI"), bank(2), ACT.Exp)
                elif step == "knT_copy":
                    core_wait(act, "pe", "knT", g)
                    nc.scalar.activation(buf("knT"), bank(0), ACT.Copy)
                    ins = nc.scalar.activation(buf("kbT"), bank(1), ACT.Copy)
                elif step == "z_init":
                    ins = nc.scalar.activation(buf("Z"), each(ident), ACT.Copy)
                elif step == "x1":
                    core_wait(act, "pe", "zT", g)
                    ins = nc.scalar.activation(buf("X"), bank(0), ACT.Copy)
                elif step.startswith("y"):
                    core_wait(act, "pe", step[:-5], g)
                    ins = nc.scalar.activation(buf("Y"), bank(0), ACT.Copy)
                elif step == "vn0_copy":
                    core_wait(act, "pe", "vn0", g)
                    ins = nc.scalar.activation(buf("vn")[:, 0:3:2, :], bank(0)[:, 0:2, :], ACT.Copy)
                elif step == "state_copy":
                    core_wait(act, "pe", "state", g)
                    ins = nc.scalar.activation(buf("SR")[:, 0:2, :], bank(1)[:, 0:2, :], ACT.Copy)
                elif step == "vn1_copy":
                    core_wait(act, "pe", "vn1", g)
                    ins = nc.scalar.activation(buf("vn")[:, 1:4:2, :], bank(0)[:, 2:4, :], ACT.Copy)
                else:
                    core_wait(act, "dve", "o", g)
                    for p in range(4):
                        ins = nc.scalar.activation(buf("kbT")[:, p, :], buf("o")[:, p, :], ACT.Square,
                                                   accum_out=oss[:, 0, 4 * g + p:4 * g + p + 1])
                ins.then_inc(core["act"], 1)

            splits(U_DNO, KC)
            pre(5)
            relu2(0)
            pre(6)

            def qk_copy(js, i):
                split(U_MB + js + AHEAD, i)
                wait_unit(act, U_MB + js, i)
                nc.scalar.activation(work[:, bass.ds(val(W_MQK + js * T, i, BODY * T), T)], small_psum(js % 3),
                                     ACT.Copy).then_inc(mb_copied, 1)
            turns(act, 0, 16, BODY, qk_copy)
            splits(U_MBV, KC)
            for t in range(NT):
                wait_unit(act, U_MBO - 1)
                nc.scalar.activation(wk(W_MV + t * D, D).rearrange("p (a n) -> p a n", a=2), acc[:, 2 * t:2 * t + 2, :],
                                     ACT.Copy).then_inc(mbv_copied, 1)
            heads(NH, NHD, MB_SCALE, False)
            splits(U_MBO, KC)
            pre(7)
            relu2(1)
            pre(8)

        @block.vector
        def _(dve):
            def split(us, i=None):
                if us >= N_UNITS:
                    return
                dve.wait_ge(hi_ready, val(us + 1, i, BODY))
                nc.vector.tensor_tensor(w_lo[:, us % RING, :], w_raw[:, us % RAW, :],
                                        w_hi[:, us % RING, :].bitcast(F32), ALU.subtract).then_inc(lo_ready, 1)

            def splits(u0, n):
                for u in range(u0, u0 + n):
                    split(u + AHEAD)

            n_hi = [0]

            def pre(n, gains):
                for t in range(NT):
                    for half in range(2):
                        dve.wait_ge(xT_ps, 4 * n + 2 * t + half + 1)
                        for g, hi, lo in gains:
                            n_hi[0] += 1
                            b = n_hi[0] % 2
                            f = xf[:, b, :].rearrange("p (k n) -> p k n", k=4)
                            at = (slice(None), slice(4 * half, 4 * half + 4), slice(t * P, (t + 1) * P))
                            nc.vector.tensor_tensor(
                                f, hp[:, 2 * t + half, :].rearrange("p (k n) -> p k n", k=4),
                                gT[:, g + 4 * half:g + 4 * half + 4].unsqueeze(2).broadcast_to([P, 4, P]),
                                ALU.mult).then_inc(xf_ready, 1)
                            dve.wait_ge(xf_ready, n_hi[0])
                            nc.vector.tensor_copy(hi[at], f).then_inc(xhi_ready, 1)
                            dve.wait_ge(xhi_ready, n_hi[0])
                            nc.vector.tensor_tensor(lo[at], f, hi[at].bitcast(F32), ALU.subtract) \
                                .then_inc(xT_ready, 1)

            def post(m):
                dve.wait_ge(gpost_loaded[m % 2], 16 * (m // 2 + 1))
                for t in range(NT):
                    e = 2 * m + t
                    dve.wait_ge(post_rstd, e + 1)
                    two = lambda v: v.rearrange("p (a n) -> p a n", a=2)
                    nc.vector.scalar_tensor_tensor(
                        out=two(xn[:, t, :]), in0=acc[:, 2 * t:2 * t + 2, :], scalar=rstd[:, 20 + e:21 + e],
                        in1=two(gpost[:, m % 2, :]), op0=ALU.mult, op1=ALU.mult).then_inc(post_tmp, 1)
                    dve.wait_ge(post_tmp, e + 1)
                    nc.vector.tensor_tensor(h[:, t, :], h[:, t, :], xn[:, t, :], ALU.add).then_inc(h_new, 1)

            def residual(m):
                for t in range(NT):
                    wait_acc(dve, m, t)
                    two = h[:, t, :].rearrange("p (a n) -> p a n", a=2)
                    nc.vector.tensor_tensor(two, acc[:, 2 * t:2 * t + 2, :], two, ALU.add).then_inc(h_new, 1)

            dve.wait_ge(rows_T, 1)
            nc.vector.tensor_copy(gT[:, :], acc[:, 0, 0:96])
            nc.vector.tensor_copy(cT[:, :], acc[:, 1, 0:96]).then_inc(gains_ready, 1)
            dve.wait_ge(gains_ready, 1)
            nc.vector.memset(wk(W_CU, 2), 0.0).then_inc(pad_zero, 1)
            dve.wait_ge(pad_zero, 1)
            pre(0, [(G_A, xh, xl)])
            for u in range(AHEAD):
                split(u)

            def mixer(js, i):
                us = U_MIX + 3 * js
                for n in range(3):
                    split(us + AHEAD + n, i)
                cu = wk(W_CU, T + 2)
                y = wk(W_Y + (js % 2) * T, T)

                def tap(w):
                    return gT[:, bass.ds(val(G_CONV + w * KC + js, i, 2), 1)]

                def done(ins, n):
                    ins.then_inc(cu_step, 1)
                    dve.wait_ge(cu_step, val(6 * js + n, i, 12))
                dve.wait_ge(c_copied, val(js + 1, i, 2))
                wait_unit(dve, us + 2, i)
                done(nc.vector.tensor_tensor(cu[:, 2:T + 2], mix_psum(js, 1), wk(W_CSB + (js % 2) * T, T), ALU.mult), 1)
                done(nc.vector.tensor_scalar(y, cu[:, 0:T], tap(0), None, ALU.mult), 2)
                done(nc.vector.scalar_tensor_tensor(out=y, in0=cu[:, 1:T + 1], scalar=tap(1), in1=y,
                                                    op0=ALU.mult, op1=ALU.add), 3)
                done(nc.vector.scalar_tensor_tensor(out=y, in0=cu[:, 2:T + 2], scalar=tap(2), in1=y,
                                                    op0=ALU.mult, op1=ALU.add), 4)
                done(nc.vector.tensor_tensor(y, mix_psum(js, 2), y, ALU.mult), 5)
                chunk = bass.ds(val(js, i, 2), 1)
                done(nc.vector.tensor_copy(yh[:, chunk, :], y.unsqueeze(1)), 6)
                nc.vector.tensor_tensor(yl[:, chunk, :], y.unsqueeze(1), yh[:, chunk, :].bitcast(F32),
                                        ALU.subtract).then_inc(y_ready, 1)
            for js in range(2):
                mixer(js, None)
            turns(dve, 2, KC - 2, 2, mixer)
            splits(U_MIXO, KC)
            post(0)
            pre(1, [(G_F0, xh, xl)])

            def hidden(js, i, cb, ring, up_bank, unit):
                n = lambda d: val(cb + js + d, i, ring)
                sg, hx = wk(W_SG + (js % ring) * T, T), wk(W_HX + (js % ring) * T, T)
                dve.wait_ge(act_done, n(1))
                wait_unit(dve, unit, i)
                nc.vector.tensor_tensor(hx, hp[:, up_bank, 0:T], sg, ALU.mult).then_inc(hid_mul, 1)
                dve.wait_ge(hid_mul, n(1))
                nc.vector.tensor_copy(hh[:, js % ring, :], hx).then_inc(hid_hi, 1)
                dve.wait_ge(hid_hi, n(1))
                nc.vector.tensor_tensor(hl[:, js % ring, :], hx, hh[:, js % ring, :].bitcast(F32), ALU.subtract) \
                    .then_inc(hid_ready, 1)

            def swiglu(layer):
                u0, cb = U_FF[layer], NF * layer
                split(u0 + AHEAD)
                split(u0 + AHEAD + 1)
                hidden(0, None, cb, 2, 1, u0 + 1)

                def step(js, i):
                    us = u0 + 2 + 3 * js
                    for n in range(3):
                        split(us + AHEAD + n, i)
                    if js >= 1 or i is not None:
                        wait_unit(dve, us - 1, i)
                    hidden(js + 1, i, cb, 2, 2 * ((js + 1) % 2) + 1, us + 1)
                step(0, None)
                turns(dve, 1, NF - 2, 2, step)
                split(u0 + 3 * NF - 1 + AHEAD)

            def relu2(layer):
                u0, cb = U_MLP[layer], 2 * NF + NM * layer
                split(u0 + AHEAD)
                hidden(0, None, cb, 3, 0, u0)
                split(u0 + AHEAD + 1)
                hidden(1, None, cb, 3, 1, u0 + 1)

                def step(js, i):
                    us = u0 + 2 + 2 * js
                    split(us + AHEAD, i)
                    split(us + AHEAD + 1, i)
                    if js >= 1 or i is not None:
                        wait_unit(dve, us - 1, i)
                    hidden(js + 2, i, cb, 3, (js + 2) % 3, us)
                step(0, None)
                turns(dve, 1, NM - 3, 3, step)
                split(u0 + 2 * NM - 2 + AHEAD)
                split(u0 + 2 * NM - 1 + AHEAD)

            def rotary(n, view, t, nh):
                t1, t2 = view[:, :, 0:ROT], view[:, :, ROT:2 * ROT]
                cos = const[:, C_COS + t * ROT:C_COS + (t + 1) * ROT].unsqueeze(1).broadcast_to([P, nh, ROT])
                sin = const[:, C_SIN + t * ROT:C_SIN + (t + 1) * ROT].unsqueeze(1).broadcast_to([P, nh, ROT])
                r = [wk(W_RT + k * P, nh * ROT).rearrange("p (g n) -> p g n", g=nh) for k in range(4)]
                if n:
                    dve.wait_ge(rot_done, 2 * n)
                for k, (u, v) in enumerate(((t1, cos), (t2, sin), (t2, cos), (t1, sin))):
                    nc.vector.tensor_tensor(r[k], u, v, ALU.mult).then_inc(rot_mul, 1)
                dve.wait_ge(rot_mul, 4 * (n + 1))
                nc.vector.tensor_tensor(t1, r[0], r[1], ALU.subtract).then_inc(rot_done, 1)
                nc.vector.tensor_tensor(t2, r[2], r[3], ALU.add).then_inc(rot_done, 1)

            def heads(first, n, sink):
                def scores(hd):
                    i = first + hd
                    s = wk(W_S + (i % 4) * 384, 384)
                    dve.wait_ge(sc_done, i + 1)
                    if i >= 4:
                        dve.wait_ge(pt_ps, i - 3)
                    ps = acc[:, i % 2, 0:384]
                    if sink:
                        ins = nc.vector.scalar_tensor_tensor(out=s, in0=ps, scalar=SW_SCALE,
                                                             in1=const[:, C_BAND:C_BAND + 384],
                                                             op0=ALU.mult, op1=ALU.add)
                    else:
                        slope = 2.0 ** (-8.0 * (hd + 1) / NHD)
                        ins = nc.vector.scalar_tensor_tensor(out=s, in0=const[:, C_DIST:C_DIST + 384],
                                                             scalar=slope / MB_SCALE, in1=ps,
                                                             op0=ALU.mult, op1=ALU.add)
                    ins.then_inc(s_made, 1)
                    dve.wait_ge(s_made, i + 1)
                    nc.vector.tensor_reduce(mx[:, i, 0:1], s[:, 0:P], X, ALU.max, negate=True).then_inc(mx_done, 1)
                    nc.vector.tensor_reduce(mx[:, i, 1:2], s[:, P:384], X, ALU.max, negate=True).then_inc(mx_done, 1)
                    dve.wait_ge(mx_done, 2 * (i + 1))
                    if sink:
                        neg_sink = pair[:, 11, hd:hd + 1].broadcast_to([P, 2])
                        nc.vector.tensor_tensor(nm[:, i, :], mx[:, i, :], neg_sink, ALU.min).then_inc(nm_ready, 1)
                        dve.wait_ge(nm_ready, i + 1)
                        nc.vector.tensor_tensor(dsk[:, i, :], nm[:, i, :], neg_sink, ALU.subtract) \
                            .then_inc(dsk_ready, 1)
                    else:
                        nc.vector.tensor_scalar(nm[:, i, :], mx[:, i, :], MB_SCALE, None, ALU.mult) \
                            .then_inc(nm_ready, 1)

                def norm(hd):
                    i = first + hd
                    dh = HD if sink else DH
                    dve.wait_ge(p_ready, i + 1)
                    total = den
                    if sink:
                        nc.vector.tensor_tensor(dtot[:, i, :], den[:, i, :], es[:, i, :], ALU.add).then_inc(den_ready, 1)
                        dve.wait_ge(den_ready, i + 1)
                        total = dtot
                    nc.vector.reciprocal(rinv[:, i, :], total[:, i, :]).then_inc(rinv_ready, 1)
                    dve.wait_ge(rinv_ready, i + 1)
                    dve.wait_ge(pv_done, i + 1)
                    nc.vector.tensor_tensor(xn[:, :, hd * dh:(hd + 1) * dh],
                                            hp[:, i % 2, 0:2 * dh].rearrange("p (t n) -> p t n", t=2),
                                            rinv[:, i, :].unsqueeze(2).broadcast_to([P, 2, dh]), ALU.mult) \
                        .then_inc(o_made, 1)
                for k in range(n + 3):
                    if k < n:
                        scores(k)
                    if k >= 3:
                        norm(k - 3)

            def out_T(s, hi, lo):
                for k in range(4):
                    t, half = k // 2, k % 2
                    n = 4 * s + k + 1
                    at = (slice(None), slice(4 * half, 4 * half + 4), slice(t * P, (t + 1) * P))
                    ps = hp[:, k, :].rearrange("p (k n) -> p k n", k=4)
                    dve.wait_ge(oT_ps, n)
                    nc.vector.tensor_copy(hi[at], ps).then_inc(oT_hi, 1)
                    dve.wait_ge(oT_hi, n)
                    nc.vector.tensor_tensor(lo[at], ps, hi[at].bitcast(F32), ALU.subtract).then_inc(oT_ready, 1)

            swiglu(0)
            post(1)
            pre(2, [(G_KV, xh, xl), (G_B, yh, yl)])
            splits(U_KV, 4)
            dve.wait_ge(late_loaded, 16 * 5)
            nc.vector.tensor_scalar(pair[:, 11, :], sinks[:, :], -1.0, None, ALU.mult).then_inc(k_dup, 1)
            dve.wait_ge(k_dup, 1)
            for t in range(NT):
                dve.wait_ge(kv_copied, t + 1)
                kd = wk(W_KDUP + t * 512, 512).rearrange("p (g c n) -> p g c n", g=4, c=2)
                rotary(t, kd[:, :, 0, :], t, NKV)
                dve.wait_ge(rot_done, 2 * (t + 1))
                nc.vector.tensor_copy(kd[:, :, 1, :], kd[:, :, 0, :]).then_inc(k_dup, 1)
            splits(U_Q, KC)
            for t in range(NT):
                dve.wait_ge(q_copied, t + 1)
                rotary(2 + t, wk(W_QTOK + t * D, D).rearrange("p (g n) -> p g n", g=NH), t, NH)
            heads(0, NH, True)
            out_T(0, xh, xl)
            splits(U_O, KC)
            post(2)
            pre(3, [(G_F1, xh, xl)])
            swiglu(1)
            post(3)
            nc.vector.memset(wk(W_CBUF, 520), 0.0).then_inc(pad_zero, 1)
            dve.wait_ge(pad_zero, 2)
            pre(4, [(G_X0, xh, xl)])

            dve.wait_ge(ba_ps, 1)
            nc.vector.tensor_copy(ba[:, :, :], acc[:, 0, 0:32].rearrange("p (t n) -> p t n", t=2)).then_inc(ba_step, 1)
            dve.wait_ge(ba_step, 1)
            th = lambda v: v.rearrange("p (h t) -> p h t", t=2)
            nc.vector.tensor_tensor(th(sp[:, 5, :]), ba[:, :, 8:16].rearrange("p t h -> p h t"),
                                    dtb[:, :].unsqueeze(2).broadcast_to([P, NHD, 2]), ALU.add).then_inc(ba_step, 1)
            dve.wait_ge(ba_step, 2)
            nc.vector.scalar_tensor_tensor(out=sp[:, 1, :], in0=sp[:, 5, :], scalar=-1.0, in1=sp[:, 5, :],
                                           op0=ALU.mult, op1=ALU.max).then_inc(ba_step, 1)

            def conv(js, i):
                split(U_DN + js + AHEAD, i)
                c = wk(W_CBUF + (js % 2) * 260, 260)
                y = wk(W_YBUF + (js % 2) * T, T)
                dve.wait_ge(conv_in, val(js + 1, i, BODY))
                if js >= 2 or i is not None:
                    dve.wait_ge(conv_silu, val(js - 1, i, BODY))
                for w in range(4):
                    tap = cT[:, bass.ds(val(w * 24 + js, i, BODY), 1)]
                    if w == 0:
                        ins = nc.vector.tensor_scalar(y, c[:, 0:T], tap, None, ALU.mult)
                    else:
                        dve.wait_ge(conv_step, val(4 * js + w, i, 4 * BODY))
                        ins = nc.vector.scalar_tensor_tensor(out=y, in0=c[:, w:w + T], scalar=tap, in1=y,
                                                             op0=ALU.mult, op1=ALU.add)
                    ins.then_inc(conv_step, 1)
            for js in range(BODY):
                conv(js, None)
            turns(dve, BODY, 24 - BODY, BODY, conv)
            for j in range(24, 32):
                split(U_DN + j + AHEAD)
            dve.wait_ge(ba_act, 2)
            nc.vector.tensor_scalar(sp[:, 6, :], sp[:, 0, :], 1.0, None, ALU.add).then_inc(ba_step, 1)
            dve.wait_ge(ba_step, 4)
            nc.vector.reciprocal(pair[:, 2, :], sp[:, 6, :]).then_inc(ba_step, 1)
            nc.vector.scalar_tensor_tensor(out=sp[:, 7, :], in0=sp[:, 5, :], scalar=0.0, in1=sp[:, 4, :],
                                           op0=ALU.max, op1=ALU.add).then_inc(ba_step, 1)
            dve.wait_ge(ba_step, 6)
            nc.vector.scalar_tensor_tensor(out=th(pair[:, 3, :]), in0=th(sp[:, 7, :]), scalar=-1.0,
                                           in1=sp[:, 3, 0:8].unsqueeze(2).broadcast_to([P, NHD, 2]),
                                           op0=ALU.mult, op1=ALU.mult).then_inc(ba_step, 1)
            dve.wait_ge(qk_ps, 1)
            nc.vector.tensor_copy(qkss[:, 2:4, :], acc[:, 1, 0:32].rearrange("p (a n) -> p a n", a=2)) \
                .then_inc(ba_step, 1)
            dve.wait_ge(ba_pool, 2)
            dve.wait_ge(ba_act, 3)
            row = lambda r: pair[:, r, :]
            nc.vector.tensor_tensor(row(6), row(1), row(2), ALU.mult).then_inc(ba_step, 1)
            nc.vector.tensor_tensor(row(7), row(1), row(5), ALU.mult).then_inc(ba_step, 1)
            nc.vector.scalar_tensor_tensor(out=row(8), in0=row(2), scalar=-1.0, in1=row(4),
                                           op0=ALU.mult, op1=ALU.mult).then_inc(ba_step, 1)
            nc.vector.tensor_scalar(row(9), row(0), DH ** -0.5, None, ALU.mult).then_inc(ba_step, 1)
            nc.vector.scalar_tensor_tensor(out=row(10), in0=row(0), scalar=DH ** -0.5, in1=row(4),
                                           op0=ALU.mult, op1=ALU.mult).then_inc(ba_step, 1)
            dve.wait_ge(ba_step, 13)
            nc.vector.tensor_copy(oss[:, 0, :], row(10)).then_inc(ba_step, 1)
            dve.wait_ge(ba_step, 14)

            dve.wait_ge(masks_loaded, 16)
            level = lambda n, flip: lmask[:, 2 * n + flip, :].unsqueeze(1).broadcast_to([P, 4, P])
            for e, step, g in CORE_ORDER:
                if e != "dve":
                    continue
                bank = lambda b: core_bank(g, b)
                buf = lambda name: core_buf(g, name)
                if step == "kscale":
                    core_wait(dve, "pe", "kvT", g)
                    tt = nc.vector.tensor_tensor
                    tt(buf("kn"), bank(0), per_pair(1, g), ALU.mult)
                    tt(buf("kb"), bank(0), per_pair(6, g), ALU.mult)
                    tt(buf("vb"), bank(1), per_pair(2, g), ALU.mult)
                    ins = tt(buf("kd"), bank(0), per_pair(7, g), ALU.mult)
                elif step == "attn":
                    core_wait(dve, "pe", "scores", g)
                    core_wait(dve, "pool", "decmask", g)
                    ins = nc.vector.tensor_tensor(buf("attnT"), bank(2), buf("decI"), ALU.mult)
                elif step == "b":
                    ins = nc.vector.tensor_tensor(buf("B"), bank(3), buf("decS"), ALU.mult)
                elif step == "z1":
                    core_wait(dve, "act", "z_init", g)
                    core_wait(dve, "dve", "b", g)
                    ins = nc.vector.copy_predicated(buf("Z"), level(0, 1), buf("B"))
                elif step.startswith("xz"):
                    n = int(step[2:])
                    core_wait(dve, "pe", f"dxz{n}", g)
                    if n < LEVELS - 1:
                        nc.vector.copy_predicated(buf("X"), level(n, 0), bank(1))
                    ins = nc.vector.copy_predicated(buf("Z"), level(n, 1), bank(2))
                elif step == "rhs1":
                    core_wait(dve, "pe", "kqs", g)
                    for hd in range(2):
                        p = 4 * g + 2 * hd + 1
                        ins = nc.vector.scalar_tensor_tensor(
                            out=buf("SR")[:, 2 + hd, :], in0=bank(3)[:, hd, :], scalar=pair[:, 8, p:p + 1],
                            in1=buf("vb")[:, 2 * hd + 1, :], op0=ALU.mult, op1=ALU.add)
                elif step == "t1":
                    for hd in range(2):
                        p = 4 * g + 2 * hd + 1
                        ins = nc.vector.tensor_scalar(buf("t1")[:, hd, :], bank(3)[:, 2 + hd, :],
                                                      pair[:, 10, p:p + 1], None, ALU.mult)
                elif step == "o":
                    core_wait(dve, "pe", "o1", g)
                    core_wait(dve, "dve", "t1", g)
                    for hd in range(2):
                        p = 4 * g + 2 * hd
                        nc.vector.tensor_scalar(buf("o")[:, 2 * hd, :], bank(2)[:, 2 * hd, :],
                                                pair[:, 9, p:p + 1], None, ALU.mult)
                        ins = nc.vector.scalar_tensor_tensor(
                            out=buf("o")[:, 2 * hd + 1, :], in0=bank(2)[:, 2 * hd + 1, :],
                            scalar=pair[:, 9, p + 1:p + 2], in1=buf("t1")[:, hd, :], op0=ALU.mult, op1=ALU.add)
                elif step == "on":
                    core_wait(dve, "pool", "orstd", g)
                    ins = nc.vector.tensor_tensor(
                        buf("o"), buf("o"), oss[:, 2, 4 * g:4 * g + 4].unsqueeze(2).broadcast_to([P, 4, P]), ALU.mult)
                elif step == "y":
                    core_wait(dve, "pe", "oT", g)
                    ins = nc.vector.scalar_tensor_tensor(
                        out=buf("y").rearrange("p a n -> p (a n)"), in0=bank(3).rearrange("p a n -> p (a n)"),
                        scalar=og[:, 0:1], in1=wk(W_Z + 2 * g * T, 2 * T), op0=ALU.mult, op1=ALU.mult)
                elif step == "yh":
                    core_wait(dve, "dve", "y", g)
                    ins = nc.vector.tensor_copy(yh[:, 2 * g:2 * g + 2, :].rearrange("p a n -> p (a n)"),
                                                buf("y").rearrange("p a n -> p (a n)"))
                else:
                    core_wait(dve, "dve", "yh", g)
                    ins = nc.vector.tensor_tensor(yl[:, 2 * g:2 * g + 2, :].rearrange("p a n -> p (a n)"),
                                                  buf("y").rearrange("p a n -> p (a n)"),
                                                  yh[:, 2 * g:2 * g + 2, :].bitcast(F32).rearrange("p a n -> p (a n)"),
                                                  ALU.subtract)
                ins.then_inc(core["dve"], 1)

            splits(U_DNO, KC)
            residual(4)
            pre(5, [(G_M0, xh, xl)])
            relu2(0)
            residual(5)
            pre(6, [(G_X1, xh, xl)])
            for n in range(2 * NHD + KC):
                split(U_MB + n + AHEAD)
            heads(NH, NHD, False)
            out_T(1, xh, xl)
            splits(U_MBO, KC)
            residual(6)
            pre(7, [(G_M1, xh, xl)])
            relu2(1)
            residual(7)
            dve.wait_ge(gpost_loaded[0], 16 * 3)
            for t in range(NT):
                q = 16 + t
                dve.wait_ge(pre_rstd, q + 1)
                nc.vector.scalar_tensor_tensor(out=xn[:, t, :], in0=h[:, t, :], scalar=rstd[:, q:q + 1],
                                               in1=gpost[:, 0, :], op0=ALU.mult, op1=ALU.mult).then_inc(out_ready, 1)

        @block.tensor
        def _(pe):
            mm = nc.tensor.matmul

            def take(us, i=None):
                pe.wait_ge(lo_ready, val(us + 1, i, BODY))

            def feature_chunk(us, i, ps, hi, lo):
                take(us, i)
                wh = w_hi[:, us % RING, :].rearrange("p (k n) -> p k n", k=KC)
                wl = w_lo[:, us % RING, :].rearrange("p (k n) -> p k n", k=KC)
                for k in range(KC):
                    mm(ps, wh[:, k, :], hi[:, k, :], start=(k == 0), stop=False)
                    mm(ps, wh[:, k, :], lo[:, k, :], start=False, stop=False)
                    ins = mm(ps, wl[:, k, :], hi[:, k, :], start=False, stop=(k == KC - 1))
                ins.then_inc(unit_used, 1)
                return ins

            def row_unit(us, i, hi, lo, first, last, branch=False):
                take(us, i)
                wh, wl = w_hi[:, us % RING, :], w_lo[:, us % RING, :]
                for t in range(NT):
                    th, tl = hi[:, t * P:(t + 1) * P], lo[:, t * P:(t + 1) * P]
                    for half in range(2):
                        cols = slice(512 * half, 512 * half + 512)
                        ps = acc[:, 2 * t + half, :]
                        mm(ps, th, wh[:, cols], start=first, stop=False)
                        mm(ps, th, wl[:, cols], start=False, stop=False)
                        ins = mm(ps, tl, wh[:, cols], start=False, stop=last)
                    if t == 0 and last and branch:
                        ins.then_inc(acc_first, 1)
                ins.then_inc(unit_used, 1)

            def project(u0, hi, lo, branch=False):
                for k in range(KC):
                    row_unit(u0 + k, None, hi[:, k, :], lo[:, k, :], k == 0, k == KC - 1, branch)

            def transpose_rows(n, ready, value, sem_done):
                for t in range(NT):
                    pe.wait_ge(ready, value(t))
                    for half in range(2):
                        for k in range(4):
                            c = (4 * half + k) * P
                            ins = nc.tensor.transpose(hp[:, 2 * t + half, k * P:(k + 1) * P], xn[:, t, c:c + P], ident)
                        ins.then_inc(sem_done, 1)

            def pre(n, sets=1):
                transpose_rows(n, xn_ready, lambda t: 2 * n + t + 1, xT_ps)
                pre.ready += 4 * sets
                pe.wait_ge(xT_ready, pre.ready)
            pre.ready = 0

            pe.wait_ge(early_loaded, 16 * 12)
            nc.tensor.transpose(acc[:, 0, 0:96], rows[:, 0, :], const[0:96, C_ID:C_ID + 96])
            nc.tensor.transpose(acc[:, 1, 0:96], rows[:, 1, :], const[0:96, C_ID:C_ID + 96]).then_inc(rows_T, 1)
            pe.wait_ge(gains_ready, 1)
            pre(0)

            def mixer(js, i):
                us = U_MIX + 3 * js
                if js >= 2 or i is not None:
                    pe.wait_ge(y_ready, val(js - 1, i, 2))
                for kind in range(3):
                    feature_chunk(us + kind, i, mix_psum(js, kind), xh, xl)
            for js in range(2):
                mixer(js, None)
            turns(pe, 2, KC - 2, 2, mixer)
            pe.wait_ge(y_ready, KC)
            project(U_MIXO, yh, yl, True)
            pre(1)

            def down(us, i, js, cb, ring, first=False, last=False):
                pe.wait_ge(hid_ready, val(cb + js + 1, i, ring))
                row_unit(us, i, hh[:, js % ring, :], hl[:, js % ring, :], first, last, True)

            def swiglu(layer):
                u0, cb = U_FF[layer], NF * layer

                def gate_up(us, i, js):
                    for n in range(2):
                        feature_chunk(us + n, i, hp[:, 2 * (js % 2) + n, 0:T], xh, xl)

                def step(js, i):
                    us = u0 + 2 + 3 * js
                    gate_up(us, i, js + 1)
                    down(us + 2, i, js, cb, 2, first=(js == 0))
                gate_up(u0, None, 0)
                step(0, None)
                turns(pe, 1, NF - 2, 2, step)
                down(u0 + 3 * NF - 1, None, NF - 1, cb, 2, last=True)

            def relu2(layer):
                u0, cb = U_MLP[layer], 2 * NF + NM * layer

                def up(us, i, js):
                    feature_chunk(us, i, hp[:, js % 3, 0:T], xh, xl)

                def step(js, i):
                    us = u0 + 2 + 2 * js
                    up(us, i, js + 2)
                    down(us + 1, i, js, cb, 3, first=(js == 0))
                up(u0, None, 0)
                up(u0 + 1, None, 1)
                step(0, None)
                turns(pe, 1, NM - 3, 3, step)
                down(u0 + 2 * NM - 2, None, NM - 2, cb, 3)
                down(u0 + 2 * NM - 1, None, NM - 1, cb, 3, last=True)

            def heads(first, n, sink):
                dh = HD if sink else DH

                def qk(hd):
                    if sink:
                        rows_ = slice(HD * (hd % 2), HD * (hd % 2) + HD)
                        q_at, k_at = W_QT + (hd // 2) * T, W_KT + (hd // 4) * T
                        return work[rows_, q_at:q_at + T], work[rows_, k_at:k_at + T]
                    return wk(W_MQK + hd * T, T), wk(W_MQK + (NHD + hd) * T, T)

                def scores(hd):
                    i = first + hd
                    if i >= 2:
                        pe.wait_ge(s_made, i - 1)
                    q, k = qk(hd)
                    mm(acc[:, i % 2, 0:P], q[:, 0:P], k[:, 0:P], start=True, stop=True)
                    mm(acc[:, i % 2, P:384], q[:, P:T], k, start=True, stop=True).then_inc(sc_done, 1)

                def turn(hd):
                    i = first + hd
                    pe.wait_ge(p_ready, i + 1)
                    if i >= 2:
                        pe.wait_ge(pt_ready, i - 1)
                    s = wk(W_S + (i % 4) * 384, 384)
                    for b in range(3):
                        ins = nc.tensor.transpose(acc[:, 2 + i % 2, b * P:(b + 1) * P], s[:, b * P:(b + 1) * P], ident)
                    ins.then_inc(pt_ps, 1)

                def values(hd):
                    i = first + hd
                    pe.wait_ge(pt_ready, i + 1)
                    if i >= 2:
                        pe.wait_ge(o_made, i - 1)
                    pt = wk(W_PT + (i % 2) * 384, 384)
                    v = [wk((W_V + t * 256 + (hd // 4) * HD) if sink else (W_MV + t * D + hd * DH), dh) for t in range(NT)]
                    o = hp[:, i % 2, :]
                    mm(o[:, 0:dh], pt[:, 0:P], v[0], start=True, stop=True)
                    mm(o[:, dh:2 * dh], pt[:, P:2 * P], v[0], start=True, stop=False)
                    mm(o[:, dh:2 * dh], pt[:, 2 * P:3 * P], v[1], start=False, stop=True).then_inc(pv_done, 1)
                for k in range(n + 3):
                    if k < n:
                        scores(k)
                    if 2 <= k < n + 2:
                        turn(k - 2)
                    if k >= 3:
                        values(k - 3)

            swiglu(0)
            pre(2, 2)
            for n in range(4):
                us = U_KV + n
                take(us)
                for kk in range(2):
                    k, cols = 2 * n + kk, slice(512 * kk, 512 * kk + 512)
                    for t in range(NT):
                        rows_ = slice(t * P, (t + 1) * P)
                        mm(hp[:, t, :], xh[:, k, rows_], w_hi[:, us % RING, cols], start=(k == 0), stop=False)
                        mm(hp[:, t, :], xh[:, k, rows_], w_lo[:, us % RING, cols], start=False, stop=False)
                        ins = mm(hp[:, t, :], xl[:, k, rows_], w_hi[:, us % RING, cols], start=False, stop=(k == KC - 1))
                ins.then_inc(unit_used, 1)
            project(U_Q, yh, yl)
            for t in range(NT):
                pe.wait_ge(k_dup, t + 2)
                for g in range(NKV):
                    at = W_KDUP + t * 512 + g * P
                    ins = nc.tensor.transpose(hp[:, 2 + t, g * P:(g + 1) * P], wk(at, P), ident)
                ins.then_inc(kT_ps, 1)
            for t in range(NT):
                pe.wait_ge(rot_done, 2 * (2 + t + 1))
                if t == 1:
                    pe.wait_ge(kT_copied, NT)
                for half in range(2):
                    for k in range(4):
                        at = W_QTOK + t * D + (4 * half + k) * P
                        ins = nc.tensor.transpose(hp[:, 2 * t + half, k * P:(k + 1) * P], wk(at, P), ident)
                    ins.then_inc(qT_ps, 1)
            pe.wait_ge(qT_copied, 4)
            heads(0, NH, True)
            transpose_rows(0, o_made, lambda t: NH, oT_ps)
            pe.wait_ge(oT_ready, 4)
            project(U_O, xh, xl, True)
            pre(3)
            swiglu(1)
            pre(4)

            pe.wait_ge(late_loaded, 16 * 5)
            for t in range(NT):
                for k in range(KC):
                    for part, x in enumerate((xh, xl)):
                        ins = mm(acc[:, 0, 16 * t:16 * t + 16], x[:, k, t * P:(t + 1) * P].bitcast(F32), wba[:, k, :],
                                 start=(k == 0 and part == 0), stop=(k == KC - 1 and part == 1))
            ins.then_inc(ba_ps, 1)

            def dn_chunk(js, i):
                if js >= 3 or i is not None:
                    pe.wait_ge(conv_in, val(js - 2, i, BODY))
                feature_chunk(U_DN + js, i, small_psum(js % 3), xh, xl)
            for js in range(BODY):
                dn_chunk(js, None)
            turns(pe, BODY, 24 - BODY, BODY, dn_chunk)
            for j in range(24, 32):
                if j < 27:
                    pe.wait_ge(conv_in, j - 2)
                else:
                    pe.wait_ge(z_ready, j - 26)
                feature_chunk(U_DN + j, None, small_psum(j % 3), xh, xl)
            pe.wait_ge(ba_step, 7)
            mm(acc[:, 2, 0:16], const[:, C_INCL:C_INCL + P], pair[:, 3, :], start=True, stop=True)
            mm(acc[:, 2, 16:32], const[:, C_STRICT:C_STRICT + P], pair[:, 3, :], start=True, stop=True).then_inc(gc_ps, 1)
            pe.wait_ge(qk_sq, 4)
            for c in range(2 * 16):
                ins = mm(acc[:, 1, c:c + 1], wk(W_SQ + c * P, P), const[:, C_ONE:C_ONE + 1], start=True, stop=True)
            ins.then_inc(qk_ps, 1)
            pe.wait_ge(conv_silu, 24)
            pe.wait_ge(z_ready, 8)
            pe.wait_ge(ba_step, 14)

            for e, step, g in CORE_ORDER:
                if e != "pe":
                    continue
                bank = lambda b: core_bank(g, b)
                buf = lambda name: core_buf(g, name)

                def qT(p):
                    return qkvT(2 * g + p // 2)[:, (p % 2) * P:(p % 2 + 1) * P]

                def chunk_of(kind, p):
                    return qkvT(kind * NHD + 2 * g + p // 2)[:, (p % 2) * P:(p % 2 + 1) * P]
                pairs = range(4)
                if step == "kvT":
                    for p in pairs:
                        nc.tensor.transpose(bank(0)[:, p, :], chunk_of(1, p), ident)
                    for p in pairs:
                        ins = nc.tensor.transpose(bank(1)[:, p, :], chunk_of(2, p), ident)
                elif step == "decay":
                    core_wait(pe, "pool", "gs", g)
                    for p in pairs:
                        ins = mm(bank(2)[:, p, :], buf("gs")[:, p, :], const[:, C_INCL:C_INCL + P], start=True, stop=True)
                elif step == "knT":
                    core_wait(pe, "dve", "kscale", g)
                    for p in pairs:
                        nc.tensor.transpose(bank(0)[:, p, :], buf("kn")[:, p, :], ident)
                    for p in pairs:
                        ins = nc.tensor.transpose(bank(1)[:, p, :], buf("kb")[:, p, :], ident)
                elif step == "scores":
                    core_wait(pe, "act", "knT_copy", g)
                    if g >= 2:
                        core_wait(pe, "dve", "y", g - 2)
                    for p in pairs:
                        mm(bank(2)[:, p, :], buf("knT")[:, p, :], qT(p), start=True, stop=True)
                        ins = mm(bank(3)[:, p, :], buf("knT")[:, p, :], buf("kbT")[:, p, :], start=True, stop=True)
                elif step == "zT":
                    core_wait(pe, "dve", "z1", g)
                    for p in pairs:
                        ins = nc.tensor.transpose(bank(0)[:, p, :], buf("Z")[:, p, :], ident)
                elif step.startswith("y"):
                    n = int(step[1:])
                    if n == 1:
                        core_wait(pe, "act", "x1", g)
                    else:
                        core_wait(pe, "dve", f"xz{n - 1}", g)
                    for p in pairs:
                        ins = mm(bank(0)[:, p, :], buf("B")[:, p, :], buf("X")[:, p, :], start=True, stop=True)
                elif step.startswith("dxz"):
                    n = int(step[3:])
                    core_wait(pe, "act", f"y{n}_copy", g)
                    for p in pairs:
                        if n < LEVELS - 1:
                            mm(bank(1)[:, p, :], buf("Z")[:, p, :], buf("Y")[:, p, :], start=True, stop=True)
                        ins = mm(bank(2)[:, p, :], buf("Y")[:, p, :], buf("Z")[:, p, :], start=True, stop=True)
                elif step == "vn0":
                    core_wait(pe, "dve", f"xz{LEVELS - 1}", g)
                    for hd in range(2):
                        ins = mm(bank(0)[:, hd, :], buf("Z")[:, 2 * hd, :], buf("vb")[:, 2 * hd, :], start=True, stop=True)
                elif step == "state":
                    core_wait(pe, "act", "vn0_copy", g)
                    for hd in range(2):
                        ins = mm(bank(1)[:, hd, :], buf("kd")[:, 2 * hd, :], buf("vn")[:, 2 * hd, :], start=True, stop=True)
                elif step == "o0":
                    for hd in range(2):
                        ins = mm(bank(2)[:, 2 * hd, :], buf("attnT")[:, 2 * hd, :], buf("vn")[:, 2 * hd, :],
                                 start=True, stop=True)
                elif step == "kqs":
                    core_wait(pe, "act", "state_copy", g)
                    for hd in range(2):
                        mm(bank(3)[:, hd, :], buf("knT")[:, 2 * hd + 1, :], buf("SR")[:, hd, :], start=True, stop=True)
                        ins = mm(bank(3)[:, 2 + hd, :], qT(2 * hd + 1), buf("SR")[:, hd, :], start=True, stop=True)
                elif step == "vn1":
                    core_wait(pe, "dve", "rhs1", g)
                    for hd in range(2):
                        ins = mm(bank(0)[:, 2 + hd, :], buf("Z")[:, 2 * hd + 1, :], buf("SR")[:, 2 + hd, :],
                                 start=True, stop=True)
                elif step == "o1":
                    core_wait(pe, "act", "vn1_copy", g)
                    for hd in range(2):
                        ins = mm(bank(2)[:, 2 * hd + 1, :], buf("attnT")[:, 2 * hd + 1, :], buf("vn")[:, 2 * hd + 1, :],
                                 start=True, stop=True)
                else:
                    core_wait(pe, "dve", "on", g)
                    for p in pairs:
                        ins = nc.tensor.transpose(bank(3)[:, p, :], buf("o")[:, p, :], ident)
                ins.then_inc(core["pe"], 1)

            core_wait(pe, "dve", "yl", 3)
            project(U_DNO, yh, yl, True)
            pre(5)
            relu2(0)
            pre(6)

            def mb_chunk(js, i):
                if js >= 3 or i is not None:
                    pe.wait_ge(mb_copied, val(js - 2, i, BODY))
                feature_chunk(U_MB + js, i, small_psum(js % 3), xh, xl)
            for js in range(3):
                mb_chunk(js, None)
            turns(pe, 3, 2 * NHD - 3, BODY, mb_chunk)
            project(U_MBV, xh, xl)
            pe.wait_ge(mb_copied, 2 * NHD)
            pe.wait_ge(mbv_copied, NT)
            heads(NH, NHD, False)
            transpose_rows(0, o_made, lambda t: NH + NHD, oT_ps)
            pe.wait_ge(oT_ready, 8)
            project(U_MBO, xh, xl, True)
            pre(7)
            relu2(1)


_INS = ["x", "a_pre_norm", "a_w_in", "a_conv_w", "a_w_out", "a_post_norm", "ffn_pre_norm", "ffn_w_gate_up",
        "ffn_w_down", "ffn_post_norm", "kv_norm", "w_kv", "b_pre_norm", "b_w_q", "b_sinks", "b_w_o", "b_post_norm",
        "mix_norm_g_2", "mlp_norm_g_2", "dn_w_in_2", "dn_conv_w_2", "dn_a_log_2", "dn_dt_bias_2",
        "dn_out_norm_g_2", "dn_w_out_2", "mb_w_in_2", "mb_w_out_2", "mlp_w_up_2", "mlp_w_down_2", "final_norm_g_2"]


def constants():
    import numpy as np
    j, i = np.arange(P)[:, None], np.arange(P)[None, :]
    q, k = j, np.arange(T)[None, :]
    c = np.zeros((P, N_CONST), np.float32)
    c[:, C_ID:C_ID + P] = j == i
    c[:, C_INCL:C_INCL + P] = j <= i
    c[:, C_STRICT:C_STRICT + P] = j > i
    c[:, C_NEG:C_NEG + P] = -1.0 * (i > j)
    c[:, C_ONE:C_ONE + P] = 1.0
    c[:, C_BAND:C_BAND + P] = np.where(i <= j, 0.0, -1e30)
    c[:, C_BAND + P:C_BAND + 3 * P] = np.where((k <= q + P) & (k > q + P - 128), 0.0, -1e30)
    c[:, C_DIST:C_DIST + P] = np.where(i <= j, i - j, -1e30)
    c[:, C_DIST + P:C_DIST + 3 * P] = np.where(k <= q + P, k - q - P, -1e30)
    inv_freq = np.float32(500000.0) ** (-np.arange(0, 2 * ROT, 2, dtype=np.float32) / np.float32(2 * ROT))
    angle = (np.arange(T, dtype=np.float32)[:, None] * inv_freq[None, :]).reshape(NT, P, ROT).transpose(1, 0, 2)
    c[:, C_COS:C_COS + NT * ROT] = np.cos(angle).reshape(P, -1)
    c[:, C_SIN:C_SIN + NT * ROT] = np.sin(angle).reshape(P, -1)
    masks = np.zeros((P, 2 * LEVELS, P), np.float32)
    for n in range(LEVELS):
        b = 2 ** n
        low = (j // (2 * b) == i // (2 * b)) & (j % (2 * b) >= b) & (i % (2 * b) < b)
        masks[:, 2 * n, :] = low
        masks[:, 2 * n + 1, :] = low.T
    return c, masks


def kernel(**inputs):
    import numpy as _np
    import concourse.bacc as _bacc
    from concourse import mybir as _mybir
    from concourse.bass_utils import run_bass_kernel_spmd as _run

    nc = _bacc.Bacc("TRN2", target_bir_lowering=False, num_devices=1)
    arrays, args = {}, {}
    consts, masks = constants()
    given = {name: _np.ascontiguousarray(inputs[name]) for name in _INS}
    given["consts"], given["masks"] = consts, masks
    for name, v in given.items():
        arrays[f"in_{name}_dram"] = v
        args[name] = nc.dram_tensor(f"in_{name}_dram", v.shape, _mybir.dt.from_np(v.dtype), kind="ExternalInput").ap()
    out = nc.dram_tensor("out_0_dram", (1, T, D), F32, kind="ExternalOutput").ap()
    build(nc, args, out)
    r = _run(nc, [arrays], core_ids=[0])
    return r.results[0]["out_0_dram"]
```

```python
from contextlib import ExitStack

import concourse.bass as bass
from concourse import mybir

ALU = mybir.AluOpType
ACT = mybir.ActivationFunctionType
F32 = mybir.dt.float32
F32R = mybir.dt.float32r
U8 = mybir.dt.uint8
X = mybir.AxisListType.X

P = 128
T = 256
NT = T // P
D = 1024
KC = D // P
FF = 2816
NF = FF // P
FF2 = 4096
NM = FF2 // P
EPS = 1e-6
HD = 64
NH = 16
NKV = 4
ROT = 8
DH = 128
NHD = 8
SW_SCALE = HD ** -0.5
MB_SCALE = DH ** -0.5

RING = 6
RAW = 3
AHEAD = 4
BODY = RING

U_MIX = 0
U_MIXO = U_MIX + 3 * KC
U_FF = [U_MIXO + KC, 0]
U_KV = U_FF[0] + 3 * NF
U_Q = U_KV + 4
U_O = U_Q + KC
U_FF[1] = U_O + KC
U_DN = U_FF[1] + 3 * NF
U_DNO = U_DN + 4 * NHD
U_MLP = [U_DNO + KC, 0]
U_MB = U_MLP[0] + 2 * NM
U_MBV = U_MB + 2 * NHD
U_MBO = U_MBV + KC
U_MLP[1] = U_MBO + KC
N_UNITS = U_MLP[1] + 2 * NM
LAST_UNIT = [u - 1 for u in (U_FF[0], U_KV, U_FF[1], U_DN, U_MLP[0], U_MB, U_MLP[1], N_UNITS)]

G_A, G_F0, G_F1, G_KV, G_B, G_X0, G_X1, G_M0, G_M1 = [KC * n for n in range(9)]
G_CONV = 9 * KC
C_ID, C_INCL, C_STRICT, C_NEG, C_ONE = [P * n for n in range(5)]
C_BAND = C_ONE + 4
C_DIST = C_BAND + 3 * P
C_COS = C_DIST + 3 * P
C_SIN = C_COS + NT * ROT
N_CONST = C_SIN + NT * ROT
LEVELS = 7
DN_STRAIGHT = 3 * BODY

W_SG, W_HX = 0, 3 * T
W_CSB, W_CU, W_Y = 6 * T, 8 * T, 10 * T
W_QTOK, W_QT, W_KDUP, W_KT, W_V, W_RT = 0, 2048, 4096, 5120, 6144, 6656
W_S, W_PT = 7168, 7168 + 3 * 768
W_MQK, W_MV = 0, 4096
W_QKV, W_Z, W_GRP = 0, 24 * T, 32 * T
W_SQ, W_CBUF, W_YBUF = W_GRP, W_GRP + 16 * T, W_GRP + 16 * T + 3 * 260
N_WORK = W_GRP + 2 * 9 * 512
W_JUNK = N_WORK - 4 * D

CORE_HEAD = [("pool", "gs"), ("pe", "kvT"), ("pe", "decay"), ("dve", "kscale"), ("dve", "kd")]
CORE_BODY = [("act", "dec"), ("pool", "decmask"), ("pe", "knT"), ("act", "knT_copy"), ("act", "z_init"),
             ("pe", "scores"), ("dve", "attn"), ("dve", "b"), ("dve", "z0"), ("pe", "xT"), ("act", "x_copy")]
for _l in range(1, LEVELS):
    CORE_BODY += [("pe", f"y{_l}"), ("act", f"y{_l}_copy")]
    if 1 < _l:
        CORE_BODY += [("pe", f"zT{_l - 1}"), ("act", f"zT{_l - 1}_copy")]
    CORE_BODY += [("pe", f"d{_l}"), ("dve", f"x{_l}" if _l < LEVELS - 1 else "z_last")]
CORE_BODY += [("pe", "vn0"), ("act", "vn0_copy"), ("pe", "state"), ("act", "state_copy"), ("pe", "o0"),
              ("pe", "kqs"), ("dve", "rhs1"), ("dve", "t1"), ("pe", "vn1"), ("act", "vn1_copy"), ("pe", "o1")]
CORE_OUT = [("dve", "o"), ("act", "osq"), ("pool", "omean"), ("pool", "orstd")]
CORE_TAIL = [("dve", "on"), ("pe", "oT"), ("dve", "y"), ("dve", "yh"), ("dve", "yl")]
CORE_ORDER = [(e, s, g) for steps, groups in (
    (CORE_HEAD, (0, 1)), (CORE_BODY, (0, 1)), (CORE_HEAD[:1], (2, 3)), (CORE_OUT, (0, 1)),
    (CORE_HEAD[1:], (2, 3)), (CORE_TAIL, (0, 1)), (CORE_BODY, (2, 3)), (CORE_OUT, (2, 3)), (CORE_TAIL, (2, 3)))
              for e, s in steps for g in groups]
BA_IN, BA_G, BA_SUMS = 4, 8, 9


def core_value(engine, step, g):
    mine = [(s, k) for e, s, k in CORE_ORDER if e == engine]
    return mine.index((step, g)) + 1


def val(static, i, per):
    return static if i is None else i * per + static


def turns(eng, first, n, body, step):
    whole = n // body
    if whole > 1:
        with eng.Fori(0, whole) as i:
            for js in range(first, first + body):
                step(js, i)
        first, n = first + whole * body, n - whole * body
    for js in range(first, first + n):
        step(js, None)


def build(nc, a, out):
    ctx = ExitStack()
    with ctx:
        def sb(name, shape, dt=F32):
            return ctx.enter_context(nc.sbuf_tensor(name, shape, dt))

        def sem(name):
            return ctx.enter_context(nc.semaphore(name))

        w_raw = sb("w_raw", [P, RAW, 1024])
        w_hi = sb("w_hi", [P, RING, 1024], F32R)
        w_lo = sb("w_lo", [P, RING, 1024], F32R)
        h = sb("h", [P, NT, D])
        xh, xl = sb("xh", [P, KC, T], F32R), sb("xl", [P, KC, T], F32R)
        yh, yl = sb("yh", [P, KC, T], F32R), sb("yl", [P, KC, T], F32R)
        xn = sb("xn", [P, NT, D])
        xf = sb("xf", [P, 2, 512])
        gpost = sb("gpost", [P, 2, D])
        diag = sb("diag", [P, NT, P])
        hh, hl = sb("hh", [P, 3, T], F32R), sb("hl", [P, 3, T], F32R)
        work = sb("work", [P, N_WORK])
        const = sb("const", [P, N_CONST])
        lmask = sb("lmask", [P, 2 * LEVELS, P], U8)
        rows = work[0:96, W_CBUF:W_CBUF + 2 * P].rearrange("p (a n) -> p a n", a=2)
        wba = work[:, W_CBUF + 2 * P:W_CBUF + 3 * P].rearrange("p (k n) -> p k n", k=KC)
        gT = sb("gT", [P, 96])
        cT = sb("cT", [P, 96])
        og = sb("og", [P, 1])
        wba_split = sb("wba_split", [P, KC, 2, 16], F32R)
        sinks = sb("sinks", [P, NH])
        dtb, alog = sb("dtb", [P, NHD]), sb("alog", [P, NHD])
        sums = sb("sums", [P, 52])
        means = sb("means", [P, 52])
        rstd = sb("rstd", [P, 52])
        half_neg = sb("half_neg", [P, 32])
        mx = sb("mx", [P, 24, 2])
        nm = sb("nm", [P, 24, 2])
        dsk = sb("dsk", [P, NH, 2])
        es = sb("es", [P, NH, 2])
        den = sb("den", [P, 24, 2])
        dtot = sb("dtot", [P, 24, 2])
        rinv = sb("rinv", [P, 24, 2])
        ba = sb("ba", [P, NT, 16])
        sp = sb("sp", [P, 8, 16])
        qkss = sb("qkss", [P, 4, 16])
        pair = sb("pair", [P, 12, 16])
        oss = sb("oss", [P, 3, 16])

        acc = ctx.enter_context(nc.psum_tensor("acc", [P, 4, 512], F32))
        hp = ctx.enter_context(nc.psum_tensor("hp", [P, 4, 512], F32))

        ident = const[:, C_ID:C_ID + P]

        landed = [sem(f"landed{s}") for s in range(RAW)]
        hi_ready, lo_ready, unit_used = sem("hi_ready"), sem("lo_ready"), sem("unit_used")
        x_loaded, early_loaded, late_loaded, masks_loaded = (
            sem("x_loaded"), sem("early_loaded"), sem("late_loaded"), sem("masks_loaded"))
        gpost_loaded = [sem(f"gpost_loaded{s}") for s in range(2)]
        rows_T, gains_ready, pool_const = sem("rows_T"), sem("gains_ready"), sem("pool_const")
        pre_sq, pre_mean, pre_rstd = sem("pre_sq"), sem("pre_mean"), sem("pre_rstd")
        diag_ready, xT_ps, xf_ready, xhi_ready, xT_ready = (
            sem("diag_ready"), sem("xT_ps"), sem("xf_ready"), sem("xhi_ready"), sem("xT_ready"))
        acc_first, post_sq, post_mean, post_rstd = (
            sem("acc_first"), sem("post_sq"), sem("post_mean"), sem("post_rstd"))
        post_tmp, h_new, out_ready, stored = (
            sem("post_tmp"), sem("h_new"), sem("out_ready"), sem("stored"))
        c_copied, pad_zero, cu_step, y_ready = (
            sem("c_copied"), sem("pad_zero"), sem("cu_step"), sem("y_ready"))
        act_done, hid_mul, hid_hi, hid_ready = (
            sem("act_done"), sem("hid_mul"), sem("hid_hi"), sem("hid_ready"))
        kv_copied, q_copied = sem("kv_copied"), sem("q_copied")
        rot_mul, rot_done, k_dup = sem("rot_mul"), sem("rot_done"), sem("k_dup")
        kT_ps, kT_copied, qT_ps, qT_copied = sem("kT_ps"), sem("kT_copied"), sem("qT_ps"), sem("qT_copied")
        sc_done, s_made, mx_done, nm_ready = sem("sc_done"), sem("s_made"), sem("mx_done"), sem("nm_ready")
        dsk_ready, p_ready, pt_ps, pt_ready = sem("dsk_ready"), sem("p_ready"), sem("pt_ps"), sem("pt_ready")
        pv_done, den_ready, rinv_ready, o_made = (
            sem("pv_done"), sem("den_ready"), sem("rinv_ready"), sem("o_made"))
        oT_ps, oT_hi, oT_ready = sem("oT_ps"), sem("oT_hi"), sem("oT_ready")
        mb_copied, mbv_copied = sem("mb_copied"), sem("mbv_copied")
        wba_step, ba_ps, ba_step, ba_act, ba_pool = (
            sem("wba_step"), sem("ba_ps"), sem("ba_step"), sem("ba_act"), sem("ba_pool"))
        conv_in, conv_first, conv_step, conv_silu = (
            sem("conv_in"), sem("conv_first"), sem("conv_step"), sem("conv_silu"))
        z_ready, qk_sq, qk_ps = sem("z_ready"), sem("qk_sq"), sem("qk_ps")
        gc_ps = sem("gc_ps")
        core = {"pe": sem("core_tensor"), "act": sem("core_scalar"),
                "dve": sem("core_vector"), "pool": sem("core_pool")}

        def wk(at, n):
            return work[:, at:at + n]

        def small_psum(slot):
            return hp[:, slot, 0:T]

        def mix_psum(js, kind):
            return (acc if js % 2 == 0 else hp)[:, kind, 0:T]

        def core_bank(g, b):
            return (acc if g % 2 == 0 else hp)[:, b, :].rearrange("p (a n) -> p a n", a=4)

        def core_buf(g, name):
            where = {"kn": 0, "X": 0, "kb": 1, "Z": 1, "vb": 2, "kd": 3, "knT": 4, "y": 4,
                     "kbT": 5, "Y": 5, "decS": 6, "SR": 6, "attnT": 7, "B": 8, "t1": 8}
            if name in ("gs", "vn"):
                return xn[:, g % 2, 0:512].rearrange("p (a n) -> p a n", a=4)
            if name in ("decI", "o"):
                return xn[:, g % 2, 512:1024].rearrange("p (a n) -> p a n", a=4)
            at = W_GRP + ((g % 2) * 9 + where[name]) * 512
            return wk(at, 512).rearrange("p (a n) -> p a n", a=4)

        def qkvT(j):
            return work[:, W_QKV + j * T:W_QKV + (j + 1) * T]

        def score_buf(i):
            return wk(W_S + (i % 3) * 768, 768).rearrange("p (h n) -> p h n", h=2)

        def pt_buf(i):
            return wk(W_PT + (i % 2) * 768, 768).rearrange("p (h n) -> p h n", h=2)

        def each(tile, n=4):
            return tile.unsqueeze(1).broadcast_to([P, n, P])

        def per_pair(row, g):
            return pair[:, row, 4 * g:4 * g + 4].unsqueeze(2).broadcast_to([P, 4, P])

        def core_wait(eng, engine, step, g):
            eng.wait_ge(core[engine], core_value(engine, step, g))

        def wait_unit(eng, us, i=None):
            eng.wait_ge(unit_used, val(us + 1, i, BODY))

        def wait_h(eng, n, t, half):
            eng.wait_ge(h_new, 4 * (n - 1) + 2 * t + half + 1)

        def wait_acc(eng, m, t):
            if t == 0:
                eng.wait_ge(acc_first, m + 1)
            else:
                wait_unit(eng, LAST_UNIT[m])

        block = ctx.enter_context(nc.Block())

        @block.sync
        def _(sp_):
            x_t = a["x"].rearrange("b (t p) d -> p (b t) d", p=P)
            sp_.dma_start(h[:, :, :], x_t).then_inc(x_loaded, 16)

            sp_.dma_start(const[:, :], a["consts"]).then_inc(early_loaded, 16)

            def rows_in(at, k, vector):
                sp_.dma_start(rows[at:at + k, 0, :], vector).then_inc(early_loaded, 16)

            for at, name, l in ((G_A, "a_pre_norm", 0), (G_F0, "ffn_pre_norm", 0), (G_F1, "ffn_pre_norm", 1),
                                (G_B, "b_pre_norm", 0), (G_X0, "mix_norm_g_2", 0), (G_X1, "mix_norm_g_2", 1),
                                (G_M0, "mlp_norm_g_2", 0), (G_M1, "mlp_norm_g_2", 1)):
                rows_in(at, KC, a[name][l].rearrange("(k p) -> k p", p=P))
            rows_in(G_KV, KC, a["kv_norm"].rearrange("(k p) -> k p", p=P))
            rows_in(G_CONV, 3 * KC, a["a_conv_w"].rearrange("a w (k p) -> (a w k) p", p=P))
            sp_.dma_start(rows[:, 1, :], a["dn_conv_w_2"].rearrange("a w (k p) -> (a w k) p", p=P)) \
                .then_inc(early_loaded, 16)

            def late_loads():
                sp_.dma_start(og[:, :], a["dn_out_norm_g_2"].rearrange("a d -> d a")).then_inc(late_loaded, 16)
                sp_.dma_start(wba, a["dn_w_in_2"][0].rearrange("(k p) n -> p k n", p=P)[:, :, 4 * D:4 * D + 16]) \
                    .then_inc(late_loaded, 16)
                sp_.dma_start(sinks[:, :], a["b_sinks"].broadcast_to([P, NH])).then_inc(late_loaded, 16)
                sp_.dma_start(dtb[:, :], a["dn_dt_bias_2"].broadcast_to([P, NHD])).then_inc(late_loaded, 16)
                sp_.dma_start(alog[:, :], a["dn_a_log_2"].broadcast_to([P, NHD])).then_inc(late_loaded, 16)

            def load_gpost(p):
                vector = [a["a_post_norm"], a["ffn_post_norm"][0:1], a["b_post_norm"],
                          a["ffn_post_norm"][1:2], a["final_norm_g_2"].rearrange("(a d) -> a d", a=1)][p]
                if p >= 2:
                    sp_.wait_ge(h_new, 4 * (p - 2) + 4)
                sp_.dma_start(gpost[:, p % 2, :], vector.broadcast_to([P, D])).then_inc(gpost_loaded[p % 2], 16)

            def load(us, i, src, k):
                if us >= RAW or i is not None:
                    sp_.wait_ge(lo_ready, val(us - RAW + 1, i, BODY))
                sp_.dma_start(w_raw[:, us % RAW, :].rearrange("p (k n) -> p k n", k=k), src) \
                    .then_inc(landed[us % RAW], 16)

            def columns(w):
                return w.rearrange("(k p) n -> p k n", p=P)

            def col_chunk(w, start):
                return columns(w)[:, :, bass.ds(start, P)]

            def row_chunk(w, start):
                return w[bass.ds(start, P), :].unsqueeze(1)

            w_in = a["a_w_in"][0]

            def mixer(js, i):
                for n, kind in enumerate((1, 2, 0)):
                    us = U_MIX + 3 * js + n
                    src = col_chunk(w_in, val(kind * D + js * P, i, 2 * P))
                    load(us, i, src, KC)
            for js in range(2):
                mixer(js, None)
            load_gpost(0)
            load_gpost(1)
            late_loads()
            turns(sp_, 2, KC - 2, 2, mixer)

            def rows_of(u0, w, n=KC):
                for k in range(n):
                    load(u0 + k, None, row_chunk(w, k * P), 1)

            rows_of(U_MIXO, a["a_w_out"][0])

            def swiglu(layer):
                up, down = a["ffn_w_gate_up"][layer], a["ffn_w_down"][layer]
                u0 = U_FF[layer]
                load(u0, None, col_chunk(up, 0), KC)
                load(u0 + 1, None, col_chunk(up, FF), KC)

                def step(js, i):
                    us = u0 + 2 + 3 * js
                    load(us, i, col_chunk(up, val((js + 1) * P, i, 2 * P)), KC)
                    load(us + 1, i, col_chunk(up, val(FF + (js + 1) * P, i, 2 * P)), KC)
                    load(us + 2, i, row_chunk(down, val(js * P, i, 2 * P)), 1)
                step(0, None)
                turns(sp_, 1, NF - 2, 2, step)
                load(u0 + 3 * NF - 1, None, row_chunk(down, (NF - 1) * P), 1)

            def relu2(layer):
                up, down = a["mlp_w_up_2"][layer], a["mlp_w_down_2"][layer]
                u0 = U_MLP[layer]
                load(u0, None, col_chunk(up, 0), KC)
                load(u0 + 1, None, col_chunk(up, P), KC)

                def step(js, i):
                    us = u0 + 2 + 2 * js
                    load(us, i, col_chunk(up, val((js + 2) * P, i, 3 * P)), KC)
                    load(us + 1, i, row_chunk(down, val(js * P, i, 3 * P)), 1)
                step(0, None)
                turns(sp_, 1, NM - 3, 3, step)
                load(u0 + 2 * NM - 2, None, row_chunk(down, (NM - 2) * P), 1)
                load(u0 + 2 * NM - 1, None, row_chunk(down, (NM - 1) * P), 1)

            swiglu(0)
            load_gpost(2)
            w_kv = a["w_kv"].rearrange("(k p) n -> p k n", p=P)
            for n in range(4):
                load(U_KV + n, None, w_kv[:, 2 * n:2 * n + 2, :], 2)
            rows_of(U_Q, a["b_w_q"][0])
            rows_of(U_O, a["b_w_o"][0])
            load_gpost(3)
            swiglu(1)
            load_gpost(4)

            dn = a["dn_w_in_2"][0]
            turns(sp_, 0, 32, BODY, lambda js, i: load(U_DN + js, i, col_chunk(dn, val(js * P, i, BODY * P)), KC))
            rows_of(U_DNO, a["dn_w_out_2"][0])
            relu2(0)
            mb = a["mb_w_in_2"][0]
            turns(sp_, 0, 16, BODY, lambda js, i: load(U_MB + js, i, col_chunk(mb, val(js * P, i, BODY * P)), KC))
            rows_of(U_MBV, mb[:, 2 * D:3 * D])
            rows_of(U_MBO, a["mb_w_out_2"][0])
            relu2(1)

            for t in range(NT):
                sp_.wait_ge(out_ready, t + 1)
                sp_.dma_start(out[0, t * P:(t + 1) * P, :], xn[:, t, :]).then_inc(stored, 16)
            sp_.wait_ge(stored, 16 * NT)

        @block.gpsimd
        def _(pool):
            nc.gpsimd.memset(half_neg[:, :], -0.5).then_inc(pool_const, 1)
            pool.wait_ge(pool_const, 1)
            pool.dma_start(lmask[:, :, :], a["masks"]).then_inc(masks_loaded, 16)

            def pre(n, t):
                q, c = 2 * n + t, 4 * n + 2 * t
                pool.wait_ge(pre_sq, 2 * q + 2)
                nc.gpsimd.tensor_scalar(means[:, c:c + 1], sums[:, c:c + 1], sums[:, c + 1:c + 2], EPS,
                                        ALU.add, ALU.add).then_inc(pre_mean, 1)
                pool.wait_ge(pre_mean, q + 1)
                nc.gpsimd.tensor_tensor(rstd[:, c:c + 1], means[:, c:c + 1], half_neg[:, 0:1], ALU.pow) \
                    .then_inc(pre_rstd, 1)

            def post(m, t):
                e = 2 * m + t
                c = 36 + 2 * e
                pool.wait_ge(post_sq, 2 * e + 2)
                nc.gpsimd.tensor_scalar(means[:, c:c + 1], sums[:, c:c + 1], sums[:, c + 1:c + 2], EPS,
                                        ALU.add, ALU.add).then_inc(post_mean, 1)
                pool.wait_ge(post_mean, e + 1)
                nc.gpsimd.tensor_tensor(rstd[:, c:c + 1], means[:, c:c + 1], half_neg[:, 0:1], ALU.pow) \
                    .then_inc(post_rstd, 1)

            for t in range(NT):
                pre(0, t)
            for m in range(4):
                for t in range(NT):
                    post(m, t)
                    pre(m + 1, t)
            pool.wait_ge(ba_step, BA_SUMS)
            nc.gpsimd.tensor_scalar(qkss[:, 0:2, :], qkss[:, 2:4, :], 1.0, 1e-6, ALU.mult, ALU.add).then_inc(ba_pool, 1)
            pool.wait_ge(ba_pool, 1)
            nc.gpsimd.tensor_tensor(pair[:, 0:2, :], qkss[:, 0:2, :],
                                    half_neg[:, :].rearrange("p (a n) -> p a n", a=2), ALU.pow).then_inc(ba_pool, 1)
            pool.wait_ge(ba_step, BA_G)
            for e, step, g in CORE_ORDER:
                if e != "pool":
                    continue
                if step == "gs":
                    if g >= 2:
                        core_wait(pool, "pe", "o1", g - 2)
                    ins = nc.gpsimd.tensor_tensor(core_buf(g, "gs"), each(const[:, C_STRICT:C_STRICT + P]),
                                                  per_pair(3, g), ALU.mult)
                elif step == "decmask":
                    core_wait(pool, "act", "dec", g)
                    nc.gpsimd.tensor_tensor(core_buf(g, "decS"), core_buf(g, "decI"),
                                            each(const[:, C_NEG:C_NEG + P]), ALU.mult)
                    ins = nc.gpsimd.tensor_tensor(core_buf(g, "decI"), core_buf(g, "decI"),
                                                  each(const[:, C_INCL:C_INCL + P]), ALU.mult)
                elif step == "omean":
                    core_wait(pool, "act", "osq", g)
                    ins = nc.gpsimd.tensor_scalar(oss[:, 1, 4 * g:4 * g + 4], oss[:, 0, 4 * g:4 * g + 4],
                                                  1.0 / DH, EPS, ALU.mult, ALU.add)
                else:
                    core_wait(pool, "pool", "omean", g)
                    ins = nc.gpsimd.tensor_tensor(oss[:, 2, 4 * g:4 * g + 4], oss[:, 1, 4 * g:4 * g + 4],
                                                  half_neg[:, 0:4], ALU.pow)
                ins.then_inc(core["pool"], 1)
            for n in range(5, 9):
                for t in range(NT):
                    pre(n, t)

        @block.scalar
        def _(act):
            def split(us, i=None):
                if us >= N_UNITS:
                    return
                act.wait_ge(landed[us % RAW], val(16 * (us // RAW + 1), i, 16 * BODY // RAW))
                if us >= RING or i is not None:
                    act.wait_ge(unit_used, val(us - RING + 1, i, BODY))
                nc.scalar.activation(w_hi[:, us % RING, :], w_raw[:, us % RAW, :], ACT.Copy).then_inc(hi_ready, 1)

            def splits(u0, n):
                for u in range(u0, u0 + n):
                    split(u + AHEAD)

            def pre_square(n, t):
                for half in range(2):
                    c = 4 * n + 2 * t + half
                    if n == 0:
                        act.wait_ge(x_loaded, 16)
                    else:
                        wait_h(act, n, t, half)
                    nc.scalar.activation(wk(W_JUNK + 1024 * t + 512 * half, 512), h[:, t, 512 * half:512 * half + 512],
                                         ACT.Square, scale=D ** -0.5, accum_out=sums[:, c:c + 1]).then_inc(pre_sq, 1)

            def post_square(m, t):
                wait_acc(act, m, t)
                for half in range(2):
                    c = 36 + 4 * m + 2 * t + half
                    nc.scalar.activation(wk(W_JUNK + (2 + t) * D + 512 * half, 512), acc[:, 2 * t + half, :],
                                         ACT.Square, scale=D ** -0.5, accum_out=sums[:, c:c + 1]).then_inc(post_sq, 1)

            def pre_diag(n, t):
                if n == 0:
                    act.wait_ge(early_loaded, 16 * 12)
                act.wait_ge(pre_rstd, 2 * n + t + 1)
                nc.scalar.activation(diag[:, t, :], ident, ACT.Copy, scale=rstd[:, 4 * n + 2 * t:4 * n + 2 * t + 1]) \
                    .then_inc(diag_ready, 1)

            n_hi = [0]

            def pre_hi(hi, t, half):
                n_hi[0] += 1
                act.wait_ge(xf_ready, n_hi[0])
                nc.scalar.activation(hi[:, 4 * half:4 * half + 4, t * P:(t + 1) * P],
                                     xf[:, n_hi[0] % 2, :].rearrange("p (k n) -> p k n", k=4), ACT.Copy) \
                    .then_inc(xhi_ready, 1)

            def norm(n, post, his=None):
                his = his or [xh]
                if post:
                    post_square(n - 1, 0)
                pre_square(n, 0)
                if post:
                    post_square(n - 1, 1)
                if n:
                    pre_diag(n, 0)
                pre_square(n, 1)
                if not n:
                    pre_diag(n, 0)
                pre_hi(his[0], 0, 0)
                pre_diag(n, 1)
                for r, hi in enumerate(his):
                    for t in range(NT):
                        for half in range(2):
                            if r or t or half:
                                pre_hi(hi, t, half)

            norm(0, False)
            for u in range(AHEAD):
                split(u)

            def mixer(js, i):
                us = U_MIX + 3 * js
                split(us + AHEAD, i)
                split(us + AHEAD + 1, i)
                wait_unit(act, us, i)
                if js >= 2 or i is not None:
                    act.wait_ge(y_ready, val(js - 1, i, 2))
                nc.scalar.activation(wk(W_CSB + (js % 2) * T, T), mix_psum(js, 0), ACT.Copy).then_inc(c_copied, 1)
                split(us + AHEAD + 2, i)
            for js in range(2):
                mixer(js, None)
            turns(act, 2, KC - 2, 2, mixer)
            splits(U_MIXO, KC)
            norm(1, True)

            def swiglu(layer):
                u0, fb = U_FF[layer], NF * layer

                def silu(js, i, unit):
                    wait_unit(act, unit, i)
                    if fb + js >= 2 or i is not None:
                        act.wait_ge(hid_mul, val(fb + js - 1, i, 2))
                    nc.scalar.activation(wk(W_SG + (js % 2) * T, T), hp[:, 2 * (js % 2), 0:T], ACT.Silu) \
                        .then_inc(act_done, 1)
                split(u0 + AHEAD)
                split(u0 + AHEAD + 1)
                silu(0, None, u0)

                def step(js, i):
                    us = u0 + 2 + 3 * js
                    split(us + AHEAD, i)
                    split(us + AHEAD + 1, i)
                    silu(js + 1, i, us)
                    split(us + AHEAD + 2, i)
                step(0, None)
                turns(act, 1, NF - 2, 2, step)
                split(u0 + 3 * NF - 1 + AHEAD)

            def relu2(layer):
                u0, cb = U_MLP[layer], 2 * NF + NM * layer

                def relu(js, i, unit):
                    wait_unit(act, unit, i)
                    act.wait_ge(hid_mul, val(cb + js - 2, i, 3))
                    nc.scalar.activation(wk(W_SG + (js % 3) * T, T), hp[:, js % 3, 0:T], ACT.Relu) \
                        .then_inc(act_done, 1)
                split(u0 + AHEAD)
                relu(0, None, u0)
                split(u0 + AHEAD + 1)
                relu(1, None, u0 + 1)

                def step(js, i):
                    us = u0 + 2 + 2 * js
                    split(us + AHEAD, i)
                    split(us + AHEAD + 1, i)
                    relu(js + 2, i, us)
                step(0, None)
                turns(act, 1, NM - 3, 3, step)
                split(u0 + 2 * NM - 2 + AHEAD)
                split(u0 + 2 * NM - 1 + AHEAD)

            def heads(first, n, scale, sink):
                def exp(k):
                    i = first + k
                    s = score_buf(i)
                    act.wait_ge(nm_ready, i + 1)
                    if sink:
                        act.wait_ge(dsk_ready, i + 1)
                        nc.scalar.activation(es[:, 2 * i:2 * i + 2, :], dsk[:, 2 * i:2 * i + 2, :], ACT.Exp)
                    for hd in range(2):
                        for t, cols in enumerate((slice(0, P), slice(P, 384))):
                            ins = nc.scalar.activation(s[:, hd, cols], s[:, hd, cols], ACT.Exp,
                                                       bias=nm[:, 2 * i + hd, t:t + 1], scale=scale,
                                                       accum_out=den[:, 2 * i + hd, t:t + 1])
                    ins.then_inc(p_ready, 1)

                def pt_copy(k):
                    i = first + k
                    act.wait_ge(pt_ps, i + 1)
                    if i >= 2:
                        act.wait_ge(pv_done, i - 1)
                    nc.scalar.activation(pt_buf(i), hp[:, 0:2, 0:384], ACT.Copy).then_inc(pt_ready, 1)
                for k in range(n + 2):
                    if 1 <= k <= n:
                        exp(k - 1)
                    if k >= 2:
                        pt_copy(k - 2)

            swiglu(0)
            norm(2, True, [xh, yh])
            splits(U_KV, 4)
            for t in range(NT):
                wait_unit(act, U_Q - 1)
                nc.scalar.activation(wk(W_KDUP + t * 512, 512).rearrange("p (g c n) -> p g c n", g=4, c=2)[:, :, 0, :],
                                     acc[:, 2 + t, 0:256].rearrange("p (g n) -> p g n", g=4), ACT.Copy)
                nc.scalar.activation(wk(W_V + t * 256, 256), acc[:, 2 + t, 256:512], ACT.Copy).then_inc(kv_copied, 1)
            splits(U_Q, KC)
            for t in range(NT):
                wait_unit(act, U_O - 1)
                nc.scalar.activation(wk(W_QTOK + t * D, D).rearrange("p (a n) -> p a n", a=2), acc[:, 2 * t:2 * t + 2, :],
                                     ACT.Copy).then_inc(q_copied, 1)
            for t in range(NT):
                act.wait_ge(kT_ps, t + 1)
                nc.scalar.activation(wk(W_KT, 1024).rearrange("p (g n) -> p g n", g=4)[:, :, t * P:(t + 1) * P],
                                     hp[:, 2 + t, :].rearrange("p (g n) -> p g n", g=4), ACT.Copy).then_inc(kT_copied, 1)
            for t in range(NT):
                for half in range(2):
                    act.wait_ge(qT_ps, 2 * t + half + 1)
                    nc.scalar.activation(
                        wk(W_QT + half * 1024, 1024).rearrange("p (g n) -> p g n", g=4)[:, :, t * P:(t + 1) * P],
                        hp[:, 2 * t + half, :].rearrange("p (g n) -> p g n", g=4), ACT.Copy).then_inc(qT_copied, 1)
            heads(0, NH // 2, 1.0, True)
            splits(U_O, KC)
            norm(3, True)
            swiglu(1)
            norm(4, True)

            def gates():
                act.wait_ge(ba_step, BA_IN)
                nc.scalar.activation(sp[:, 0, :].rearrange("p (h t) -> p h t", t=2),
                                     ba[:, :, 0:8].rearrange("p t h -> p h t"), ACT.Exp, scale=-1.0)
                nc.scalar.activation(sp[:, 2, :], sp[:, 1, :], ACT.Exp, scale=-1.0)
                nc.scalar.activation(sp[:, 3, 0:8], alog[:, :], ACT.Exp).then_inc(ba_act, 1)
                act.wait_ge(ba_act, 1)
                nc.scalar.activation(sp[:, 4, :], sp[:, 2, :], ACT.Ln, bias=1.0).then_inc(ba_act, 1)

            def conv(js, i):
                split(U_DN + js + AHEAD, i)
                if js >= 2 or i is not None:
                    silu(js - 2, i)
                wait_unit(act, U_DN + js, i)
                c, y = W_CBUF + (js % 3) * 260, W_YBUF + (js % 3) * T
                if js >= 3 or i is not None:
                    act.wait_ge(conv_step, val(3 * (js - 2), i, 3 * BODY))
                nc.scalar.activation(wk(c + 3, T), small_psum(js % 3), ACT.Copy).then_inc(conv_in, 1)
                act.wait_ge(conv_in, val(js + 1, i, BODY))
                if js >= 3 or i is not None:
                    act.wait_ge(conv_silu, val(js - 2, i, BODY))
                nc.scalar.activation(wk(y, T), wk(c, T), ACT.Copy, scale=cT[:, bass.ds(val(js, i, BODY), 1)]) \
                    .then_inc(conv_first, 1)

            def silu(js, i):
                act.wait_ge(conv_step, val(3 * (js + 1), i, 3 * BODY))
                at = val(W_QKV + js * T, i, BODY * T)
                nc.scalar.activation(work[:, bass.ds(at, T)], wk(W_YBUF + (js % 3) * T, T), ACT.Silu) \
                    .then_inc(conv_silu, 1)
            for js in range(BODY):
                conv(js, None)
                if js == 3:
                    gates()
            turns(act, BODY, DN_STRAIGHT - BODY, BODY, conv)
            for js in range(DN_STRAIGHT, 24):
                conv(js, None)
                if js - DN_STRAIGHT < 4:
                    part = js - DN_STRAIGHT
                    if part == 3:
                        act.wait_ge(conv_silu, 16)
                    nc.scalar.activation(wk(W_SQ + part * 4 * T, 4 * T), wk(W_QKV + part * 4 * T, 4 * T), ACT.Square) \
                        .then_inc(qk_sq, 1)
            silu(22, None)
            silu(23, None)
            for j in range(24, 32):
                split(U_DN + j + AHEAD)
                wait_unit(act, U_DN + j)
                nc.scalar.activation(wk(W_Z + (j - 24) * T, T), small_psum(j % 3), ACT.Silu).then_inc(z_ready, 1)
            act.wait_ge(gc_ps, 1)
            nc.scalar.activation(pair[:, 4:6, :], acc[:, 2, 0:32].rearrange("p (a n) -> p a n", a=2), ACT.Exp) \
                .then_inc(ba_act, 1)

            for e, step, g in CORE_ORDER:
                if e != "act":
                    continue
                bank = lambda b: core_bank(g, b)
                buf = lambda name: core_buf(g, name)
                if step == "dec":
                    core_wait(act, "pe", "decay", g)
                    if g >= 2:
                        core_wait(act, "pe", "oT", g - 2)
                    ins = nc.scalar.activation(buf("decI"), bank(2), ACT.Exp)
                elif step == "knT_copy":
                    core_wait(act, "pe", "knT", g)
                    if g >= 2:
                        core_wait(act, "dve", "yl", g - 2)
                    nc.scalar.activation(buf("knT"), bank(0), ACT.Copy)
                    ins = nc.scalar.activation(buf("kbT"), bank(1), ACT.Copy)
                elif step == "z_init":
                    ins = nc.scalar.activation(buf("Z"), each(ident), ACT.Copy)
                elif step == "x_copy":
                    core_wait(act, "pe", "xT", g)
                    core_wait(act, "dve", "kd", g)
                    ins = nc.scalar.activation(buf("X"), bank(0), ACT.Copy)
                elif step.startswith("zT"):
                    core_wait(act, "pe", step[:-5], g)
                    ins = nc.scalar.activation(buf("Z"), bank(2), ACT.Copy)
                elif step.startswith("y"):
                    core_wait(act, "pe", step[:-5], g)
                    ins = nc.scalar.activation(buf("Y"), bank(0), ACT.Copy)
                elif step == "vn0_copy":
                    core_wait(act, "pe", "vn0", g)
                    ins = nc.scalar.activation(buf("vn")[:, 0:3:2, :], bank(0)[:, 0:2, :], ACT.Copy)
                elif step == "state_copy":
                    core_wait(act, "pe", "state", g)
                    ins = nc.scalar.activation(buf("SR")[:, 0:2, :], bank(1)[:, 0:2, :], ACT.Copy)
                elif step == "vn1_copy":
                    core_wait(act, "pe", "vn1", g)
                    ins = nc.scalar.activation(buf("vn")[:, 1:4:2, :], bank(0)[:, 2:4, :], ACT.Copy)
                else:
                    core_wait(act, "dve", "o", g)
                    for p in range(4):
                        ins = nc.scalar.activation(buf("kbT")[:, p, :], buf("o")[:, p, :], ACT.Square,
                                                   accum_out=oss[:, 0, 4 * g + p:4 * g + p + 1])
                ins.then_inc(core["act"], 1)

            splits(U_DNO, KC)
            norm(5, False)
            relu2(0)
            norm(6, False)

            def qk_copy(js, i):
                split(U_MB + js + AHEAD, i)
                wait_unit(act, U_MB + js, i)
                nc.scalar.activation(work[:, bass.ds(val(W_MQK + js * T, i, BODY * T), T)], small_psum(js % 3),
                                     ACT.Copy).then_inc(mb_copied, 1)
            turns(act, 0, 16, BODY, qk_copy)
            splits(U_MBV, KC)
            for t in range(NT):
                wait_unit(act, U_MBO - 1)
                nc.scalar.activation(wk(W_MV + t * D, D).rearrange("p (a n) -> p a n", a=2), acc[:, 2 * t:2 * t + 2, :],
                                     ACT.Copy).then_inc(mbv_copied, 1)
            heads(NH // 2, NHD // 2, MB_SCALE, False)
            splits(U_MBO, KC)
            norm(7, False)
            relu2(1)
            for t in range(NT):
                pre_square(8, t)

        @block.vector
        def _(dve):
            def split(us, i=None):
                if us >= N_UNITS:
                    return
                dve.wait_ge(hi_ready, val(us + 1, i, BODY))
                nc.vector.tensor_tensor(w_lo[:, us % RING, :], w_raw[:, us % RAW, :],
                                        w_hi[:, us % RING, :].bitcast(F32), ALU.subtract).then_inc(lo_ready, 1)

            def splits(u0, n):
                for u in range(u0, u0 + n):
                    split(u + AHEAD)

            n_hi = [0]

            def pre(n, gains):
                for gain, hi, lo in gains:
                    for t in range(NT):
                        for half in range(2):
                            n_f = n_hi[0] + half + 1
                            dve.wait_ge(xT_ps, 4 * n + 2 * t + half + 1)
                            if n_f > 2:
                                dve.wait_ge(xT_ready, n_f - 2)
                            nc.vector.tensor_tensor(
                                xf[:, n_f % 2, :].rearrange("p (k n) -> p k n", k=4),
                                hp[:, 2 * t + half, :].rearrange("p (k n) -> p k n", k=4),
                                gT[:, gain + 4 * half:gain + 4 * half + 4].unsqueeze(2).broadcast_to([P, 4, P]),
                                ALU.mult).then_inc(xf_ready, 1)
                        for half in range(2):
                            n_hi[0] += 1
                            at = (slice(None), slice(4 * half, 4 * half + 4), slice(t * P, (t + 1) * P))
                            dve.wait_ge(xhi_ready, n_hi[0])
                            nc.vector.tensor_tensor(
                                lo[at], xf[:, n_hi[0] % 2, :].rearrange("p (k n) -> p k n", k=4),
                                hi[at].bitcast(F32), ALU.subtract).then_inc(xT_ready, 1)

            def post(m):
                dve.wait_ge(gpost_loaded[m % 2], 16 * (m // 2 + 1))
                for t in range(NT):
                    e = 2 * m + t
                    for half in range(2):
                        cols = slice(512 * half, 512 * half + 512)
                        dve.wait_ge(post_sq, 2 * e + half + 1)
                        nc.vector.tensor_tensor(xn[:, t, cols], acc[:, 2 * t + half, :], gpost[:, m % 2, cols],
                                                ALU.mult).then_inc(post_tmp, 1)
                    dve.wait_ge(post_tmp, 2 * e + 2)
                    dve.wait_ge(post_rstd, e + 1)
                    for half in range(2):
                        at = (slice(None), t, slice(512 * half, 512 * half + 512))
                        nc.vector.scalar_tensor_tensor(out=h[at], in0=xn[at], scalar=rstd[:, 36 + 2 * e:37 + 2 * e],
                                                       in1=h[at], op0=ALU.mult, op1=ALU.add).then_inc(h_new, 1)

            def residual(m):
                for t in range(NT):
                    wait_acc(dve, m, t)
                    for half in range(2):
                        at = (slice(None), t, slice(512 * half, 512 * half + 512))
                        nc.vector.tensor_tensor(h[at], acc[:, 2 * t + half, :], h[at], ALU.add).then_inc(h_new, 1)

            dve.wait_ge(rows_T, 1)
            nc.vector.tensor_copy(gT[:, :], acc[:, 0, 0:96])
            nc.vector.tensor_copy(cT[:, :], acc[:, 1, 0:96]).then_inc(gains_ready, 1)
            dve.wait_ge(gains_ready, 1)
            nc.vector.memset(wk(W_CU, 2), 0.0).then_inc(pad_zero, 1)
            dve.wait_ge(pad_zero, 1)
            pre(0, [(G_A, xh, xl)])
            for u in range(AHEAD):
                split(u)

            def mixer(js, i):
                us = U_MIX + 3 * js
                for n in range(3):
                    split(us + AHEAD + n, i)
                cu = wk(W_CU, T + 2)
                y = wk(W_Y + (js % 2) * T, T)

                def tap(w):
                    return gT[:, bass.ds(val(G_CONV + w * KC + js, i, 2), 1)]

                def done(ins, n):
                    ins.then_inc(cu_step, 1)
                    dve.wait_ge(cu_step, val(6 * js + n, i, 12))
                dve.wait_ge(c_copied, val(js + 1, i, 2))
                wait_unit(dve, us + 2, i)
                done(nc.vector.tensor_tensor(cu[:, 2:T + 2], mix_psum(js, 1), wk(W_CSB + (js % 2) * T, T), ALU.mult), 1)
                done(nc.vector.tensor_scalar(y, cu[:, 0:T], tap(0), None, ALU.mult), 2)
                done(nc.vector.scalar_tensor_tensor(out=y, in0=cu[:, 1:T + 1], scalar=tap(1), in1=y,
                                                    op0=ALU.mult, op1=ALU.add), 3)
                done(nc.vector.scalar_tensor_tensor(out=y, in0=cu[:, 2:T + 2], scalar=tap(2), in1=y,
                                                    op0=ALU.mult, op1=ALU.add), 4)
                done(nc.vector.tensor_tensor(y, mix_psum(js, 2), y, ALU.mult), 5)
                chunk = bass.ds(val(js, i, 2), 1)
                done(nc.vector.tensor_copy(yh[:, chunk, :], y.unsqueeze(1)), 6)
                nc.vector.tensor_tensor(yl[:, chunk, :], y.unsqueeze(1), yh[:, chunk, :].bitcast(F32),
                                        ALU.subtract).then_inc(y_ready, 1)
            for js in range(2):
                mixer(js, None)
            turns(dve, 2, KC - 2, 2, mixer)
            splits(U_MIXO, KC)
            post(0)
            pre(1, [(G_F0, xh, xl)])

            def hidden(js, i, cb, ring, up_bank, unit):
                n = lambda d: val(cb + js + d, i, ring)
                sg, hx = wk(W_SG + (js % ring) * T, T), wk(W_HX + (js % ring) * T, T)
                dve.wait_ge(act_done, n(1))
                wait_unit(dve, unit, i)
                nc.vector.tensor_tensor(hx, hp[:, up_bank, 0:T], sg, ALU.mult).then_inc(hid_mul, 1)
                dve.wait_ge(hid_mul, n(1))
                nc.vector.tensor_copy(hh[:, js % ring, :], hx).then_inc(hid_hi, 1)
                dve.wait_ge(hid_hi, n(1))
                nc.vector.tensor_tensor(hl[:, js % ring, :], hx, hh[:, js % ring, :].bitcast(F32), ALU.subtract) \
                    .then_inc(hid_ready, 1)

            def swiglu(layer):
                u0, cb = U_FF[layer], NF * layer
                split(u0 + AHEAD)
                split(u0 + AHEAD + 1)
                hidden(0, None, cb, 2, 1, u0 + 1)

                def step(js, i):
                    us = u0 + 2 + 3 * js
                    for n in range(3):
                        split(us + AHEAD + n, i)
                    if js >= 1 or i is not None:
                        wait_unit(dve, us - 1, i)
                    hidden(js + 1, i, cb, 2, 2 * ((js + 1) % 2) + 1, us + 1)
                step(0, None)
                turns(dve, 1, NF - 2, 2, step)
                split(u0 + 3 * NF - 1 + AHEAD)

            def relu2(layer):
                u0, cb = U_MLP[layer], 2 * NF + NM * layer
                split(u0 + AHEAD)
                hidden(0, None, cb, 3, 0, u0)
                split(u0 + AHEAD + 1)
                hidden(1, None, cb, 3, 1, u0 + 1)

                def step(js, i):
                    us = u0 + 2 + 2 * js
                    split(us + AHEAD, i)
                    split(us + AHEAD + 1, i)
                    if js >= 1 or i is not None:
                        wait_unit(dve, us - 1, i)
                    hidden(js + 2, i, cb, 3, (js + 2) % 3, us)
                step(0, None)
                turns(dve, 1, NM - 3, 3, step)
                split(u0 + 2 * NM - 2 + AHEAD)
                split(u0 + 2 * NM - 1 + AHEAD)

            def rotary(n, view, t, nh):
                t1, t2 = view[:, :, 0:ROT], view[:, :, ROT:2 * ROT]
                cos = const[:, C_COS + t * ROT:C_COS + (t + 1) * ROT].unsqueeze(1).broadcast_to([P, nh, ROT])
                sin = const[:, C_SIN + t * ROT:C_SIN + (t + 1) * ROT].unsqueeze(1).broadcast_to([P, nh, ROT])
                r = [wk(W_RT + k * P, nh * ROT).rearrange("p (g n) -> p g n", g=nh) for k in range(4)]
                if n:
                    dve.wait_ge(rot_done, 2 * n)
                for k, (u, v) in enumerate(((t1, cos), (t2, sin), (t2, cos), (t1, sin))):
                    nc.vector.tensor_tensor(r[k], u, v, ALU.mult).then_inc(rot_mul, 1)
                dve.wait_ge(rot_mul, 4 * (n + 1))
                nc.vector.tensor_tensor(t1, r[0], r[1], ALU.subtract).then_inc(rot_done, 1)
                nc.vector.tensor_tensor(t2, r[2], r[3], ALU.add).then_inc(rot_done, 1)

            def heads(first, n, sink):
                def scores(k):
                    i = first + k
                    s = score_buf(i)
                    of = slice(2 * i, 2 * i + 2)
                    dve.wait_ge(sc_done, i + 1)
                    if i >= 3:
                        dve.wait_ge(pt_ps, i - 2)
                    ps = acc[:, 2 * (i % 2):2 * (i % 2) + 2, 0:384]
                    if sink:
                        ins = nc.vector.scalar_tensor_tensor(
                            out=s, in0=ps, scalar=SW_SCALE, op0=ALU.mult, op1=ALU.add,
                            in1=const[:, C_BAND:C_BAND + 384].unsqueeze(1).broadcast_to([P, 2, 384]))
                    else:
                        for hd in range(2):
                            slope = 2.0 ** (-8.0 * (2 * k + hd + 1) / NHD)
                            ins = nc.vector.scalar_tensor_tensor(out=s[:, hd, :], in0=const[:, C_DIST:C_DIST + 384],
                                                                 scalar=slope / MB_SCALE, in1=ps[:, hd, :],
                                                                 op0=ALU.mult, op1=ALU.add)
                    ins.then_inc(s_made, 1)
                    dve.wait_ge(s_made, i + 1)
                    nc.vector.tensor_reduce(mx[:, of, 0], s[:, :, 0:P], X, ALU.max, negate=True).then_inc(mx_done, 1)
                    nc.vector.tensor_reduce(mx[:, of, 1], s[:, :, P:384], X, ALU.max, negate=True).then_inc(mx_done, 1)
                    dve.wait_ge(mx_done, 2 * (i + 1))
                    if sink:
                        neg_sink = pair[:, 11, 2 * k:2 * k + 2].unsqueeze(2).broadcast_to([P, 2, 2])
                        nc.vector.tensor_tensor(nm[:, of, :], mx[:, of, :], neg_sink, ALU.min).then_inc(nm_ready, 1)
                        dve.wait_ge(nm_ready, i + 1)
                        nc.vector.tensor_tensor(dsk[:, of, :], nm[:, of, :], neg_sink, ALU.subtract) \
                            .then_inc(dsk_ready, 1)
                    else:
                        nc.vector.tensor_scalar(nm[:, of, :], mx[:, of, :], MB_SCALE, None, ALU.mult) \
                            .then_inc(nm_ready, 1)

                def norm(k):
                    i = first + k
                    dh = HD if sink else DH
                    of = slice(2 * i, 2 * i + 2)
                    dve.wait_ge(p_ready, i + 1)
                    total = den
                    if sink:
                        nc.vector.tensor_tensor(dtot[:, of, :], den[:, of, :], es[:, of, :], ALU.add).then_inc(den_ready, 1)
                        dve.wait_ge(den_ready, i + 1)
                        total = dtot
                    nc.vector.reciprocal(rinv[:, of, :], total[:, of, :]).then_inc(rinv_ready, 1)
                    dve.wait_ge(rinv_ready, i + 1)
                    dve.wait_ge(pv_done, i + 1)
                    nc.vector.tensor_tensor(
                        xn[:, :, 2 * k * dh:(2 * k + 2) * dh].rearrange("p t (h n) -> p t h n", h=2),
                        hp[:, 2 + i % 2, 0:4 * dh].rearrange("p (t h n) -> p t h n", t=2, h=2),
                        rinv[:, of, :].rearrange("p h t -> p t h").unsqueeze(3).broadcast_to([P, 2, 2, dh]),
                        ALU.mult).then_inc(o_made, 1)
                for k in range(n + 3):
                    if k < n:
                        scores(k)
                    if k >= 3:
                        norm(k - 3)

            def out_T(s, hi, lo):
                for k in range(4):
                    t, half = k // 2, k % 2
                    n = 4 * s + k + 1
                    at = (slice(None), slice(4 * half, 4 * half + 4), slice(t * P, (t + 1) * P))
                    ps = hp[:, k, :].rearrange("p (k n) -> p k n", k=4)
                    dve.wait_ge(oT_ps, n)
                    nc.vector.tensor_copy(hi[at], ps).then_inc(oT_hi, 1)
                    dve.wait_ge(oT_hi, n)
                    nc.vector.tensor_tensor(lo[at], ps, hi[at].bitcast(F32), ALU.subtract).then_inc(oT_ready, 1)

            swiglu(0)
            post(1)
            pre(2, [(G_KV, xh, xl), (G_B, yh, yl)])
            dve.wait_ge(late_loaded, 16 * 5)
            nc.vector.tensor_copy(wba_split[:, :, 0, :], wba).then_inc(wba_step, 1)
            dve.wait_ge(wba_step, 1)
            nc.vector.tensor_tensor(wba_split[:, :, 1, :], wba, wba_split[:, :, 0, :].bitcast(F32), ALU.subtract) \
                .then_inc(wba_step, 1)
            splits(U_KV, 4)
            dve.wait_ge(late_loaded, 16 * 5)
            nc.vector.tensor_scalar(pair[:, 11, :], sinks[:, :], -1.0, None, ALU.mult).then_inc(k_dup, 1)
            dve.wait_ge(k_dup, 1)
            for t in range(NT):
                dve.wait_ge(kv_copied, t + 1)
                kd = wk(W_KDUP + t * 512, 512).rearrange("p (g c n) -> p g c n", g=4, c=2)
                rotary(t, kd[:, :, 0, :], t, NKV)
                dve.wait_ge(rot_done, 2 * (t + 1))
                nc.vector.tensor_copy(kd[:, :, 1, :], kd[:, :, 0, :]).then_inc(k_dup, 1)
            splits(U_Q, KC)
            for t in range(NT):
                dve.wait_ge(q_copied, t + 1)
                rotary(2 + t, wk(W_QTOK + t * D, D).rearrange("p (g n) -> p g n", g=NH), t, NH)
            heads(0, NH // 2, True)
            out_T(0, xh, xl)
            splits(U_O, KC)
            post(2)
            pre(3, [(G_F1, xh, xl)])
            swiglu(1)
            nc.vector.memset(wk(W_CBUF, 3 * 260), 0.0).then_inc(pad_zero, 1)
            post(3)
            dve.wait_ge(pad_zero, 2)
            pre(4, [(G_X0, xh, xl)])

            def gate_inputs():
                dve.wait_ge(ba_ps, NT)
                two = acc[:, 0, 0:64].rearrange("p (t s n) -> p t s n", t=2, s=2)
                nc.vector.tensor_copy(ba[:, :, :], two[:, :, 0, :]).then_inc(ba_step, 1)
                dve.wait_ge(ba_step, 1)
                nc.vector.tensor_tensor(ba[:, :, :], two[:, :, 1, :], ba[:, :, :], ALU.add).then_inc(ba_step, 1)
                dve.wait_ge(ba_step, 2)
                nc.vector.tensor_tensor(th(sp[:, 5, :]), ba[:, :, 8:16].rearrange("p t h -> p h t"),
                                        dtb[:, :].unsqueeze(2).broadcast_to([P, NHD, 2]), ALU.add).then_inc(ba_step, 1)
                dve.wait_ge(ba_step, 3)
                nc.vector.scalar_tensor_tensor(out=sp[:, 1, :], in0=sp[:, 5, :], scalar=-1.0, in1=sp[:, 5, :],
                                               op0=ALU.mult, op1=ALU.max).then_inc(ba_step, 1)

            def gates():
                dve.wait_ge(ba_act, 2)
                nc.vector.tensor_scalar(sp[:, 6, :], sp[:, 0, :], 1.0, None, ALU.add).then_inc(ba_step, 1)
                dve.wait_ge(ba_step, 5)
                nc.vector.reciprocal(pair[:, 2, :], sp[:, 6, :]).then_inc(ba_step, 1)
                nc.vector.scalar_tensor_tensor(out=sp[:, 7, :], in0=sp[:, 5, :], scalar=0.0, in1=sp[:, 4, :],
                                               op0=ALU.max, op1=ALU.add).then_inc(ba_step, 1)
                dve.wait_ge(ba_step, 7)
                nc.vector.scalar_tensor_tensor(out=th(pair[:, 3, :]), in0=th(sp[:, 7, :]), scalar=-1.0,
                                               in1=sp[:, 3, 0:8].unsqueeze(2).broadcast_to([P, NHD, 2]),
                                               op0=ALU.mult, op1=ALU.mult).then_inc(ba_step, 1)

            th = lambda v: v.rearrange("p (h t) -> p h t", t=2)
            def tap(js, i, w, step):
                dve.wait_ge(conv_step, val(step, i, 3 * BODY))
                y = wk(W_YBUF + (js % 3) * T, T)
                nc.vector.scalar_tensor_tensor(
                    out=y, in0=wk(W_CBUF + (js % 3) * 260 + w, T), scalar=cT[:, bass.ds(val(w * 24 + js, i, BODY), 1)],
                    in1=y, op0=ALU.mult, op1=ALU.add).then_inc(conv_step, 1)

            def conv(js, i):
                if js >= 1 or i is not None:
                    tap(js - 1, i, 3, 3 * js - 1)
                dve.wait_ge(conv_first, val(js + 1, i, BODY))
                y = wk(W_YBUF + (js % 3) * T, T)
                nc.vector.scalar_tensor_tensor(
                    out=y, in0=wk(W_CBUF + (js % 3) * 260 + 1, T), scalar=cT[:, bass.ds(val(24 + js, i, BODY), 1)],
                    in1=y, op0=ALU.mult, op1=ALU.add).then_inc(conv_step, 1)
                split(U_DN + js + AHEAD, i)
                tap(js, i, 2, 3 * js + 1)
            for js in range(BODY):
                if js == 3:
                    gate_inputs()
                conv(js, None)
                if js == 4:
                    gates()
            turns(dve, BODY, 24 - BODY, BODY, conv)
            tap(23, None, 3, 3 * 24 - 1)
            for j in range(24, 32):
                split(U_DN + j + AHEAD)
                if j == 28:
                    dve.wait_ge(qk_ps, 4)
                    nc.vector.tensor_copy(qkss[:, 2:4, :], acc[:, 1, 0:32].rearrange("p (a n) -> p a n", a=2)) \
                        .then_inc(ba_step, 1)
            dve.wait_ge(ba_pool, 2)
            dve.wait_ge(ba_act, 3)
            row = lambda r: pair[:, r, :]
            nc.vector.tensor_tensor(row(6), row(1), row(2), ALU.mult).then_inc(ba_step, 1)
            nc.vector.scalar_tensor_tensor(out=row(8), in0=row(2), scalar=-1.0, in1=row(4),
                                           op0=ALU.mult, op1=ALU.mult).then_inc(ba_step, 1)
            nc.vector.tensor_scalar(row(9), row(0), DH ** -0.5, None, ALU.mult).then_inc(ba_step, 1)
            nc.vector.scalar_tensor_tensor(out=row(10), in0=row(0), scalar=DH ** -0.5, in1=row(4),
                                           op0=ALU.mult, op1=ALU.mult).then_inc(ba_step, 1)
            dve.wait_ge(ba_step, BA_SUMS + 4)

            dve.wait_ge(masks_loaded, 16)
            level = lambda n, flip: lmask[:, 2 * n + flip, :].unsqueeze(1).broadcast_to([P, 4, P])
            for e, step, g in CORE_ORDER:
                if e != "dve":
                    continue
                bank = lambda b: core_bank(g, b)
                buf = lambda name: core_buf(g, name)
                if step == "kscale":
                    core_wait(dve, "pe", "kvT", g)
                    tt = nc.vector.tensor_tensor
                    tt(buf("kn"), bank(0), per_pair(1, g), ALU.mult)
                    tt(buf("kb"), bank(0), per_pair(6, g), ALU.mult)
                    ins = tt(buf("vb"), bank(1), per_pair(2, g), ALU.mult)
                elif step == "kd":
                    core_wait(dve, "dve", "kscale", g)
                    ins = nc.vector.tensor_tensor(buf("kd"), buf("kn"), per_pair(5, g), ALU.mult)
                elif step == "attn":
                    core_wait(dve, "pe", "scores", g)
                    core_wait(dve, "pool", "decmask", g)
                    ins = nc.vector.tensor_tensor(buf("attnT"), bank(2), buf("decI"), ALU.mult)
                elif step == "b":
                    ins = nc.vector.tensor_tensor(buf("B"), bank(3), buf("decS"), ALU.mult)
                elif step == "z0":
                    core_wait(dve, "act", "z_init", g)
                    core_wait(dve, "dve", "b", g)
                    ins = nc.vector.copy_predicated(buf("Z"), level(0, 1), buf("B"))
                elif step[0] == "x":
                    n = int(step[1:])
                    core_wait(dve, "pe", f"d{n}", g)
                    ins = nc.vector.copy_predicated(buf("X"), level(n, 0), bank(1))
                elif step == "z_last":
                    core_wait(dve, "pe", f"d{LEVELS - 1}", g)
                    ins = nc.vector.copy_predicated(buf("Z"), level(LEVELS - 1, 1), bank(1))
                elif step == "rhs1":
                    core_wait(dve, "pe", "kqs", g)
                    for hd in range(2):
                        p = 4 * g + 2 * hd + 1
                        ins = nc.vector.scalar_tensor_tensor(
                            out=buf("SR")[:, 2 + hd, :], in0=bank(3)[:, hd, :], scalar=pair[:, 8, p:p + 1],
                            in1=buf("vb")[:, 2 * hd + 1, :], op0=ALU.mult, op1=ALU.add)
                elif step == "t1":
                    for hd in range(2):
                        p = 4 * g + 2 * hd + 1
                        ins = nc.vector.tensor_scalar(buf("t1")[:, hd, :], bank(3)[:, 2 + hd, :],
                                                      pair[:, 10, p:p + 1], None, ALU.mult)
                elif step == "o":
                    core_wait(dve, "pe", "o1", g)
                    core_wait(dve, "dve", "t1", g)
                    for hd in range(2):
                        p = 4 * g + 2 * hd
                        nc.vector.tensor_scalar(buf("o")[:, 2 * hd, :], bank(2)[:, 2 * hd, :],
                                                pair[:, 9, p:p + 1], None, ALU.mult)
                        ins = nc.vector.scalar_tensor_tensor(
                            out=buf("o")[:, 2 * hd + 1, :], in0=bank(2)[:, 2 * hd + 1, :],
                            scalar=pair[:, 9, p + 1:p + 2], in1=buf("t1")[:, hd, :], op0=ALU.mult, op1=ALU.add)
                elif step == "on":
                    core_wait(dve, "pool", "orstd", g)
                    ins = nc.vector.tensor_tensor(
                        buf("o"), buf("o"), oss[:, 2, 4 * g:4 * g + 4].unsqueeze(2).broadcast_to([P, 4, P]), ALU.mult)
                elif step == "y":
                    core_wait(dve, "pe", "oT", g)
                    ins = nc.vector.scalar_tensor_tensor(
                        out=buf("y").rearrange("p a n -> p (a n)"), in0=bank(3).rearrange("p a n -> p (a n)"),
                        scalar=og[:, 0:1], in1=wk(W_Z + 2 * g * T, 2 * T), op0=ALU.mult, op1=ALU.mult)
                elif step == "yh":
                    core_wait(dve, "dve", "y", g)
                    ins = nc.vector.tensor_copy(yh[:, 2 * g:2 * g + 2, :].rearrange("p a n -> p (a n)"),
                                                buf("y").rearrange("p a n -> p (a n)"))
                else:
                    core_wait(dve, "dve", "yh", g)
                    ins = nc.vector.tensor_tensor(yl[:, 2 * g:2 * g + 2, :].rearrange("p a n -> p (a n)"),
                                                  buf("y").rearrange("p a n -> p (a n)"),
                                                  yh[:, 2 * g:2 * g + 2, :].bitcast(F32).rearrange("p a n -> p (a n)"),
                                                  ALU.subtract)
                ins.then_inc(core["dve"], 1)

            splits(U_DNO, KC)
            residual(4)
            pre(5, [(G_M0, xh, xl)])
            relu2(0)
            residual(5)
            pre(6, [(G_X1, xh, xl)])
            for n in range(2 * NHD + KC):
                split(U_MB + n + AHEAD)
            heads(NH // 2, NHD // 2, False)
            out_T(1, xh, xl)
            splits(U_MBO, KC)
            residual(6)
            pre(7, [(G_M1, xh, xl)])
            relu2(1)
            residual(7)
            dve.wait_ge(gpost_loaded[0], 16 * 3)
            for t in range(NT):
                q = 16 + t
                dve.wait_ge(pre_rstd, q + 1)
                nc.vector.scalar_tensor_tensor(out=xn[:, t, :], in0=h[:, t, :], scalar=rstd[:, 2 * q:2 * q + 1],
                                               in1=gpost[:, 0, :], op0=ALU.mult, op1=ALU.mult).then_inc(out_ready, 1)

        @block.tensor
        def _(pe):
            mm = nc.tensor.matmul

            def take(us, i=None):
                pe.wait_ge(lo_ready, val(us + 1, i, BODY))

            def feature_chunk(us, i, ps, hi, lo):
                take(us, i)
                wh = w_hi[:, us % RING, :].rearrange("p (k n) -> p k n", k=KC)
                wl = w_lo[:, us % RING, :].rearrange("p (k n) -> p k n", k=KC)
                for k in range(KC):
                    mm(ps, wh[:, k, :], hi[:, k, :], start=(k == 0), stop=False)
                    mm(ps, wh[:, k, :], lo[:, k, :], start=False, stop=False)
                    ins = mm(ps, wl[:, k, :], hi[:, k, :], start=False, stop=(k == KC - 1))
                ins.then_inc(unit_used, 1)
                return ins

            def row_tile(us, t, hi, lo, first, last):
                wh, wl = w_hi[:, us % RING, :], w_lo[:, us % RING, :]
                th, tl = hi[:, t * P:(t + 1) * P], lo[:, t * P:(t + 1) * P]
                for half in range(2):
                    cols = slice(512 * half, 512 * half + 512)
                    ps = acc[:, 2 * t + half, :]
                    mm(ps, th, wh[:, cols], start=first, stop=False)
                    mm(ps, th, wl[:, cols], start=False, stop=False)
                    ins = mm(ps, tl, wh[:, cols], start=False, stop=last)
                return ins

            def row_unit(us, i, hi, lo, first, last):
                take(us, i)
                for t in range(NT):
                    ins = row_tile(us, t, hi, lo, first, last)
                ins.then_inc(unit_used, 1)

            def finish(us, operands, waits):
                for t in range(NT):
                    for n, (hi, lo) in enumerate(operands):
                        if t == 0:
                            take(us + n)
                            if waits:
                                pe.wait_ge(hid_ready, waits[n])
                        ins = row_tile(us + n, t, hi, lo, False, n == len(operands) - 1)
                        if t == 1:
                            ins.then_inc(unit_used, 1)
                    if t == 0:
                        ins.then_inc(acc_first, 1)

            def project(u0, hi, lo):
                for k in range(KC):
                    row_unit(u0 + k, None, hi[:, k, :], lo[:, k, :], k == 0, k == KC - 1)

            def project_out(u0, hi, lo, sem_, value):
                for k in range(KC - 3):
                    pe.wait_ge(sem_, value(k))
                    row_unit(u0 + k, None, hi[:, k, :], lo[:, k, :], k == 0, False)
                pe.wait_ge(sem_, value(KC - 1))
                finish(u0 + KC - 3, [(hi[:, k, :], lo[:, k, :]) for k in range(KC - 3, KC)], None)

            def transpose_rows(n, ready, value, sem_done):
                for t in range(NT):
                    pe.wait_ge(ready, value(t))
                    for half in range(2):
                        for k in range(4):
                            c = (4 * half + k) * P
                            ins = nc.tensor.transpose(hp[:, 2 * t + half, k * P:(k + 1) * P], xn[:, t, c:c + P], ident)
                        ins.then_inc(sem_done, 1)

            def stay_busy(n):
                for _ in range(n):
                    mm(hp[:, 3, :], ident, const[:, 0:512], start=True, stop=True)

            def pre(n, sets=1):
                if n:
                    stay_busy(3)
                for t in range(NT):
                    pe.wait_ge(diag_ready, 2 * n + t + 1)
                    for half in range(2):
                        for k in range(4):
                            c = (4 * half + k) * P
                            ins = mm(hp[:, 2 * t + half, k * P:(k + 1) * P], h[:, t, c:c + P], diag[:, t, :],
                                     start=True, stop=True)
                        ins.then_inc(xT_ps, 1)
                pre.ready += 4 * sets
            pre.ready = 0

            def first_pair(us, banks):
                for half in range(2):
                    pe.wait_ge(xT_ready, pre.ready - 1 + half)
                    for n, ps in enumerate(banks):
                        if half == 0:
                            take(us + n)
                        wh = w_hi[:, (us + n) % RING, :].rearrange("p (k n) -> p k n", k=KC)
                        wl = w_lo[:, (us + n) % RING, :].rearrange("p (k n) -> p k n", k=KC)
                        for k in range(4 * half, 4 * half + 4):
                            mm(ps, wh[:, k, :], xh[:, k, :], start=(k == 0), stop=False)
                            mm(ps, wh[:, k, :], xl[:, k, :], start=False, stop=False)
                            ins = mm(ps, wl[:, k, :], xh[:, k, :], start=False, stop=(k == KC - 1))
                        if half == 1:
                            ins.then_inc(unit_used, 1)

            pe.wait_ge(early_loaded, 16 * 12)
            nc.tensor.transpose(acc[:, 0, 0:96], rows[:, 0, :], const[0:96, C_ID:C_ID + 96])
            nc.tensor.transpose(acc[:, 1, 0:96], rows[:, 1, :], const[0:96, C_ID:C_ID + 96]).then_inc(rows_T, 1)
            pe.wait_ge(gains_ready, 1)
            pre(0)

            def mixer(js, i):
                us = U_MIX + 3 * js
                if js >= 2 or i is not None:
                    pe.wait_ge(y_ready, val(js - 1, i, 2))
                if js == 0 and i is None:
                    first_pair(us, [mix_psum(0, 0), mix_psum(0, 1)])
                for kind in range(2 if js == 0 and i is None else 0, 3):
                    feature_chunk(us + kind, i, mix_psum(js, kind), xh, xl)
            for js in range(2):
                mixer(js, None)
            turns(pe, 2, KC - 2, 2, mixer)
            project_out(U_MIXO, yh, yl, y_ready, lambda k: max(k + 1, KC - 1))
            pre(1)

            def down(us, i, js, cb, ring, first=False):
                pe.wait_ge(hid_ready, val(cb + js + 1, i, ring))
                row_unit(us, i, hh[:, js % ring, :], hl[:, js % ring, :], first, False)

            def last_downs(us, js, cb, ring):
                finish(us, [(hh[:, (js + n) % ring, :], hl[:, (js + n) % ring, :]) for n in range(2)],
                       [cb + js + 1, cb + js + 2])

            def swiglu(layer):
                u0, cb = U_FF[layer], NF * layer

                def gate_up(us, i, js):
                    for n in range(2):
                        feature_chunk(us + n, i, hp[:, 2 * (js % 2) + n, 0:T], xh, xl)

                def step(js, i):
                    us = u0 + 2 + 3 * js
                    gate_up(us, i, js + 1)
                    down(us + 2, i, js, cb, 2, first=(js == 0))
                first_pair(u0, [hp[:, n, 0:T] for n in range(2)])
                step(0, None)
                turns(pe, 1, NF - 3, 2, step)
                gate_up(u0 + 3 * NF - 4, None, NF - 1)
                last_downs(u0 + 3 * NF - 2, NF - 2, cb, 2)

            def relu2(layer):
                u0, cb = U_MLP[layer], 2 * NF + NM * layer

                def up(us, i, js):
                    feature_chunk(us, i, hp[:, js % 3, 0:T], xh, xl)

                def step(js, i):
                    us = u0 + 2 + 2 * js
                    up(us, i, js + 2)
                    down(us + 1, i, js, cb, 3, first=(js == 0))
                first_pair(u0, [hp[:, n, 0:T] for n in range(2)])
                step(0, None)
                turns(pe, 1, NM - 3, 3, step)
                last_downs(u0 + 2 * NM - 2, NM - 2, cb, 3)

            def heads(first, n, sink):
                dh = HD if sink else DH

                def qk(hd):
                    if sink:
                        rows_ = slice(HD * (hd % 2), HD * (hd % 2) + HD)
                        q_at, k_at = W_QT + (hd // 2) * T, W_KT + (hd // 4) * T
                        return work[rows_, q_at:q_at + T], work[rows_, k_at:k_at + T]
                    return wk(W_MQK + hd * T, T), wk(W_MQK + (NHD + hd) * T, T)

                def scores(k):
                    i = first + k
                    if i >= 2:
                        pe.wait_ge(s_made, i - 1)
                    for hd in range(2):
                        q, key = qk(2 * k + hd)
                        ps = acc[:, 2 * (i % 2) + hd, :]
                        mm(ps[:, 0:P], q[:, 0:P], key[:, 0:P], start=True, stop=True)
                        ins = mm(ps[:, P:384], q[:, P:T], key, start=True, stop=True)
                    ins.then_inc(sc_done, 1)

                def turn(k):
                    i = first + k
                    pe.wait_ge(p_ready, i + 1)
                    if i >= 1:
                        pe.wait_ge(pt_ready, i)
                    for hd in range(2):
                        for b in range(3):
                            ins = nc.tensor.transpose(hp[:, hd, b * P:(b + 1) * P],
                                                      score_buf(i)[:, hd, b * P:(b + 1) * P], ident)
                    ins.then_inc(pt_ps, 1)

                def values(k):
                    i = first + k
                    pe.wait_ge(pt_ready, i + 1)
                    if i >= 2:
                        pe.wait_ge(o_made, i - 1)
                    for hd in range(2):
                        n_hd = 2 * k + hd
                        pt = pt_buf(i)[:, hd, :]
                        v = [wk((W_V + t * 256 + (n_hd // 4) * HD) if sink else (W_MV + t * D + n_hd * DH), dh)
                             for t in range(NT)]
                        o = [hp[:, 2 + i % 2, (2 * t + hd) * dh:(2 * t + hd + 1) * dh] for t in range(NT)]
                        mm(o[0], pt[:, 0:P], v[0], start=True, stop=True)
                        mm(o[1], pt[:, P:2 * P], v[0], start=True, stop=False)
                        ins = mm(o[1], pt[:, 2 * P:3 * P], v[1], start=False, stop=True)
                    ins.then_inc(pv_done, 1)
                for k in range(n + 3):
                    if k < n:
                        scores(k)
                    if k == 2:
                        stay_busy(2)
                    if 2 <= k < n + 2:
                        turn(k - 2)
                    if k >= 3:
                        values(k - 3)

            swiglu(0)
            pre(2, 2)
            for n in range(4):
                us = U_KV + n
                take(us)
                pe.wait_ge(xT_ready, pre.ready - 5 + n // 2)
                for kk in range(2):
                    k, cols = 2 * n + kk, slice(512 * kk, 512 * kk + 512)
                    for t in range(NT):
                        rows_ = slice(t * P, (t + 1) * P)
                        mm(acc[:, 2 + t, :], xh[:, k, rows_], w_hi[:, us % RING, cols], start=(k == 0), stop=False)
                        mm(acc[:, 2 + t, :], xh[:, k, rows_], w_lo[:, us % RING, cols], start=False, stop=False)
                        ins = mm(acc[:, 2 + t, :], xl[:, k, rows_], w_hi[:, us % RING, cols], start=False, stop=(k == KC - 1))
                ins.then_inc(unit_used, 1)
            for k in range(KC):
                pe.wait_ge(xT_ready, pre.ready - 1 + k // 4)
                if k == 0:
                    pe.wait_ge(kv_copied, NT)
                row_unit(U_Q + k, None, yh[:, k, :], yl[:, k, :], k == 0, k == KC - 1)
            for t in range(NT):
                pe.wait_ge(k_dup, t + 2)
                for g in range(NKV):
                    at = W_KDUP + t * 512 + g * P
                    ins = nc.tensor.transpose(hp[:, 2 + t, g * P:(g + 1) * P], wk(at, P), ident)
                ins.then_inc(kT_ps, 1)
            for t in range(NT):
                pe.wait_ge(rot_done, 2 * (2 + t + 1))
                if t == 1:
                    pe.wait_ge(kT_copied, NT)
                for half in range(2):
                    for k in range(4):
                        at = W_QTOK + t * D + (4 * half + k) * P
                        ins = nc.tensor.transpose(hp[:, 2 * t + half, k * P:(k + 1) * P], wk(at, P), ident)
                    ins.then_inc(qT_ps, 1)
            pe.wait_ge(qT_copied, 4)
            heads(0, NH // 2, True)
            transpose_rows(0, o_made, lambda t: NH // 2, oT_ps)
            project_out(U_O, xh, xl, oT_ready, lambda k: 3 + k // 4)
            pre(3)
            swiglu(1)
            pre(4)

            def gate_inputs(t):
                pe.wait_ge(wba_step, 2)
                pe.wait_ge(xT_ready, pre.ready)
                ps = acc[:, 0, 32 * t:32 * t + 32]
                rows_ = slice(t * P, (t + 1) * P)
                for k in range(KC):
                    mm(ps, xh[:, k, rows_], wba_split[:, k, :, :].rearrange("p s n -> p (s n)"),
                       start=(k == 0), stop=False)
                    ins = mm(ps[:, 0:16], xl[:, k, rows_], wba_split[:, k, 0, :], start=False, stop=(k == KC - 1))
                ins.then_inc(ba_ps, 1)

            def decays():
                pe.wait_ge(ba_step, BA_G)
                mm(acc[:, 2, 0:16], const[:, C_INCL:C_INCL + P], pair[:, 3, :], start=True, stop=True)
                mm(acc[:, 2, 16:32], const[:, C_STRICT:C_STRICT + P], pair[:, 3, :], start=True, stop=True) \
                    .then_inc(gc_ps, 1)

            def row_sums(part):
                pe.wait_ge(qk_sq, part + 1)
                for c in range(8 * part, 8 * part + 8):
                    ins = mm(acc[:, 1, c:c + 1], wk(W_SQ + c * P, P), const[:, C_ONE:C_ONE + 1], start=True, stop=True)
                ins.then_inc(qk_ps, 1)

            def dn_chunk(js, i):
                if js >= 3 or i is not None:
                    pe.wait_ge(conv_in, val(js - 2, i, BODY))
                feature_chunk(U_DN + js, i, small_psum(js % 3), xh, xl)
            first_pair(U_DN, [small_psum(0), small_psum(1)])
            gate_inputs(0)
            for js in range(2, BODY):
                dn_chunk(js, None)
                if js == 2:
                    gate_inputs(1)
            turns(pe, BODY, 24 - BODY, BODY, dn_chunk)
            decays()
            for j in range(24, 32):
                if j < 27:
                    pe.wait_ge(conv_in, j - 2)
                else:
                    pe.wait_ge(z_ready, j - 26)
                feature_chunk(U_DN + j, None, small_psum(j % 3), xh, xl)
                if j < 28:
                    row_sums(j - 24)
            pe.wait_ge(conv_silu, 24)
            pe.wait_ge(z_ready, 8)
            pe.wait_ge(ba_step, BA_SUMS)

            for e, step, g in CORE_ORDER:
                if e != "pe":
                    continue
                bank = lambda b: core_bank(g, b)
                buf = lambda name: core_buf(g, name)

                def qT(p):
                    return qkvT(2 * g + p // 2)[:, (p % 2) * P:(p % 2 + 1) * P]

                def chunk_of(kind, p):
                    return qkvT(kind * NHD + 2 * g + p // 2)[:, (p % 2) * P:(p % 2 + 1) * P]
                pairs = range(4)
                if step == "kvT":
                    for p in pairs:
                        nc.tensor.transpose(bank(0)[:, p, :], chunk_of(1, p), ident)
                    for p in pairs:
                        ins = nc.tensor.transpose(bank(1)[:, p, :], chunk_of(2, p), ident)
                elif step == "decay":
                    core_wait(pe, "pool", "gs", g)
                    if g >= 2:
                        core_wait(pe, "dve", "o", g - 2)
                    if g == 0:
                        pe.wait_ge(ba_act, 3)
                    for p in pairs:
                        ins = mm(bank(2)[:, p, :], buf("gs")[:, p, :], const[:, C_INCL:C_INCL + P], start=True, stop=True)
                elif step == "knT":
                    core_wait(pe, "dve", "kscale", g)
                    for p in pairs:
                        nc.tensor.transpose(bank(0)[:, p, :], buf("kn")[:, p, :], ident)
                    for p in pairs:
                        ins = nc.tensor.transpose(bank(1)[:, p, :], buf("kb")[:, p, :], ident)
                elif step == "scores":
                    core_wait(pe, "act", "knT_copy", g)
                    if g >= 2:
                        core_wait(pe, "dve", "y", g - 2)
                    for p in pairs:
                        mm(bank(2)[:, p, :], buf("knT")[:, p, :], qT(p), start=True, stop=True)
                        ins = mm(bank(3)[:, p, :], buf("knT")[:, p, :], buf("kbT")[:, p, :], start=True, stop=True)
                elif step == "xT":
                    core_wait(pe, "dve", "z0", g)
                    for p in pairs:
                        ins = nc.tensor.transpose(bank(0)[:, p, :], buf("Z")[:, p, :], ident)
                elif step[0] == "y":
                    n = int(step[1:])
                    if n == 1:
                        core_wait(pe, "act", "x_copy", g)
                    else:
                        core_wait(pe, "dve", f"x{n - 1}", g)
                    for p in pairs:
                        ins = mm(bank(0)[:, p, :], buf("B")[:, p, :], buf("X")[:, p, :], start=True, stop=True)
                elif step.startswith("zT"):
                    core_wait(pe, "dve", f"x{int(step[2:])}", g)
                    for p in pairs:
                        ins = nc.tensor.transpose(bank(2)[:, p, :], buf("X")[:, p, :], ident)
                elif step[0] == "d" and step != "decay":
                    n = int(step[1:])
                    core_wait(pe, "act", f"y{n}_copy", g)
                    if n > 1:
                        core_wait(pe, "act", f"zT{n - 1}_copy", g)
                    for p in pairs:
                        if n < LEVELS - 1:
                            ins = mm(bank(1)[:, p, :], buf("Z")[:, p, :], buf("Y")[:, p, :], start=True, stop=True)
                        else:
                            ins = mm(bank(1)[:, p, :], buf("Y")[:, p, :], buf("Z")[:, p, :], start=True, stop=True)
                elif step == "vn0":
                    core_wait(pe, "dve", "z_last", g)
                    for hd in range(2):
                        ins = mm(bank(0)[:, hd, :], buf("Z")[:, 2 * hd, :], buf("vb")[:, 2 * hd, :], start=True, stop=True)
                elif step == "state":
                    core_wait(pe, "act", "vn0_copy", g)
                    for hd in range(2):
                        ins = mm(bank(1)[:, hd, :], buf("kd")[:, 2 * hd, :], buf("vn")[:, 2 * hd, :], start=True, stop=True)
                elif step == "o0":
                    for hd in range(2):
                        ins = mm(bank(2)[:, 2 * hd, :], buf("attnT")[:, 2 * hd, :], buf("vn")[:, 2 * hd, :],
                                 start=True, stop=True)
                elif step == "kqs":
                    core_wait(pe, "act", "state_copy", g)
                    for hd in range(2):
                        mm(bank(3)[:, hd, :], buf("knT")[:, 2 * hd + 1, :], buf("SR")[:, hd, :], start=True, stop=True)
                        ins = mm(bank(3)[:, 2 + hd, :], qT(2 * hd + 1), buf("SR")[:, hd, :], start=True, stop=True)
                elif step == "vn1":
                    core_wait(pe, "dve", "rhs1", g)
                    for hd in range(2):
                        ins = mm(bank(0)[:, 2 + hd, :], buf("Z")[:, 2 * hd + 1, :], buf("SR")[:, 2 + hd, :],
                                 start=True, stop=True)
                elif step == "o1":
                    core_wait(pe, "act", "vn1_copy", g)
                    for hd in range(2):
                        ins = mm(bank(2)[:, 2 * hd + 1, :], buf("attnT")[:, 2 * hd + 1, :], buf("vn")[:, 2 * hd + 1, :],
                                 start=True, stop=True)
                else:
                    core_wait(pe, "dve", "on", g)
                    for p in pairs:
                        ins = nc.tensor.transpose(bank(3)[:, p, :], buf("o")[:, p, :], ident)
                ins.then_inc(core["pe"], 1)

            project_out(U_DNO, yh, yl, core["dve"], lambda k: core_value("dve", "yl", max(k // 2, 2)))
            pre(5)
            relu2(0)
            pre(6)

            def mb_chunk(js, i):
                if js >= 3 or i is not None:
                    pe.wait_ge(mb_copied, val(js - 2, i, BODY))
                feature_chunk(U_MB + js, i, small_psum(js % 3), xh, xl)
            first_pair(U_MB, [small_psum(0), small_psum(1)])
            mb_chunk(2, None)
            turns(pe, 3, 2 * NHD - 3, BODY, mb_chunk)
            project(U_MBV, xh, xl)
            pe.wait_ge(mb_copied, 2 * NHD)
            pe.wait_ge(mbv_copied, NT)
            heads(NH // 2, NHD // 2, False)
            transpose_rows(0, o_made, lambda t: (NH + NHD) // 2, oT_ps)
            project_out(U_MBO, xh, xl, oT_ready, lambda k: 7 + k // 4)
            pre(7)
            relu2(1)


_INS = ["x", "a_pre_norm", "a_w_in", "a_conv_w", "a_w_out", "a_post_norm", "ffn_pre_norm", "ffn_w_gate_up",
        "ffn_w_down", "ffn_post_norm", "kv_norm", "w_kv", "b_pre_norm", "b_w_q", "b_sinks", "b_w_o", "b_post_norm",
        "mix_norm_g_2", "mlp_norm_g_2", "dn_w_in_2", "dn_conv_w_2", "dn_a_log_2", "dn_dt_bias_2",
        "dn_out_norm_g_2", "dn_w_out_2", "mb_w_in_2", "mb_w_out_2", "mlp_w_up_2", "mlp_w_down_2", "final_norm_g_2"]


def constants():
    import numpy as np
    j, i = np.arange(P)[:, None], np.arange(P)[None, :]
    q, k = j, np.arange(T)[None, :]
    c = np.zeros((P, N_CONST), np.float32)
    c[:, C_ID:C_ID + P] = j == i
    c[:, C_INCL:C_INCL + P] = j <= i
    c[:, C_STRICT:C_STRICT + P] = j > i
    c[:, C_NEG:C_NEG + P] = -1.0 * (i > j)
    c[:, C_ONE] = 1.0
    c[:, C_BAND:C_BAND + P] = np.where(i <= j, 0.0, -1e30)
    c[:, C_BAND + P:C_BAND + 3 * P] = np.where((k <= q + P) & (k > q + P - 128), 0.0, -1e30)
    c[:, C_DIST:C_DIST + P] = np.where(i <= j, i - j, -1e30)
    c[:, C_DIST + P:C_DIST + 3 * P] = np.where(k <= q + P, k - q - P, -1e30)
    inv_freq = np.float32(500000.0) ** (-np.arange(0, 2 * ROT, 2, dtype=np.float32) / np.float32(2 * ROT))
    angle = (np.arange(T, dtype=np.float32)[:, None] * inv_freq[None, :]).reshape(NT, P, ROT).transpose(1, 0, 2)
    c[:, C_COS:C_COS + NT * ROT] = np.cos(angle).reshape(P, -1)
    c[:, C_SIN:C_SIN + NT * ROT] = np.sin(angle).reshape(P, -1)
    masks = np.zeros((P, 2 * LEVELS, P), np.float32)
    for n in range(LEVELS):
        b = 2 ** n
        low = (j // (2 * b) == i // (2 * b)) & (j % (2 * b) >= b) & (i % (2 * b) < b)
        masks[:, 2 * n, :] = low
        masks[:, 2 * n + 1, :] = low.T
    return c, masks


def kernel(**inputs):
    import numpy as _np
    import concourse.bacc as _bacc
    from concourse import mybir as _mybir
    from concourse.bass_utils import run_bass_kernel_spmd as _run

    nc = _bacc.Bacc("TRN2", target_bir_lowering=False, num_devices=1)
    arrays, args = {}, {}
    consts, masks = constants()
    given = {name: _np.ascontiguousarray(inputs[name]) for name in _INS}
    given["consts"], given["masks"] = consts, masks
    for name, v in given.items():
        arrays[f"in_{name}_dram"] = v
        args[name] = nc.dram_tensor(f"in_{name}_dram", v.shape, _mybir.dt.from_np(v.dtype), kind="ExternalInput").ap()
    out = nc.dram_tensor("out_0_dram", (1, T, D), F32, kind="ExternalOutput").ap()
    build(nc, args, out)
    r = _run(nc, [arrays], core_ids=[0])
    return r.results[0]["out_0_dram"]
```

```python
from contextlib import ExitStack

import concourse.bass as bass
from concourse import mybir

ALU = mybir.AluOpType
ACT = mybir.ActivationFunctionType
F32 = mybir.dt.float32
F32R = mybir.dt.float32r
U8 = mybir.dt.uint8
X = mybir.AxisListType.X

P = 128
T = 256
NT = T // P
D = 1024
KC = D // P
FF = 2816
NF = FF // P
FF2 = 4096
NM = FF2 // P
EPS = 1e-6
HD = 64
NH = 16
NKV = 4
ROT = 8
DH = 128
NHD = 8
SW_SCALE = HD ** -0.5
MB_SCALE = DH ** -0.5

RING = 6
RAW = 3
AHEAD = 4
BODY = RING

U_MIX = 0
U_MIXO = U_MIX + 3 * KC
U_FF = [U_MIXO + KC, 0]
U_KV = U_FF[0] + 3 * NF
U_Q = U_KV + 4
U_O = U_Q + KC
U_FF[1] = U_O + KC
U_DN = U_FF[1] + 3 * NF
U_DNO = U_DN + 4 * NHD
U_MLP = [U_DNO + KC, 0]
U_MBV = U_MLP[0] + 2 * NM
U_MB = U_MBV + KC
U_MBO = U_MB + 2 * NHD
U_MLP[1] = U_MBO + KC
N_UNITS = U_MLP[1] + 2 * NM
LAST_UNIT = [u - 1 for u in (U_FF[0], U_KV, U_FF[1], U_DN, U_MLP[0], U_MBV, U_MLP[1], N_UNITS)]

G_A, G_F0, G_F1, G_KV, G_B, G_X0, G_X1, G_M0, G_M1 = [KC * n for n in range(9)]
G_CONV = 9 * KC
C_ID, C_INCL, C_STRICT, C_NEG, C_ONE = [P * n for n in range(5)]
C_BAND = C_ONE + 4
C_DIST = C_BAND + 3 * P
C_COS = C_DIST + 3 * P
C_SIN = C_COS + NT * ROT
N_CONST = C_SIN + NT * ROT
LEVELS = 7
DN_STRAIGHT = 3 * BODY

W_SG, W_HX = 0, 3 * T
W_CSB, W_CU, W_Y = 6 * T, 8 * T, 10 * T
W_QTOK, W_QT, W_KDUP, W_KT, W_V, W_RT = 0, 2048, 4096, 5120, 6144, 6656
W_S, W_PT = 7168, 7168 + 3 * 768
W_MQK, W_MV = 0, 4096
W_QKV, W_Z, W_GRP = 0, 24 * T, 32 * T
W_SQ, W_CBUF, W_YBUF = W_GRP, W_GRP + 16 * T, W_GRP + 16 * T + 3 * 260
N_WORK = W_GRP + 2 * 9 * 512
W_JUNK = N_WORK - 4 * D

CORE_HEAD = [[("pool", "gs")], [("pe", "kvT")], [("pe", "decay")], [("dve", "kscale")], [("pe", "knT")]]
CORE_BODY = [[("dve", "kd")], [("act", "dec")], [("pool", "decmask")], [("act", "knT_copy")], [("act", "z_init")],
             [("pe", "scores")], [("dve", "b")], [("dve", "z0")], [("dve", "attn")], [("pe", "xT")], [("act", "x_copy")],
             [("pe", "y1")], [("act", "y1_copy")], [("pe", "d1")], [("dve", "x1")]]
for _l in range(2, LEVELS):
    CORE_BODY += [[("pe", f"y{_l}"), ("pe", f"zT{_l - 1}")], [("act", f"y{_l}_copy")], [("dve", f"zT{_l - 1}_copy")],
                  [("pe", f"d{_l}")], [("dve", f"x{_l}" if _l < LEVELS - 1 else "z_last")]]
CORE_BODY += [[("pe", "vn0")], [("act", "vn0_copy")], [("pe", "state")], [("act", "state_copy")], [("pe", "o0")],
              [("pe", "kqs")], [("dve", "rhs1")], [("dve", "t1")], [("pe", "vn1")], [("act", "vn1_copy")], [("pe", "o1")]]
CORE_OUT = [[("dve", "o")], [("act", "osq")], [("pool", "omean")], [("pool", "orstd")]]
CORE_NORM = [[("dve", "on")], [("pe", "oT")]]
CORE_TAIL = [[("dve", "y")], [("dve", "yh")], [("dve", "yl")]]
CORE_ORDER = [(e, s, g) for steps, groups in (
    (CORE_HEAD, (0, 1)), (CORE_BODY, (0, 1)), (CORE_HEAD[:1], (2, 3)), (CORE_OUT, (0, 1)),
    (CORE_HEAD[1:], (2, 3)), (CORE_NORM + CORE_TAIL, (0, 1)), (CORE_BODY, (2, 3)), (CORE_OUT, (2, 3)),
    (CORE_NORM, (2, 3)), (CORE_TAIL, (2,)), (CORE_TAIL, (3,)))
    for together in steps for g in groups for e, s in together]
BA_IN, BA_G, BA_SUMS = 4, 8, 9


def core_value(engine, step, g):
    mine = [(s, k) for e, s, k in CORE_ORDER if e == engine]
    return mine.index((step, g)) + 1


def val(static, i, per):
    return static if i is None else i * per + static


def turns(eng, first, n, body, step):
    whole = n // body
    if whole > 1:
        with eng.Fori(0, whole) as i:
            for js in range(first, first + body):
                step(js, i)
        first, n = first + whole * body, n - whole * body
    for js in range(first, first + n):
        step(js, None)


def build(nc, a, out):
    ctx = ExitStack()
    with ctx:
        def sb(name, shape, dt=F32):
            return ctx.enter_context(nc.sbuf_tensor(name, shape, dt))

        def sem(name):
            return ctx.enter_context(nc.semaphore(name))

        w_raw = sb("w_raw", [P, RAW, 1024])
        w_hi = sb("w_hi", [P, RING, 1024], F32R)
        w_lo = sb("w_lo", [P, RING, 1024], F32R)
        h = sb("h", [P, NT, D])
        xh, xl = sb("xh", [P, KC, T], F32R), sb("xl", [P, KC, T], F32R)
        yh, yl = sb("yh", [P, KC, T], F32R), sb("yl", [P, KC, T], F32R)
        xn = sb("xn", [P, NT, D])
        xf = sb("xf", [P, 2, 512])
        gpost = sb("gpost", [P, 2, D])
        diag = sb("diag", [P, NT, P])
        hh, hl = sb("hh", [P, 3, T], F32R), sb("hl", [P, 3, T], F32R)
        work = sb("work", [P, N_WORK])
        const = sb("const", [P, N_CONST])
        lmask = sb("lmask", [P, 2 * LEVELS, P], U8)
        rows = work[0:96, W_CBUF:W_CBUF + 2 * P].rearrange("p (a n) -> p a n", a=2)
        wba = work[:, W_CBUF + 2 * P:W_CBUF + 3 * P].rearrange("p (k n) -> p k n", k=KC)
        gT = sb("gT", [P, 96])
        cT = sb("cT", [P, 96])
        og = sb("og", [P, 1])
        wba_split = sb("wba_split", [P, KC, 2, 16], F32R)
        sinks = sb("sinks", [P, NH])
        dtb, alog = sb("dtb", [P, NHD]), sb("alog", [P, NHD])
        sums = sb("sums", [P, 52])
        means = sb("means", [P, 52])
        rstd = sb("rstd", [P, 52])
        half_neg = sb("half_neg", [P, 32])
        mx = sb("mx", [P, 24, 2])
        nm = sb("nm", [P, 24, 2])
        dsk = sb("dsk", [P, NH, 2])
        es = sb("es", [P, NH, 2])
        den = sb("den", [P, 24, 2])
        dtot = sb("dtot", [P, 24, 2])
        rinv = sb("rinv", [P, 24, 2])
        ba = sb("ba", [P, NT, 16])
        sp = sb("sp", [P, 8, 16])
        qkss = sb("qkss", [P, 4, 16])
        pair = sb("pair", [P, 12, 16])
        oss = sb("oss", [P, 3, 16])

        acc = ctx.enter_context(nc.psum_tensor("acc", [P, 4, 512], F32))
        hp = ctx.enter_context(nc.psum_tensor("hp", [P, 4, 512], F32))

        ident = const[:, C_ID:C_ID + P]

        landed = [sem(f"landed{s}") for s in range(RAW)]
        hi_ready, lo_ready, unit_used = sem("hi_ready"), sem("lo_ready"), sem("unit_used")
        x_loaded, early_loaded, late_loaded, masks_loaded = (
            sem("x_loaded"), sem("early_loaded"), sem("late_loaded"), sem("masks_loaded"))
        gpost_loaded = [sem(f"gpost_loaded{s}") for s in range(2)]
        rows_T, gains_ready, pool_const = sem("rows_T"), sem("gains_ready"), sem("pool_const")
        pre_sq, pre_mean, pre_rstd = sem("pre_sq"), sem("pre_mean"), sem("pre_rstd")
        diag_ready, xT_ps, xf_ready, xhi_ready, xT_ready = (
            sem("diag_ready"), sem("xT_ps"), sem("xf_ready"), sem("xhi_ready"), sem("xT_ready"))
        acc_part, post_sq, post_mean, post_rstd = (
            sem("acc_part"), sem("post_sq"), sem("post_mean"), sem("post_rstd"))
        post_tmp, h_new, out_ready, stored = (
            sem("post_tmp"), sem("h_new"), sem("out_ready"), sem("stored"))
        c_copied, pad_zero, cu_step, y_ready = (
            sem("c_copied"), sem("pad_zero"), sem("cu_step"), sem("y_ready"))
        act_done, hid_mul, hid_hi, hid_ready = (
            sem("act_done"), sem("hid_mul"), sem("hid_hi"), sem("hid_ready"))
        kv_copied, q_copied = sem("kv_copied"), sem("q_copied")
        rot_mul, rot_done, k_dup = sem("rot_mul"), sem("rot_done"), sem("k_dup")
        kT_ps, kT_copied, qT_ps, qT_copied = sem("kT_ps"), sem("kT_copied"), sem("qT_ps"), sem("qT_copied")
        sc_done, s_made, mx_done, nm_ready = sem("sc_done"), sem("s_made"), sem("mx_done"), sem("nm_ready")
        dsk_ready, p_ready, pt_ps, pt_ready = sem("dsk_ready"), sem("p_ready"), sem("pt_ps"), sem("pt_ready")
        pv_done, den_ready, rinv_ready, o_made = (
            sem("pv_done"), sem("den_ready"), sem("rinv_ready"), sem("o_made"))
        oT_ps, oT_hi, oT_ready = sem("oT_ps"), sem("oT_hi"), sem("oT_ready")
        mb_copied, mbv_copied, qv_part = sem("mb_copied"), sem("mbv_copied"), sem("qv_part")
        wba_step, ba_ps, ba_step, ba_act, ba_pool = (
            sem("wba_step"), sem("ba_ps"), sem("ba_step"), sem("ba_act"), sem("ba_pool"))
        conv_in, conv_first, conv_step, conv_silu = (
            sem("conv_in"), sem("conv_first"), sem("conv_step"), sem("conv_silu"))
        z_ready, qk_sq, qk_ps = sem("z_ready"), sem("qk_sq"), sem("qk_ps")
        gc_ps = sem("gc_ps")
        core = {"pe": sem("core_tensor"), "act": sem("core_scalar"),
                "dve": sem("core_vector"), "pool": sem("core_pool")}

        def wk(at, n):
            return work[:, at:at + n]

        def small_psum(slot):
            return hp[:, slot, 0:T]

        def mix_psum(js, kind):
            return (acc if js % 2 == 0 else hp)[:, kind, 0:T]

        def core_bank(g, b):
            return (acc if g % 2 == 0 else hp)[:, b, :].rearrange("p (a n) -> p a n", a=4)

        def core_buf(g, name):
            where = {"kn": 0, "X": 0, "kb": 1, "Z": 1, "vb": 2, "kd": 3, "knT": 4,
                     "kbT": 5, "Y": 5, "decS": 6, "SR": 6, "decI": 7, "attnT": 7, "B": 8, "t1": 8}
            if name in ("gs", "vn"):
                return xn[:, g % 2, 0:512].rearrange("p (a n) -> p a n", a=4)
            if name in ("o", "y"):
                return xn[:, g % 2, 512:1024].rearrange("p (a n) -> p a n", a=4)
            at = W_GRP + ((g % 2) * 9 + where[name]) * 512
            return wk(at, 512).rearrange("p (a n) -> p a n", a=4)

        def qkvT(j):
            return work[:, W_QKV + j * T:W_QKV + (j + 1) * T]

        def score_buf(i):
            return wk(W_S + (i % 3) * 768, 768).rearrange("p (h n) -> p h n", h=2)

        def out_psum(half, t):
            return (acc if half == 0 else hp)[:, t, :].rearrange("p (k n) -> p k n", k=4)

        def pt_buf(i):
            return wk(W_PT + (i % 2) * 768, 768).rearrange("p (h n) -> p h n", h=2)

        def each(tile, n=4):
            return tile.unsqueeze(1).broadcast_to([P, n, P])

        def per_pair(row, g):
            return pair[:, row, 4 * g:4 * g + 4].unsqueeze(2).broadcast_to([P, 4, P])

        def core_wait(eng, engine, step, g):
            eng.wait_ge(core[engine], core_value(engine, step, g))

        def wait_unit(eng, us, i=None):
            eng.wait_ge(unit_used, val(us + 1, i, BODY))

        def wait_h(eng, n, t, half):
            eng.wait_ge(h_new, 4 * (n - 1) + 2 * t + half + 1)

        def wait_acc(eng, m, t, half):
            q = 2 * t + half
            if q < 3:
                eng.wait_ge(acc_part, 3 * m + q + 1)
            else:
                wait_unit(eng, LAST_UNIT[m])

        block = ctx.enter_context(nc.Block())

        @block.sync
        def _(sp_):
            x_t = a["x"].rearrange("b (t p) d -> p (b t) d", p=P)
            sp_.dma_start(h[:, :, :], x_t).then_inc(x_loaded, 16)

            sp_.dma_start(const[:, :], a["consts"]).then_inc(early_loaded, 16)

            def rows_in(at, k, vector):
                sp_.dma_start(rows[at:at + k, 0, :], vector).then_inc(early_loaded, 16)

            for at, name in ((G_A, "a_pre_norm"), (G_F0, "ffn_pre_norm"), (G_B, "b_pre_norm"),
                             (G_X0, "mix_norm_g_2"), (G_M0, "mlp_norm_g_2")):
                rows_in(at, a[name].shape[0] * KC, a[name].rearrange("l (k p) -> (l k) p", p=P))
            rows_in(G_KV, KC, a["kv_norm"].rearrange("(k p) -> k p", p=P))
            rows_in(G_CONV, 3 * KC, a["a_conv_w"].rearrange("a w (k p) -> (a w k) p", p=P))
            sp_.dma_start(rows[:, 1, :], a["dn_conv_w_2"].rearrange("a w (k p) -> (a w k) p", p=P)) \
                .then_inc(early_loaded, 16)

            def late_loads():
                sp_.dma_start(og[:, :], a["dn_out_norm_g_2"].rearrange("a d -> d a")).then_inc(late_loaded, 16)
                sp_.dma_start(wba, a["dn_w_in_2"][0].rearrange("(k p) n -> p k n", p=P)[:, :, 4 * D:4 * D + 16]) \
                    .then_inc(late_loaded, 16)
                sp_.dma_start(sinks[:, :], a["b_sinks"].broadcast_to([P, NH])).then_inc(late_loaded, 16)
                sp_.dma_start(dtb[:, :], a["dn_dt_bias_2"].broadcast_to([P, NHD])).then_inc(late_loaded, 16)
                sp_.dma_start(alog[:, :], a["dn_a_log_2"].broadcast_to([P, NHD])).then_inc(late_loaded, 16)

            def load_gpost(p):
                vector = [a["a_post_norm"], a["ffn_post_norm"][0:1], a["b_post_norm"],
                          a["ffn_post_norm"][1:2], a["final_norm_g_2"].rearrange("(a d) -> a d", a=1)][p]
                if p >= 2:
                    sp_.wait_ge(h_new, 4 * (p - 2) + 4)
                sp_.dma_start(gpost[:, p % 2, :], vector.broadcast_to([P, D])).then_inc(gpost_loaded[p % 2], 16)

            def load(us, i, src, k):
                if us >= RAW or i is not None:
                    sp_.wait_ge(lo_ready, val(us - RAW + 1, i, BODY))
                sp_.dma_start(w_raw[:, us % RAW, :].rearrange("p (k n) -> p k n", k=k), src) \
                    .then_inc(landed[us % RAW], 16)

            def columns(w):
                return w.rearrange("(k p) n -> p k n", p=P)

            def col_chunk(w, start):
                return columns(w)[:, :, bass.ds(start, P)]

            def row_chunk(w, start):
                return w[bass.ds(start, P), :].unsqueeze(1)

            w_in = a["a_w_in"][0]

            def mixer(js, i):
                for n, kind in enumerate((1, 2, 0)):
                    us = U_MIX + 3 * js + n
                    src = col_chunk(w_in, val(kind * D + js * P, i, 2 * P))
                    load(us, i, src, KC)
            for js in range(2):
                mixer(js, None)
            load_gpost(0)
            load_gpost(1)
            late_loads()
            turns(sp_, 2, KC - 2, 2, mixer)

            def rows_of(u0, w, n=KC):
                for k in range(n):
                    load(u0 + k, None, row_chunk(w, k * P), 1)

            rows_of(U_MIXO, a["a_w_out"][0])

            def swiglu(layer):
                up, down = a["ffn_w_gate_up"][layer], a["ffn_w_down"][layer]
                u0 = U_FF[layer]
                load(u0, None, col_chunk(up, 0), KC)
                load(u0 + 1, None, col_chunk(up, FF), KC)

                def step(js, i):
                    us = u0 + 2 + 3 * js
                    load(us, i, col_chunk(up, val((js + 1) * P, i, 2 * P)), KC)
                    load(us + 1, i, col_chunk(up, val(FF + (js + 1) * P, i, 2 * P)), KC)
                    load(us + 2, i, row_chunk(down, val(js * P, i, 2 * P)), 1)
                step(0, None)
                turns(sp_, 1, NF - 2, 2, step)
                load(u0 + 3 * NF - 1, None, row_chunk(down, (NF - 1) * P), 1)

            def relu2(layer):
                up, down = a["mlp_w_up_2"][layer], a["mlp_w_down_2"][layer]
                u0 = U_MLP[layer]
                load(u0, None, col_chunk(up, 0), KC)
                load(u0 + 1, None, col_chunk(up, P), KC)

                def step(js, i):
                    us = u0 + 2 + 2 * js
                    load(us, i, col_chunk(up, val((js + 2) * P, i, 3 * P)), KC)
                    load(us + 1, i, row_chunk(down, val(js * P, i, 3 * P)), 1)
                step(0, None)
                turns(sp_, 1, NM - 3, 3, step)
                load(u0 + 2 * NM - 2, None, row_chunk(down, (NM - 2) * P), 1)
                load(u0 + 2 * NM - 1, None, row_chunk(down, (NM - 1) * P), 1)

            swiglu(0)
            load_gpost(2)
            w_kv = a["w_kv"].rearrange("(k p) n -> p k n", p=P)
            for n in range(4):
                load(U_KV + n, None, w_kv[:, 2 * n:2 * n + 2, :], 2)
            rows_of(U_Q, a["b_w_q"][0])
            rows_of(U_O, a["b_w_o"][0])
            load_gpost(3)
            swiglu(1)
            load_gpost(4)

            dn = a["dn_w_in_2"][0]
            turns(sp_, 0, 32, BODY, lambda js, i: load(U_DN + js, i, col_chunk(dn, val(js * P, i, BODY * P)), KC))
            rows_of(U_DNO, a["dn_w_out_2"][0])
            relu2(0)
            mb = a["mb_w_in_2"][0]
            rows_of(U_MBV, mb[:, 2 * D:3 * D])
            turns(sp_, 0, 16, BODY, lambda js, i: load(U_MB + js, i, col_chunk(mb, val(js * P, i, BODY * P)), KC))
            rows_of(U_MBO, a["mb_w_out_2"][0])
            relu2(1)

            for t in range(NT):
                sp_.wait_ge(out_ready, t + 1)
                sp_.dma_start(out[0, t * P:(t + 1) * P, :], xn[:, t, :]).then_inc(stored, 16)
            sp_.wait_ge(stored, 16 * NT)

        @block.gpsimd
        def _(pool):
            nc.gpsimd.memset(half_neg[:, :], -0.5).then_inc(pool_const, 1)
            pool.wait_ge(pool_const, 1)
            pool.dma_start(lmask[:, :, :], a["masks"]).then_inc(masks_loaded, 16)

            def pre(n, t):
                q, c = 2 * n + t, 4 * n + 2 * t
                pool.wait_ge(pre_sq, 2 * q + 2)
                nc.gpsimd.tensor_scalar(means[:, c:c + 1], sums[:, c:c + 1], sums[:, c + 1:c + 2], EPS,
                                        ALU.add, ALU.add).then_inc(pre_mean, 1)
                pool.wait_ge(pre_mean, q + 1)
                nc.gpsimd.tensor_tensor(rstd[:, c:c + 1], means[:, c:c + 1], half_neg[:, 0:1], ALU.pow) \
                    .then_inc(pre_rstd, 1)

            def post(m, t):
                e = 2 * m + t
                c = 36 + 2 * e
                pool.wait_ge(post_sq, 2 * e + 2)
                nc.gpsimd.tensor_scalar(means[:, c:c + 1], sums[:, c:c + 1], sums[:, c + 1:c + 2], EPS,
                                        ALU.add, ALU.add).then_inc(post_mean, 1)
                pool.wait_ge(post_mean, e + 1)
                nc.gpsimd.tensor_tensor(rstd[:, c:c + 1], means[:, c:c + 1], half_neg[:, 0:1], ALU.pow) \
                    .then_inc(post_rstd, 1)

            for t in range(NT):
                pre(0, t)
            for us in range(2):
                pool.wait_ge(hi_ready, us + 1)
                if us:
                    pool.wait_ge(lo_ready, us)
                nc.gpsimd.tensor_tensor(w_lo[:, us, :], w_raw[:, us, :], w_hi[:, us, :].bitcast(F32),
                                        ALU.subtract).then_inc(lo_ready, 1)
            for m in range(4):
                for t in range(NT):
                    post(m, t)
                for t in range(NT):
                    pre(m + 1, t)
            pool.wait_ge(ba_step, BA_SUMS)
            nc.gpsimd.tensor_scalar(qkss[:, 0:2, :], qkss[:, 2:4, :], 1.0, 1e-6, ALU.mult, ALU.add).then_inc(ba_pool, 1)
            pool.wait_ge(ba_pool, 1)
            nc.gpsimd.tensor_tensor(pair[:, 0:2, :], qkss[:, 0:2, :],
                                    half_neg[:, :].rearrange("p (a n) -> p a n", a=2), ALU.pow).then_inc(ba_pool, 1)
            pool.wait_ge(ba_step, BA_G)
            for e, step, g in CORE_ORDER:
                if e != "pool":
                    continue
                if step == "gs":
                    if g >= 2:
                        core_wait(pool, "pe", "o1", g - 2)
                    ins = nc.gpsimd.tensor_tensor(core_buf(g, "gs"), each(const[:, C_STRICT:C_STRICT + P]),
                                                  per_pair(3, g), ALU.mult)
                elif step == "decmask":
                    core_wait(pool, "act", "dec", g)
                    nc.gpsimd.tensor_tensor(core_buf(g, "decS"), core_buf(g, "decI"),
                                            each(const[:, C_NEG:C_NEG + P]), ALU.mult)
                    ins = nc.gpsimd.tensor_tensor(core_buf(g, "decI"), core_buf(g, "decI"),
                                                  each(const[:, C_INCL:C_INCL + P]), ALU.mult)
                elif step == "omean":
                    core_wait(pool, "act", "osq", g)
                    ins = nc.gpsimd.tensor_scalar(oss[:, 1, 4 * g:4 * g + 4], oss[:, 0, 4 * g:4 * g + 4],
                                                  1.0 / DH, EPS, ALU.mult, ALU.add)
                else:
                    core_wait(pool, "pool", "omean", g)
                    ins = nc.gpsimd.tensor_tensor(oss[:, 2, 4 * g:4 * g + 4], oss[:, 1, 4 * g:4 * g + 4],
                                                  half_neg[:, 0:4], ALU.pow)
                ins.then_inc(core["pool"], 1)
            for n in range(5, 9):
                for t in range(NT):
                    pre(n, t)

        @block.scalar
        def _(act):
            def split(us, i=None):
                if us >= N_UNITS:
                    return
                act.wait_ge(landed[us % RAW], val(16 * (us // RAW + 1), i, 16 * BODY // RAW))
                if us >= RING or i is not None:
                    act.wait_ge(unit_used, val(us - RING + 1, i, BODY))
                nc.scalar.activation(w_hi[:, us % RING, :], w_raw[:, us % RAW, :], ACT.Copy).then_inc(hi_ready, 1)

            def splits(u0, n):
                for u in range(u0, u0 + n):
                    split(u + AHEAD)

            def last_split(u0):
                split(u0 + KC - 1 + AHEAD)

            def pre_square(n, t, half):
                c = 4 * n + 2 * t + half
                if n == 0:
                    act.wait_ge(x_loaded, 16)
                else:
                    wait_h(act, n, t, half)
                nc.scalar.activation(wk(W_JUNK + 1024 * t + 512 * half, 512), h[:, t, 512 * half:512 * half + 512],
                                     ACT.Square, scale=D ** -0.5, accum_out=sums[:, c:c + 1]).then_inc(pre_sq, 1)

            def post_square(m, t, half):
                c = 36 + 4 * m + 2 * t + half
                wait_acc(act, m, t, half)
                nc.scalar.activation(wk(W_JUNK + (2 + t) * D + 512 * half, 512), acc[:, 2 * t + half, :],
                                     ACT.Square, scale=D ** -0.5, accum_out=sums[:, c:c + 1]).then_inc(post_sq, 1)

            def pre_diag(n, t):
                if n == 0:
                    act.wait_ge(early_loaded, 16 * 9)
                act.wait_ge(pre_rstd, 2 * n + t + 1)
                nc.scalar.activation(diag[:, t, :], ident, ACT.Copy, scale=rstd[:, 4 * n + 2 * t:4 * n + 2 * t + 1]) \
                    .then_inc(diag_ready, 1)

            n_hi = [0]

            def pre_hi(hi, t, half):
                n_hi[0] += 1
                act.wait_ge(xf_ready, n_hi[0])
                nc.scalar.activation(hi[:, 4 * half:4 * half + 4, t * P:(t + 1) * P],
                                     xf[:, n_hi[0] % 2, :].rearrange("p (k n) -> p k n", k=4), ACT.Copy) \
                    .then_inc(xhi_ready, 1)

            def norm(n, post, his=None):
                his = his or [xh]
                if post:
                    post_square(n - 1, 0, 0)
                    post_square(n - 1, 0, 1)
                    post_square(n - 1, 1, 0)
                pre_square(n, 0, 0)
                if post:
                    post_square(n - 1, 1, 1)
                pre_square(n, 0, 1)
                if n:
                    pre_diag(n, 0)
                pre_square(n, 1, 0)
                pre_square(n, 1, 1)
                if not n:
                    pre_diag(n, 0)
                    pre_diag(n, 1)
                    split(0)
                    split(1)
                pre_hi(his[0], 0, 0)
                if n:
                    pre_diag(n, 1)
                for r, hi in enumerate(his):
                    for t in range(NT):
                        for half in range(2):
                            if r or t or half:
                                pre_hi(hi, t, half)

            norm(0, False)
            for u in range(2, AHEAD):
                split(u)

            def mixer(js, i):
                us = U_MIX + 3 * js
                split(us + AHEAD, i)
                split(us + AHEAD + 1, i)
                wait_unit(act, us, i)
                if js >= 2 or i is not None:
                    act.wait_ge(y_ready, val(js - 1, i, 2))
                nc.scalar.activation(wk(W_CSB + (js % 2) * T, T), mix_psum(js, 0), ACT.Copy).then_inc(c_copied, 1)
                split(us + AHEAD + 2, i)
            for js in range(2):
                mixer(js, None)
            turns(act, 2, KC - 2, 2, mixer)
            splits(U_MIXO, KC - 1)
            norm(1, True)
            last_split(U_MIXO)

            def swiglu(layer):
                u0, fb = U_FF[layer], NF * layer

                def silu(js, i, unit):
                    wait_unit(act, unit, i)
                    if fb + js >= 2 or i is not None:
                        act.wait_ge(hid_mul, val(fb + js - 1, i, 2))
                    nc.scalar.activation(wk(W_SG + (js % 2) * T, T), hp[:, 2 * (js % 2), 0:T], ACT.Silu) \
                        .then_inc(act_done, 1)
                split(u0 + AHEAD)
                split(u0 + AHEAD + 1)
                silu(0, None, u0)

                def step(js, i):
                    us = u0 + 2 + 3 * js
                    split(us + AHEAD, i)
                    split(us + AHEAD + 1, i)
                    silu(js + 1, i, us)
                    split(us + AHEAD + 2, i)
                step(0, None)
                turns(act, 1, NF - 2, 2, step)
                split(u0 + 3 * NF - 1 + AHEAD)

            def relu2(layer):
                u0, cb = U_MLP[layer], 2 * NF + NM * layer

                def relu(js, i, unit):
                    wait_unit(act, unit, i)
                    act.wait_ge(hid_mul, val(cb + js - 2, i, 3))
                    nc.scalar.activation(wk(W_SG + (js % 3) * T, T), hp[:, js % 3, 0:T], ACT.Relu) \
                        .then_inc(act_done, 1)
                split(u0 + AHEAD)
                relu(0, None, u0)
                split(u0 + AHEAD + 1)
                relu(1, None, u0 + 1)

                def step(js, i):
                    us = u0 + 2 + 2 * js
                    split(us + AHEAD, i)
                    split(us + AHEAD + 1, i)
                    relu(js + 2, i, us)
                step(0, None)
                turns(act, 1, NM - 3, 3, step)
                split(u0 + 2 * NM - 2 + AHEAD)
                split(u0 + 2 * NM - 1 + AHEAD)

            def heads(first, n, scale, sink):
                def exp(k):
                    i = first + k
                    s = score_buf(i)
                    act.wait_ge(nm_ready, i + 1)
                    if sink:
                        act.wait_ge(dsk_ready, i + 1)
                        nc.scalar.activation(es[:, 2 * i:2 * i + 2, :], dsk[:, 2 * i:2 * i + 2, :], ACT.Exp)
                    for hd in range(2):
                        for t, cols in enumerate((slice(0, P), slice(P, 384))):
                            ins = nc.scalar.activation(s[:, hd, cols], s[:, hd, cols], ACT.Exp,
                                                       bias=nm[:, 2 * i + hd, t:t + 1], scale=scale,
                                                       accum_out=den[:, 2 * i + hd, t:t + 1])
                    ins.then_inc(p_ready, 1)

                def pt_copy(k):
                    i = first + k
                    act.wait_ge(pt_ps, i + 1)
                    if i >= 2:
                        act.wait_ge(pv_done, i - 1)
                    nc.scalar.activation(pt_buf(i), hp[:, 0:2, 0:384], ACT.Copy).then_inc(pt_ready, 1)
                for k in range(n + 2):
                    if 1 <= k <= n:
                        exp(k - 1)
                    if k >= 2:
                        pt_copy(k - 2)
                for m in range(4):
                    half, t = m // 2, m % 2
                    act.wait_ge(oT_ps, (0 if sink else 4) + m + 1)
                    nc.scalar.activation(xh[:, 4 * half:4 * half + 4, t * P:(t + 1) * P], out_psum(half, t), ACT.Copy) \
                        .then_inc(oT_hi, 1)

            swiglu(0)
            norm(2, True, [xh, yh])
            splits(U_KV, 2)
            for t in range(NT):
                wait_unit(act, U_Q - 1)
                nc.scalar.activation(wk(W_KDUP + t * 512, 512).rearrange("p (g c n) -> p g c n", g=4, c=2)[:, :, 0, :],
                                     acc[:, 2 + t, 0:256].rearrange("p (g n) -> p g n", g=4), ACT.Copy)
                nc.scalar.activation(wk(W_V + t * 256, 256), acc[:, 2 + t, 256:512], ACT.Copy).then_inc(kv_copied, 1)
            splits(U_KV + 2, 2)
            splits(U_Q, KC - 1)
            for t in range(NT):
                if t == 0:
                    act.wait_ge(qv_part, 2)
                else:
                    wait_unit(act, U_O - 1)
                nc.scalar.activation(wk(W_QTOK + t * D, D).rearrange("p (a n) -> p a n", a=2), acc[:, 2 * t:2 * t + 2, :],
                                     ACT.Copy).then_inc(q_copied, 1)
            last_split(U_Q)
            for t in range(NT):
                act.wait_ge(kT_ps, t + 1)
                nc.scalar.activation(wk(W_KT, 1024).rearrange("p (g n) -> p g n", g=4)[:, :, t * P:(t + 1) * P],
                                     hp[:, 2 + t, :].rearrange("p (g n) -> p g n", g=4), ACT.Copy).then_inc(kT_copied, 1)
            for t in range(NT):
                for half in range(2):
                    act.wait_ge(qT_ps, 2 * t + half + 1)
                    nc.scalar.activation(
                        wk(W_QT + half * 1024, 1024).rearrange("p (g n) -> p g n", g=4)[:, :, t * P:(t + 1) * P],
                        hp[:, 2 * t + half, :].rearrange("p (g n) -> p g n", g=4), ACT.Copy).then_inc(qT_copied, 1)
            heads(0, NH // 2, 1.0, True)
            splits(U_O, KC - 1)
            norm(3, True)
            last_split(U_O)
            swiglu(1)
            norm(4, True)

            def gates():
                act.wait_ge(ba_step, BA_IN)
                nc.scalar.activation(sp[:, 0, :].rearrange("p (h t) -> p h t", t=2),
                                     ba[:, :, 0:8].rearrange("p t h -> p h t"), ACT.Exp, scale=-1.0)
                nc.scalar.activation(sp[:, 2, :], sp[:, 1, :], ACT.Exp, scale=-1.0)
                nc.scalar.activation(sp[:, 3, 0:8], alog[:, :], ACT.Exp).then_inc(ba_act, 1)
                act.wait_ge(ba_act, 1)
                nc.scalar.activation(sp[:, 4, :], sp[:, 2, :], ACT.Ln, bias=1.0).then_inc(ba_act, 1)

            def conv(js, i):
                split(U_DN + js + AHEAD, i)
                if js >= 2 or i is not None:
                    silu(js - 2, i)
                wait_unit(act, U_DN + js, i)
                c, y = W_CBUF + (js % 3) * 260, W_YBUF + (js % 3) * T
                if js >= 3 or i is not None:
                    act.wait_ge(conv_step, val(3 * (js - 2), i, 3 * BODY))
                nc.scalar.activation(wk(c + 3, T), small_psum(js % 3), ACT.Copy).then_inc(conv_in, 1)
                act.wait_ge(conv_in, val(js + 1, i, BODY))
                if js >= 3 or i is not None:
                    act.wait_ge(conv_silu, val(js - 2, i, BODY))
                nc.scalar.activation(wk(y, T), wk(c, T), ACT.Copy, scale=cT[:, bass.ds(val(js, i, BODY), 1)]) \
                    .then_inc(conv_first, 1)

            def silu(js, i):
                act.wait_ge(conv_step, val(3 * (js + 1), i, 3 * BODY))
                at = val(W_QKV + js * T, i, BODY * T)
                nc.scalar.activation(work[:, bass.ds(at, T)], wk(W_YBUF + (js % 3) * T, T), ACT.Silu) \
                    .then_inc(conv_silu, 1)
            for js in range(BODY):
                conv(js, None)
                if js == 3:
                    gates()
            turns(act, BODY, DN_STRAIGHT - BODY, BODY, conv)
            for js in range(DN_STRAIGHT, 24):
                conv(js, None)
                if js - DN_STRAIGHT < 4:
                    part = js - DN_STRAIGHT
                    if part == 3:
                        act.wait_ge(conv_silu, 16)
                    nc.scalar.activation(wk(W_SQ + part * 4 * T, 4 * T), wk(W_QKV + part * 4 * T, 4 * T), ACT.Square) \
                        .then_inc(qk_sq, 1)
            silu(22, None)
            silu(23, None)
            for j in range(24, 32):
                split(U_DN + j + AHEAD)
                wait_unit(act, U_DN + j)
                nc.scalar.activation(wk(W_Z + (j - 24) * T, T), small_psum(j % 3), ACT.Silu).then_inc(z_ready, 1)
            act.wait_ge(gc_ps, 1)
            nc.scalar.activation(pair[:, 4:6, :], acc[:, 2, 0:32].rearrange("p (a n) -> p a n", a=2), ACT.Exp) \
                .then_inc(ba_act, 1)

            for e, step, g in CORE_ORDER:
                if e != "act":
                    continue
                bank = lambda b: core_bank(g, b)
                buf = lambda name: core_buf(g, name)
                if step == "dec":
                    core_wait(act, "pe", "decay", g)
                    ins = nc.scalar.activation(buf("decI"), bank(2), ACT.Exp)
                elif step == "knT_copy":
                    core_wait(act, "pe", "knT", g)
                    if g >= 2:
                        core_wait(act, "act", "osq", g - 2)
                    nc.scalar.activation(buf("knT"), bank(0), ACT.Copy)
                    ins = nc.scalar.activation(buf("kbT"), bank(1), ACT.Copy)
                elif step == "z_init":
                    ins = nc.scalar.activation(buf("Z"), each(ident), ACT.Copy)
                elif step == "x_copy":
                    core_wait(act, "pe", "xT", g)
                    core_wait(act, "dve", "kd", g)
                    ins = nc.scalar.activation(buf("X"), bank(0), ACT.Copy)
                elif step.startswith("y"):
                    core_wait(act, "pe", step[:-5], g)
                    ins = nc.scalar.activation(buf("Y"), bank(0), ACT.Copy)
                elif step == "vn0_copy":
                    core_wait(act, "pe", "vn0", g)
                    ins = nc.scalar.activation(buf("vn")[:, 0:3:2, :], bank(0)[:, 0:2, :], ACT.Copy)
                elif step == "state_copy":
                    core_wait(act, "pe", "state", g)
                    ins = nc.scalar.activation(buf("SR")[:, 0:2, :], bank(1)[:, 0:2, :], ACT.Copy)
                elif step == "vn1_copy":
                    core_wait(act, "pe", "vn1", g)
                    ins = nc.scalar.activation(buf("vn")[:, 1:4:2, :], bank(0)[:, 2:4, :], ACT.Copy)
                else:
                    core_wait(act, "dve", "o", g)
                    for p in range(4):
                        ins = nc.scalar.activation(buf("kbT")[:, p, :], buf("o")[:, p, :], ACT.Square,
                                                   accum_out=oss[:, 0, 4 * g + p:4 * g + p + 1])
                ins.then_inc(core["act"], 1)

            splits(U_DNO, KC - 1)
            norm(5, False)
            last_split(U_DNO)
            relu2(0)
            norm(6, False)

            def qk_copy(js, i):
                split(U_MB + js + AHEAD, i)
                wait_unit(act, U_MB + js, i)
                nc.scalar.activation(work[:, bass.ds(val(W_MQK + js * T, i, BODY * T), T)], small_psum(js % 3),
                                     ACT.Copy).then_inc(mb_copied, 1)
            splits(U_MBV, KC)
            for t in range(NT):
                wait_unit(act, U_MB - 1)
                nc.scalar.activation(wk(W_MV + t * D, D).rearrange("p (a n) -> p a n", a=2), acc[:, 2 * t:2 * t + 2, :],
                                     ACT.Copy).then_inc(mbv_copied, 1)
            turns(act, 0, 16, BODY, qk_copy)
            heads(NH // 2, NHD // 2, MB_SCALE, False)
            splits(U_MBO, KC - 1)
            norm(7, False)
            last_split(U_MBO)
            relu2(1)
            for t in range(NT):
                for half in range(2):
                    pre_square(8, t, half)

        @block.vector
        def _(dve):
            def split(us, i=None):
                if us >= N_UNITS:
                    return
                dve.wait_ge(hi_ready, val(us + 1, i, BODY))
                nc.vector.tensor_tensor(w_lo[:, us % RING, :], w_raw[:, us % RAW, :],
                                        w_hi[:, us % RING, :].bitcast(F32), ALU.subtract).then_inc(lo_ready, 1)

            def splits(u0, n):
                for u in range(u0, u0 + n):
                    split(u + AHEAD)

            def last_split(u0):
                split(u0 + KC - 1 + AHEAD)

            n_hi = [0]

            def pre(n, gains):
                for gain, hi, lo in gains:
                    for t in range(NT):
                        for half in range(2):
                            n_f = n_hi[0] + half + 1
                            dve.wait_ge(xT_ps, 4 * n + 2 * t + half + 1)
                            if n_f > 2:
                                dve.wait_ge(xT_ready, n_f - 2)
                            nc.vector.tensor_tensor(
                                xf[:, n_f % 2, :].rearrange("p (k n) -> p k n", k=4),
                                hp[:, 2 * t + half, :].rearrange("p (k n) -> p k n", k=4),
                                gT[:, gain + 4 * half:gain + 4 * half + 4].unsqueeze(2).broadcast_to([P, 4, P]),
                                ALU.mult).then_inc(xf_ready, 1)
                        for half in range(2):
                            n_hi[0] += 1
                            at = (slice(None), slice(4 * half, 4 * half + 4), slice(t * P, (t + 1) * P))
                            dve.wait_ge(xhi_ready, n_hi[0])
                            nc.vector.tensor_tensor(
                                lo[at], xf[:, n_hi[0] % 2, :].rearrange("p (k n) -> p k n", k=4),
                                hi[at].bitcast(F32), ALU.subtract).then_inc(xT_ready, 1)

            def post(m):
                dve.wait_ge(gpost_loaded[m % 2], 16 * (m // 2 + 1))
                for t in range(NT):
                    e = 2 * m + t
                    for half in range(2):
                        cols = slice(512 * half, 512 * half + 512)
                        dve.wait_ge(post_sq, 2 * e + half + 1)
                        nc.vector.tensor_tensor(xn[:, t, cols], acc[:, 2 * t + half, :], gpost[:, m % 2, cols],
                                                ALU.mult).then_inc(post_tmp, 1)
                    dve.wait_ge(post_tmp, 2 * e + 2)
                    dve.wait_ge(post_rstd, e + 1)
                    for half in range(2):
                        at = (slice(None), t, slice(512 * half, 512 * half + 512))
                        nc.vector.scalar_tensor_tensor(out=h[at], in0=xn[at], scalar=rstd[:, 36 + 2 * e:37 + 2 * e],
                                                       in1=h[at], op0=ALU.mult, op1=ALU.add).then_inc(h_new, 1)

            def residual(m):
                for t in range(NT):
                    for half in range(2):
                        wait_acc(dve, m, t, half)
                        at = (slice(None), t, slice(512 * half, 512 * half + 512))
                        nc.vector.tensor_tensor(h[at], acc[:, 2 * t + half, :], h[at], ALU.add).then_inc(h_new, 1)

            dve.wait_ge(rows_T, 1)
            nc.vector.tensor_copy(gT[:, :], acc[:, 0, 0:96])
            nc.vector.tensor_copy(cT[:, :], acc[:, 1, 0:96]).then_inc(gains_ready, 1)
            dve.wait_ge(gains_ready, 1)
            nc.vector.memset(wk(W_CU, 2), 0.0).then_inc(pad_zero, 1)
            dve.wait_ge(pad_zero, 1)
            pre(0, [(G_A, xh, xl)])
            dve.wait_ge(lo_ready, 2)
            for u in range(2, AHEAD):
                split(u)

            def mixer(js, i):
                us = U_MIX + 3 * js
                for n in range(3):
                    split(us + AHEAD + n, i)
                cu = wk(W_CU, T + 2)
                y = wk(W_Y + (js % 2) * T, T)

                def tap(w):
                    return gT[:, bass.ds(val(G_CONV + w * KC + js, i, 2), 1)]

                def done(ins, n):
                    ins.then_inc(cu_step, 1)
                    dve.wait_ge(cu_step, val(6 * js + n, i, 12))
                dve.wait_ge(c_copied, val(js + 1, i, 2))
                wait_unit(dve, us + 2, i)
                done(nc.vector.tensor_tensor(cu[:, 2:T + 2], mix_psum(js, 1), wk(W_CSB + (js % 2) * T, T), ALU.mult), 1)
                done(nc.vector.tensor_scalar(y, cu[:, 0:T], tap(0), None, ALU.mult), 2)
                done(nc.vector.scalar_tensor_tensor(out=y, in0=cu[:, 1:T + 1], scalar=tap(1), in1=y,
                                                    op0=ALU.mult, op1=ALU.add), 3)
                done(nc.vector.scalar_tensor_tensor(out=y, in0=cu[:, 2:T + 2], scalar=tap(2), in1=y,
                                                    op0=ALU.mult, op1=ALU.add), 4)
                done(nc.vector.tensor_tensor(y, mix_psum(js, 2), y, ALU.mult), 5)
                chunk = bass.ds(val(js, i, 2), 1)
                done(nc.vector.tensor_copy(yh[:, chunk, :], y.unsqueeze(1)), 6)
                nc.vector.tensor_tensor(yl[:, chunk, :], y.unsqueeze(1), yh[:, chunk, :].bitcast(F32),
                                        ALU.subtract).then_inc(y_ready, 1)
            for js in range(2):
                mixer(js, None)
            turns(dve, 2, KC - 2, 2, mixer)
            splits(U_MIXO, KC - 1)
            post(0)
            pre(1, [(G_F0, xh, xl)])
            last_split(U_MIXO)

            def hidden(js, i, cb, ring, up_bank, unit):
                n = lambda d: val(cb + js + d, i, ring)
                sg, hx = wk(W_SG + (js % ring) * T, T), wk(W_HX + (js % ring) * T, T)
                dve.wait_ge(act_done, n(1))
                wait_unit(dve, unit, i)
                nc.vector.tensor_tensor(hx, hp[:, up_bank, 0:T], sg, ALU.mult).then_inc(hid_mul, 1)
                dve.wait_ge(hid_mul, n(1))
                nc.vector.tensor_copy(hh[:, js % ring, :], hx).then_inc(hid_hi, 1)
                dve.wait_ge(hid_hi, n(1))
                nc.vector.tensor_tensor(hl[:, js % ring, :], hx, hh[:, js % ring, :].bitcast(F32), ALU.subtract) \
                    .then_inc(hid_ready, 1)

            def swiglu(layer):
                u0, cb = U_FF[layer], NF * layer
                split(u0 + AHEAD)
                split(u0 + AHEAD + 1)
                hidden(0, None, cb, 2, 1, u0 + 1)

                def step(js, i):
                    us = u0 + 2 + 3 * js
                    for n in range(3):
                        split(us + AHEAD + n, i)
                    if js >= 1 or i is not None:
                        wait_unit(dve, us - 1, i)
                    hidden(js + 1, i, cb, 2, 2 * ((js + 1) % 2) + 1, us + 1)
                step(0, None)
                turns(dve, 1, NF - 2, 2, step)
                split(u0 + 3 * NF - 1 + AHEAD)

            def relu2(layer):
                u0, cb = U_MLP[layer], 2 * NF + NM * layer
                split(u0 + AHEAD)
                hidden(0, None, cb, 3, 0, u0)
                split(u0 + AHEAD + 1)
                hidden(1, None, cb, 3, 1, u0 + 1)

                def step(js, i):
                    us = u0 + 2 + 2 * js
                    split(us + AHEAD, i)
                    split(us + AHEAD + 1, i)
                    if js >= 1 or i is not None:
                        wait_unit(dve, us - 1, i)
                    hidden(js + 2, i, cb, 3, (js + 2) % 3, us)
                step(0, None)
                turns(dve, 1, NM - 3, 3, step)
                split(u0 + 2 * NM - 2 + AHEAD)
                split(u0 + 2 * NM - 1 + AHEAD)

            def rotary(n, view, t, nh):
                t1, t2 = view[:, :, 0:ROT], view[:, :, ROT:2 * ROT]
                cos = const[:, C_COS + t * ROT:C_COS + (t + 1) * ROT].unsqueeze(1).broadcast_to([P, nh, ROT])
                sin = const[:, C_SIN + t * ROT:C_SIN + (t + 1) * ROT].unsqueeze(1).broadcast_to([P, nh, ROT])
                r = [wk(W_RT + k * P, nh * ROT).rearrange("p (g n) -> p g n", g=nh) for k in range(4)]
                if n:
                    dve.wait_ge(rot_done, 2 * n)
                for k, (u, v) in enumerate(((t1, cos), (t2, sin), (t2, cos), (t1, sin))):
                    nc.vector.tensor_tensor(r[k], u, v, ALU.mult).then_inc(rot_mul, 1)
                dve.wait_ge(rot_mul, 4 * (n + 1))
                nc.vector.tensor_tensor(t1, r[0], r[1], ALU.subtract).then_inc(rot_done, 1)
                nc.vector.tensor_tensor(t2, r[2], r[3], ALU.add).then_inc(rot_done, 1)

            def heads(first, n, sink):
                def scores(k):
                    i = first + k
                    s = score_buf(i)
                    of = slice(2 * i, 2 * i + 2)
                    dve.wait_ge(sc_done, i + 1)
                    if i >= 3:
                        dve.wait_ge(pt_ps, i - 2)
                    ps = acc[:, 2 * (i % 2):2 * (i % 2) + 2, 0:384]
                    if sink:
                        ins = nc.vector.scalar_tensor_tensor(
                            out=s, in0=ps, scalar=SW_SCALE, op0=ALU.mult, op1=ALU.add,
                            in1=const[:, C_BAND:C_BAND + 384].unsqueeze(1).broadcast_to([P, 2, 384]))
                    else:
                        for hd in range(2):
                            slope = 2.0 ** (-8.0 * (2 * k + hd + 1) / NHD)
                            ins = nc.vector.scalar_tensor_tensor(out=s[:, hd, :], in0=const[:, C_DIST:C_DIST + 384],
                                                                 scalar=slope / MB_SCALE, in1=ps[:, hd, :],
                                                                 op0=ALU.mult, op1=ALU.add)
                    ins.then_inc(s_made, 1)
                    dve.wait_ge(s_made, i + 1)
                    nc.vector.tensor_reduce(mx[:, of, 0], s[:, :, 0:P], X, ALU.max, negate=True).then_inc(mx_done, 1)
                    nc.vector.tensor_reduce(mx[:, of, 1], s[:, :, P:384], X, ALU.max, negate=True).then_inc(mx_done, 1)
                    dve.wait_ge(mx_done, 2 * (i + 1))
                    if sink:
                        neg_sink = pair[:, 11, 2 * k:2 * k + 2].unsqueeze(2).broadcast_to([P, 2, 2])
                        nc.vector.tensor_tensor(nm[:, of, :], mx[:, of, :], neg_sink, ALU.min).then_inc(nm_ready, 1)
                        dve.wait_ge(nm_ready, i + 1)
                        nc.vector.tensor_tensor(dsk[:, of, :], nm[:, of, :], neg_sink, ALU.subtract) \
                            .then_inc(dsk_ready, 1)
                    else:
                        nc.vector.tensor_scalar(nm[:, of, :], mx[:, of, :], MB_SCALE, None, ALU.mult) \
                            .then_inc(nm_ready, 1)

                def norm(k):
                    i = first + k
                    dh = HD if sink else DH
                    of = slice(2 * i, 2 * i + 2)
                    dve.wait_ge(p_ready, i + 1)
                    total = den
                    if sink:
                        nc.vector.tensor_tensor(dtot[:, of, :], den[:, of, :], es[:, of, :], ALU.add).then_inc(den_ready, 1)
                        dve.wait_ge(den_ready, i + 1)
                        total = dtot
                    nc.vector.reciprocal(rinv[:, of, :], total[:, of, :]).then_inc(rinv_ready, 1)
                    dve.wait_ge(rinv_ready, i + 1)
                    dve.wait_ge(pv_done, i + 1)
                    nc.vector.tensor_tensor(
                        xn[:, :, 2 * k * dh:(2 * k + 2) * dh].rearrange("p t (h n) -> p t h n", h=2),
                        hp[:, 2 + i % 2, 0:4 * dh].rearrange("p (t h n) -> p t h n", t=2, h=2),
                        rinv[:, of, :].rearrange("p h t -> p t h").unsqueeze(3).broadcast_to([P, 2, 2, dh]),
                        ALU.mult).then_inc(o_made, 1)
                for k in range(n + 3):
                    if k < n:
                        scores(k)
                    if k >= 3:
                        norm(k - 3)
                out_T(xh, xl, 0 if sink else 1)

            def out_T(hi, lo, s):
                for n in range(4):
                    half, t = n // 2, n % 2
                    at = (slice(None), slice(4 * half, 4 * half + 4), slice(t * P, (t + 1) * P))
                    dve.wait_ge(oT_hi, 4 * s + n + 1)
                    nc.vector.tensor_tensor(lo[at], out_psum(half, t), hi[at].bitcast(F32), ALU.subtract) \
                        .then_inc(oT_ready, 1)

            swiglu(0)
            post(1)
            pre(2, [(G_KV, xh, xl), (G_B, yh, yl)])
            dve.wait_ge(late_loaded, 16 * 5)
            nc.vector.tensor_copy(wba_split[:, :, 0, :], wba).then_inc(wba_step, 1)
            dve.wait_ge(wba_step, 1)
            nc.vector.tensor_tensor(wba_split[:, :, 1, :], wba, wba_split[:, :, 0, :].bitcast(F32), ALU.subtract) \
                .then_inc(wba_step, 1)
            splits(U_KV, 4)
            dve.wait_ge(late_loaded, 16 * 5)
            nc.vector.tensor_scalar(pair[:, 11, :], sinks[:, :], -1.0, None, ALU.mult).then_inc(k_dup, 1)
            dve.wait_ge(k_dup, 1)
            for t in range(NT):
                dve.wait_ge(kv_copied, t + 1)
                kd = wk(W_KDUP + t * 512, 512).rearrange("p (g c n) -> p g c n", g=4, c=2)
                rotary(t, kd[:, :, 0, :], t, NKV)
                dve.wait_ge(rot_done, 2 * (t + 1))
                nc.vector.tensor_copy(kd[:, :, 1, :], kd[:, :, 0, :]).then_inc(k_dup, 1)
            splits(U_Q, KC - 1)
            for t in range(NT):
                dve.wait_ge(q_copied, t + 1)
                rotary(2 + t, wk(W_QTOK + t * D, D).rearrange("p (g n) -> p g n", g=NH), t, NH)
            last_split(U_Q)
            heads(0, NH // 2, True)
            splits(U_O, KC - 1)
            post(2)
            pre(3, [(G_F1, xh, xl)])
            last_split(U_O)
            swiglu(1)
            nc.vector.memset(wk(W_CBUF, 3 * 260), 0.0).then_inc(pad_zero, 1)
            post(3)
            dve.wait_ge(pad_zero, 2)
            pre(4, [(G_X0, xh, xl)])

            def gate_inputs():
                dve.wait_ge(ba_ps, NT)
                two = acc[:, 0, 0:64].rearrange("p (t s n) -> p t s n", t=2, s=2)
                nc.vector.tensor_copy(ba[:, :, :], two[:, :, 0, :]).then_inc(ba_step, 1)
                dve.wait_ge(ba_step, 1)
                nc.vector.tensor_tensor(ba[:, :, :], two[:, :, 1, :], ba[:, :, :], ALU.add).then_inc(ba_step, 1)
                dve.wait_ge(ba_step, 2)
                nc.vector.tensor_tensor(th(sp[:, 5, :]), ba[:, :, 8:16].rearrange("p t h -> p h t"),
                                        dtb[:, :].unsqueeze(2).broadcast_to([P, NHD, 2]), ALU.add).then_inc(ba_step, 1)
                dve.wait_ge(ba_step, 3)
                nc.vector.scalar_tensor_tensor(out=sp[:, 1, :], in0=sp[:, 5, :], scalar=-1.0, in1=sp[:, 5, :],
                                               op0=ALU.mult, op1=ALU.max).then_inc(ba_step, 1)

            def gates():
                dve.wait_ge(ba_act, 2)
                nc.vector.tensor_scalar(sp[:, 6, :], sp[:, 0, :], 1.0, None, ALU.add).then_inc(ba_step, 1)
                dve.wait_ge(ba_step, 5)
                nc.vector.reciprocal(pair[:, 2, :], sp[:, 6, :]).then_inc(ba_step, 1)
                nc.vector.scalar_tensor_tensor(out=sp[:, 7, :], in0=sp[:, 5, :], scalar=0.0, in1=sp[:, 4, :],
                                               op0=ALU.max, op1=ALU.add).then_inc(ba_step, 1)
                dve.wait_ge(ba_step, 7)
                nc.vector.scalar_tensor_tensor(out=th(pair[:, 3, :]), in0=th(sp[:, 7, :]), scalar=-1.0,
                                               in1=sp[:, 3, 0:8].unsqueeze(2).broadcast_to([P, NHD, 2]),
                                               op0=ALU.mult, op1=ALU.mult).then_inc(ba_step, 1)

            th = lambda v: v.rearrange("p (h t) -> p h t", t=2)
            def tap(js, i, w, step):
                dve.wait_ge(conv_step, val(step, i, 3 * BODY))
                y = wk(W_YBUF + (js % 3) * T, T)
                nc.vector.scalar_tensor_tensor(
                    out=y, in0=wk(W_CBUF + (js % 3) * 260 + w, T), scalar=cT[:, bass.ds(val(w * 24 + js, i, BODY), 1)],
                    in1=y, op0=ALU.mult, op1=ALU.add).then_inc(conv_step, 1)

            def conv(js, i):
                if js >= 1 or i is not None:
                    tap(js - 1, i, 3, 3 * js - 1)
                dve.wait_ge(conv_first, val(js + 1, i, BODY))
                y = wk(W_YBUF + (js % 3) * T, T)
                nc.vector.scalar_tensor_tensor(
                    out=y, in0=wk(W_CBUF + (js % 3) * 260 + 1, T), scalar=cT[:, bass.ds(val(24 + js, i, BODY), 1)],
                    in1=y, op0=ALU.mult, op1=ALU.add).then_inc(conv_step, 1)
                split(U_DN + js + AHEAD, i)
                tap(js, i, 2, 3 * js + 1)
            for js in range(BODY):
                if js == 3:
                    gate_inputs()
                conv(js, None)
                if js == 4:
                    gates()
            turns(dve, BODY, 24 - BODY, BODY, conv)
            tap(23, None, 3, 3 * 24 - 1)
            for j in range(24, 32):
                split(U_DN + j + AHEAD)
                if j == 28:
                    dve.wait_ge(qk_ps, 4)
                    nc.vector.tensor_copy(qkss[:, 2:4, :], acc[:, 1, 0:32].rearrange("p (a n) -> p a n", a=2)) \
                        .then_inc(ba_step, 1)
            dve.wait_ge(ba_pool, 2)
            dve.wait_ge(ba_act, 3)
            row = lambda r: pair[:, r, :]
            nc.vector.tensor_tensor(row(6), row(1), row(2), ALU.mult).then_inc(ba_step, 1)
            nc.vector.scalar_tensor_tensor(out=row(8), in0=row(2), scalar=-1.0, in1=row(4),
                                           op0=ALU.mult, op1=ALU.mult).then_inc(ba_step, 1)
            nc.vector.tensor_scalar(row(9), row(0), DH ** -0.5, None, ALU.mult).then_inc(ba_step, 1)
            nc.vector.scalar_tensor_tensor(out=row(10), in0=row(0), scalar=DH ** -0.5, in1=row(4),
                                           op0=ALU.mult, op1=ALU.mult).then_inc(ba_step, 1)
            dve.wait_ge(ba_step, BA_SUMS + 4)

            dve.wait_ge(masks_loaded, 16)
            level = lambda n, flip: lmask[:, 2 * n + flip, :].unsqueeze(1).broadcast_to([P, 4, P])
            for e, step, g in CORE_ORDER:
                if e != "dve":
                    continue
                bank = lambda b: core_bank(g, b)
                buf = lambda name: core_buf(g, name)
                if step == "kscale":
                    core_wait(dve, "pe", "kvT", g)
                    tt = nc.vector.tensor_tensor
                    tt(buf("kn"), bank(0), per_pair(1, g), ALU.mult)
                    tt(buf("kb"), bank(0), per_pair(6, g), ALU.mult)
                    ins = tt(buf("vb"), bank(1), per_pair(2, g), ALU.mult)
                elif step == "kd":
                    core_wait(dve, "dve", "kscale", g)
                    ins = nc.vector.tensor_tensor(buf("kd"), buf("kn"), per_pair(5, g), ALU.mult)
                elif step == "attn":
                    core_wait(dve, "pe", "scores", g)
                    core_wait(dve, "pool", "decmask", g)
                    ins = nc.vector.tensor_tensor(buf("attnT"), bank(2), buf("decI"), ALU.mult)
                elif step == "b":
                    core_wait(dve, "pe", "scores", g)
                    core_wait(dve, "pool", "decmask", g)
                    ins = nc.vector.tensor_tensor(buf("B"), bank(3), buf("decS"), ALU.mult)
                elif step == "z0":
                    core_wait(dve, "act", "z_init", g)
                    core_wait(dve, "dve", "b", g)
                    ins = nc.vector.copy_predicated(buf("Z"), level(0, 1), buf("B"))
                elif step[0] == "x":
                    n = int(step[1:])
                    core_wait(dve, "pe", f"d{n}", g)
                    ins = nc.vector.copy_predicated(buf("X"), level(n, 0), bank(1))
                elif step.startswith("zT"):
                    core_wait(dve, "pe", step[:-5], g)
                    ins = nc.vector.tensor_copy(buf("Z"), bank(2))
                elif step == "z_last":
                    core_wait(dve, "pe", f"d{LEVELS - 1}", g)
                    ins = nc.vector.copy_predicated(buf("Z"), level(LEVELS - 1, 1), bank(1))
                elif step == "rhs1":
                    core_wait(dve, "pe", "kqs", g)
                    for hd in range(2):
                        p = 4 * g + 2 * hd + 1
                        ins = nc.vector.scalar_tensor_tensor(
                            out=buf("SR")[:, 2 + hd, :], in0=bank(3)[:, hd, :], scalar=pair[:, 8, p:p + 1],
                            in1=buf("vb")[:, 2 * hd + 1, :], op0=ALU.mult, op1=ALU.add)
                elif step == "t1":
                    for hd in range(2):
                        p = 4 * g + 2 * hd + 1
                        ins = nc.vector.tensor_scalar(buf("t1")[:, hd, :], bank(3)[:, 2 + hd, :],
                                                      pair[:, 10, p:p + 1], None, ALU.mult)
                elif step == "o":
                    core_wait(dve, "pe", "o1", g)
                    core_wait(dve, "dve", "t1", g)
                    if g >= 2:
                        core_wait(dve, "dve", "yl", g - 2)
                    for hd in range(2):
                        p = 4 * g + 2 * hd
                        nc.vector.tensor_scalar(buf("o")[:, 2 * hd, :], bank(2)[:, 2 * hd, :],
                                                pair[:, 9, p:p + 1], None, ALU.mult)
                        ins = nc.vector.scalar_tensor_tensor(
                            out=buf("o")[:, 2 * hd + 1, :], in0=bank(2)[:, 2 * hd + 1, :],
                            scalar=pair[:, 9, p + 1:p + 2], in1=buf("t1")[:, hd, :], op0=ALU.mult, op1=ALU.add)
                elif step == "on":
                    core_wait(dve, "pool", "orstd", g)
                    ins = nc.vector.tensor_tensor(
                        buf("o"), buf("o"), oss[:, 2, 4 * g:4 * g + 4].unsqueeze(2).broadcast_to([P, 4, P]), ALU.mult)
                elif step == "y":
                    core_wait(dve, "pe", "oT", g)
                    ins = nc.vector.scalar_tensor_tensor(
                        out=buf("y").rearrange("p a n -> p (a n)"), in0=bank(3).rearrange("p a n -> p (a n)"),
                        scalar=og[:, 0:1], in1=wk(W_Z + 2 * g * T, 2 * T), op0=ALU.mult, op1=ALU.mult)
                elif step == "yh":
                    core_wait(dve, "dve", "y", g)
                    ins = nc.vector.tensor_copy(yh[:, 2 * g:2 * g + 2, :].rearrange("p a n -> p (a n)"),
                                                buf("y").rearrange("p a n -> p (a n)"))
                else:
                    core_wait(dve, "dve", "yh", g)
                    ins = nc.vector.tensor_tensor(yl[:, 2 * g:2 * g + 2, :].rearrange("p a n -> p (a n)"),
                                                  buf("y").rearrange("p a n -> p (a n)"),
                                                  yh[:, 2 * g:2 * g + 2, :].bitcast(F32).rearrange("p a n -> p (a n)"),
                                                  ALU.subtract)
                ins.then_inc(core["dve"], 1)

            splits(U_DNO, KC - 1)
            residual(4)
            pre(5, [(G_M0, xh, xl)])
            last_split(U_DNO)
            relu2(0)
            residual(5)
            pre(6, [(G_X1, xh, xl)])
            for n in range(2 * NHD + KC):
                split(U_MBV + n + AHEAD)
            heads(NH // 2, NHD // 2, False)
            splits(U_MBO, KC - 1)
            residual(6)
            pre(7, [(G_M1, xh, xl)])
            last_split(U_MBO)
            relu2(1)
            residual(7)
            dve.wait_ge(gpost_loaded[0], 16 * 3)
            for t in range(NT):
                q = 16 + t
                dve.wait_ge(pre_rstd, q + 1)
                nc.vector.scalar_tensor_tensor(out=xn[:, t, :], in0=h[:, t, :], scalar=rstd[:, 2 * q:2 * q + 1],
                                               in1=gpost[:, 0, :], op0=ALU.mult, op1=ALU.mult).then_inc(out_ready, 1)

        @block.tensor
        def _(pe):
            mm = nc.tensor.matmul

            def take(us, i=None):
                pe.wait_ge(lo_ready, val(us + 1, i, BODY))

            def feature_chunk(us, i, ps, hi, lo):
                take(us, i)
                wh = w_hi[:, us % RING, :].rearrange("p (k n) -> p k n", k=KC)
                wl = w_lo[:, us % RING, :].rearrange("p (k n) -> p k n", k=KC)
                for k in range(KC):
                    mm(ps, wh[:, k, :], hi[:, k, :], start=(k == 0), stop=False)
                    mm(ps, wh[:, k, :], lo[:, k, :], start=False, stop=False)
                    ins = mm(ps, wl[:, k, :], hi[:, k, :], start=False, stop=(k == KC - 1))
                ins.then_inc(unit_used, 1)
                return ins

            def row_bank(us, t, half, hi, lo, first, last):
                cols = slice(512 * half, 512 * half + 512)
                wh, wl = w_hi[:, us % RING, cols], w_lo[:, us % RING, cols]
                th, tl = hi[:, t * P:(t + 1) * P], lo[:, t * P:(t + 1) * P]
                ps = acc[:, 2 * t + half, :]
                mm(ps, th, wh, start=first, stop=False)
                mm(ps, th, wl, start=False, stop=False)
                return mm(ps, tl, wh, start=False, stop=last)

            def row_tile(us, t, hi, lo, first, last):
                row_bank(us, t, 0, hi, lo, first, last)
                return row_bank(us, t, 1, hi, lo, first, last)

            def row_unit(us, i, hi, lo, first, last):
                take(us, i)
                for t in range(NT):
                    ins = row_tile(us, t, hi, lo, first, last)
                ins.then_inc(unit_used, 1)

            def finish(us, operands, waits, part_done):
                last = len(operands) - 1
                order = [(q, n) for q in range(2) for n in range(last + 1)]
                if waits:
                    order.sort(key=lambda qn: qn[1])
                order += [(q, n) for q in range(2, 4) for n in range(last + 1)]
                taken = set()
                for q, n in order:
                    hi, lo = operands[n]
                    if n not in taken:
                        taken.add(n)
                        take(us + n)
                        if waits:
                            pe.wait_ge(hid_ready, waits[n])
                    ins = row_bank(us + n, q // 2, q % 2, hi, lo, False, n == last)
                    if q == 3:
                        ins.then_inc(unit_used, 1)
                    elif n == last:
                        ins.then_inc(part_done, 1)

            def project_out(u0, hi, lo, sem_, value):
                for k in range(KC - 3):
                    pe.wait_ge(sem_, value(k))
                    row_unit(u0 + k, None, hi[:, k, :], lo[:, k, :], k == 0, False)
                pe.wait_ge(sem_, value(KC - 1))
                finish(u0 + KC - 3, [(hi[:, k, :], lo[:, k, :]) for k in range(KC - 3, KC)], None, acc_part)

            def stay_busy(n, bank=hp[:, 3, :]):
                for _ in range(n):
                    mm(bank, ident, const[:, 0:512], start=True, stop=True)

            def pre(n, sets=1):
                if n:
                    stay_busy(3)
                for t in range(NT):
                    pre_turn(n, t)
                pre.ready += 4 * sets

            def pre_turn(n, t):
                pe.wait_ge(diag_ready, 2 * n + t + 1)
                for half in range(2):
                    for k in range(4):
                        c = (4 * half + k) * P
                        ins = mm(hp[:, 2 * t + half, k * P:(k + 1) * P], h[:, t, c:c + P], diag[:, t, :],
                                 start=True, stop=True)
                    ins.then_inc(xT_ps, 1)
            pre.ready = 0

            def first_pair(us, banks):
                for half in range(2):
                    for part in range(2):
                        pe.wait_ge((xhi_ready, xT_ready)[part], pre.ready - 1 + half)
                        for n, ps in enumerate(banks):
                            if half == 0 and part == 0:
                                take(us + n)
                            wh = w_hi[:, (us + n) % RING, :].rearrange("p (k n) -> p k n", k=KC)
                            wl = w_lo[:, (us + n) % RING, :].rearrange("p (k n) -> p k n", k=KC)
                            for k in range(4 * half, 4 * half + 4):
                                if part == 0:
                                    mm(ps, wh[:, k, :], xh[:, k, :], start=(k == 0), stop=False)
                                    mm(ps, wl[:, k, :], xh[:, k, :], start=False, stop=False)
                                else:
                                    ins = mm(ps, wh[:, k, :], xl[:, k, :], start=False, stop=(k == KC - 1))
                            if half == 1 and part == 1:
                                ins.then_inc(unit_used, 1)

            pe.wait_ge(early_loaded, 16 * 9)
            nc.tensor.transpose(acc[:, 0, 0:96], rows[:, 0, :], const[0:96, C_ID:C_ID + 96])
            nc.tensor.transpose(acc[:, 1, 0:96], rows[:, 1, :], const[0:96, C_ID:C_ID + 96]).then_inc(rows_T, 1)
            pe.wait_ge(gains_ready, 1)
            pre(0)

            def mixer(js, i):
                us = U_MIX + 3 * js
                if js >= 2 or i is not None:
                    pe.wait_ge(y_ready, val(js - 1, i, 2))
                if js == 0 and i is None:
                    first_pair(us, [mix_psum(0, 0), mix_psum(0, 1)])
                for kind in range(2 if js == 0 and i is None else 0, 3):
                    feature_chunk(us + kind, i, mix_psum(js, kind), xh, xl)
            for js in range(2):
                mixer(js, None)
            turns(pe, 2, KC - 2, 2, mixer)
            project_out(U_MIXO, yh, yl, y_ready, lambda k: max(k + 1, KC - 1))
            pre(1)

            def down(us, i, js, cb, ring, first=False):
                pe.wait_ge(hid_ready, val(cb + js + 1, i, ring))
                row_unit(us, i, hh[:, js % ring, :], hl[:, js % ring, :], first, False)

            def last_downs(us, js, cb, ring):
                finish(us, [(hh[:, (js + n) % ring, :], hl[:, (js + n) % ring, :]) for n in range(2)],
                       [cb + js + 1, cb + js + 2], acc_part)

            def swiglu(layer):
                u0, cb = U_FF[layer], NF * layer

                def gate_up(us, i, js):
                    for n in range(2):
                        feature_chunk(us + n, i, hp[:, 2 * (js % 2) + n, 0:T], xh, xl)

                def step(js, i):
                    us = u0 + 2 + 3 * js
                    gate_up(us, i, js + 1)
                    down(us + 2, i, js, cb, 2, first=(js == 0))
                first_pair(u0, [hp[:, n, 0:T] for n in range(2)])
                step(0, None)
                turns(pe, 1, NF - 3, 2, step)
                gate_up(u0 + 3 * NF - 4, None, NF - 1)
                last_downs(u0 + 3 * NF - 2, NF - 2, cb, 2)

            def relu2(layer):
                u0, cb = U_MLP[layer], 2 * NF + NM * layer

                def up(us, i, js):
                    feature_chunk(us, i, hp[:, js % 3, 0:T], xh, xl)

                def step(js, i):
                    us = u0 + 2 + 2 * js
                    up(us, i, js + 2)
                    down(us + 1, i, js, cb, 3, first=(js == 0))
                first_pair(u0, [hp[:, n, 0:T] for n in range(2)])
                step(0, None)
                turns(pe, 1, NM - 3, 3, step)
                last_downs(u0 + 2 * NM - 2, NM - 2, cb, 3)

            def heads(first, n, sink):
                dh = HD if sink else DH

                def qk(hd):
                    if sink:
                        rows_ = slice(HD * (hd % 2), HD * (hd % 2) + HD)
                        q_at, k_at = W_QT + (hd // 2) * T, W_KT + (hd // 4) * T
                        return work[rows_, q_at:q_at + T], work[rows_, k_at:k_at + T]
                    return wk(W_MQK + hd * T, T), wk(W_MQK + (NHD + hd) * T, T)

                def scores(k):
                    i = first + k
                    if i >= 2:
                        pe.wait_ge(s_made, i - 1)
                    if not sink and k < NT:
                        pe.wait_ge(mbv_copied, k + 1)
                    for hd in range(2):
                        q, key = qk(2 * k + hd)
                        ps = acc[:, 2 * (i % 2) + hd, :]
                        mm(ps[:, 0:P], q[:, 0:P], key[:, 0:P], start=True, stop=True)
                        ins = mm(ps[:, P:384], q[:, P:T], key, start=True, stop=True)
                    ins.then_inc(sc_done, 1)

                def turn_out(half, made):
                    pe.wait_ge(o_made, made)
                    for t in range(NT):
                        for k in range(4):
                            c = (4 * half + k) * P
                            ins = nc.tensor.transpose(out_psum(half, t)[:, k, :], xn[:, t, c:c + P], ident)
                        ins.then_inc(oT_ps, 1)

                def turn(k):
                    i = first + k
                    pe.wait_ge(p_ready, i + 1)
                    if i >= 1:
                        pe.wait_ge(pt_ready, i)
                    for hd in range(2):
                        for b in range(3):
                            ins = nc.tensor.transpose(hp[:, hd, b * P:(b + 1) * P],
                                                      score_buf(i)[:, hd, b * P:(b + 1) * P], ident)
                    ins.then_inc(pt_ps, 1)

                def values(k):
                    i = first + k
                    pe.wait_ge(pt_ready, i + 1)
                    if i >= 2:
                        pe.wait_ge(o_made, i - 1)
                    for hd in range(2):
                        n_hd = 2 * k + hd
                        pt = pt_buf(i)[:, hd, :]
                        v = [wk((W_V + t * 256 + (n_hd // 4) * HD) if sink else (W_MV + t * D + n_hd * DH), dh)
                             for t in range(NT)]
                        o = [hp[:, 2 + i % 2, (2 * t + hd) * dh:(2 * t + hd + 1) * dh] for t in range(NT)]
                        mm(o[0], pt[:, 0:P], v[0], start=True, stop=True)
                        mm(o[1], pt[:, P:2 * P], v[0], start=True, stop=False)
                        ins = mm(o[1], pt[:, 2 * P:3 * P], v[1], start=False, stop=True)
                    ins.then_inc(pv_done, 1)
                for k in range(n + 3):
                    if k < n:
                        scores(k)
                    if k == 2:
                        stay_busy(2)
                    if 2 <= k < n + 2:
                        turn(k - 2)
                    if k >= 3:
                        values(k - 3)
                    if k == n + 1:
                        pe.wait_ge(s_made, first + n)
                        turn_out(0, first + n // 2)
                u0, base = (U_O, 0) if sink else (U_MBO, 4)
                stay_busy(1, acc[:, 3, :])
                for k in range(KC - 3):
                    pe.wait_ge(oT_ready, base + (2 if k < 4 else 4))
                    row_unit(u0 + k, None, xh[:, k, :], xl[:, k, :], k == 0, False)
                    if k == 0:
                        turn_out(1, first + n)
                finish(u0 + KC - 3, [(xh[:, k, :], xl[:, k, :]) for k in range(KC - 3, KC)], None, acc_part)

            swiglu(0)
            def kv_unit(n, t):
                us = U_KV + n
                if t == 0:
                    take(us)
                pe.wait_ge(xT_ready, pre.ready + 2 * t + n // 2 + 1)
                for k in range(2 * n, 2 * n + 2):
                    cols, rows_ = slice(512 * (k % 2), 512 * (k % 2) + 512), slice(t * P, (t + 1) * P)
                    mm(acc[:, 2 + t, :], xh[:, k, rows_], w_hi[:, us % RING, cols], start=(k == 0), stop=False)
                    mm(acc[:, 2 + t, :], xh[:, k, rows_], w_lo[:, us % RING, cols], start=False, stop=False)
                    ins = mm(acc[:, 2 + t, :], xl[:, k, rows_], w_hi[:, us % RING, cols], start=False, stop=(k == KC - 1))
                return ins
            stay_busy(3)
            pre_turn(2, 0)
            kv_unit(0, 0)
            kv_unit(1, 0)
            pre_turn(2, 1)
            kv_unit(2, 0)
            kv_unit(3, 0)
            for n in range(4):
                kv_unit(n, 1).then_inc(unit_used, 1)
            pre.ready += 8
            take(U_Q)
            pe.wait_ge(xT_ready, pre.ready - 1)
            row_tile(U_Q, 0, yh[:, 0, :], yl[:, 0, :], True, False)
            pe.wait_ge(kv_copied, NT)
            row_tile(U_Q, 1, yh[:, 0, :], yl[:, 0, :], True, False).then_inc(unit_used, 1)
            for k in range(1, KC - 3):
                pe.wait_ge(xT_ready, pre.ready - 1 + k // 4)
                row_unit(U_Q + k, None, yh[:, k, :], yl[:, k, :], False, False)
            finish(U_Q + KC - 3, [(yh[:, k, :], yl[:, k, :]) for k in range(KC - 3, KC)], None, qv_part)
            for t in range(NT):
                pe.wait_ge(k_dup, t + 2)
                for g in range(NKV):
                    at = W_KDUP + t * 512 + g * P
                    ins = nc.tensor.transpose(hp[:, 2 + t, g * P:(g + 1) * P], wk(at, P), ident)
                ins.then_inc(kT_ps, 1)
            for t in range(NT):
                pe.wait_ge(rot_done, 2 * (2 + t + 1))
                if t == 1:
                    pe.wait_ge(kT_copied, NT)
                for half in range(2):
                    for k in range(4):
                        at = W_QTOK + t * D + (4 * half + k) * P
                        ins = nc.tensor.transpose(hp[:, 2 * t + half, k * P:(k + 1) * P], wk(at, P), ident)
                    ins.then_inc(qT_ps, 1)
            pe.wait_ge(qT_copied, 4)
            heads(0, NH // 2, True)
            pre(3)
            swiglu(1)
            pre(4)

            def gate_inputs(t):
                pe.wait_ge(wba_step, 2)
                pe.wait_ge(xT_ready, pre.ready)
                ps = acc[:, 0, 32 * t:32 * t + 32]
                rows_ = slice(t * P, (t + 1) * P)
                for k in range(KC):
                    mm(ps, xh[:, k, rows_], wba_split[:, k, :, :].rearrange("p s n -> p (s n)"),
                       start=(k == 0), stop=False)
                    ins = mm(ps[:, 0:16], xl[:, k, rows_], wba_split[:, k, 0, :], start=False, stop=(k == KC - 1))
                ins.then_inc(ba_ps, 1)

            def decays():
                pe.wait_ge(ba_step, BA_G)
                mm(acc[:, 2, 0:16], const[:, C_INCL:C_INCL + P], pair[:, 3, :], start=True, stop=True)
                mm(acc[:, 2, 16:32], const[:, C_STRICT:C_STRICT + P], pair[:, 3, :], start=True, stop=True) \
                    .then_inc(gc_ps, 1)

            def row_sums(part):
                pe.wait_ge(qk_sq, part + 1)
                for c in range(8 * part, 8 * part + 8):
                    ins = mm(acc[:, 1, c:c + 1], wk(W_SQ + c * P, P), const[:, C_ONE:C_ONE + 1], start=True, stop=True)
                ins.then_inc(qk_ps, 1)

            def dn_chunk(js, i):
                if js >= 3 or i is not None:
                    pe.wait_ge(conv_in, val(js - 2, i, BODY))
                feature_chunk(U_DN + js, i, small_psum(js % 3), xh, xl)
            first_pair(U_DN, [small_psum(0), small_psum(1)])
            gate_inputs(0)
            for js in range(2, BODY):
                dn_chunk(js, None)
                if js == 2:
                    gate_inputs(1)
            turns(pe, BODY, 24 - BODY, BODY, dn_chunk)
            decays()
            for j in range(24, 32):
                if j < 27:
                    pe.wait_ge(conv_in, j - 2)
                else:
                    pe.wait_ge(z_ready, j - 26)
                feature_chunk(U_DN + j, None, small_psum(j % 3), xh, xl)
                if j < 28:
                    row_sums(j - 24)
            pe.wait_ge(conv_silu, 24)
            pe.wait_ge(z_ready, 8)
            pe.wait_ge(ba_step, BA_SUMS)

            for e, step, g in CORE_ORDER:
                if e != "pe":
                    continue
                bank = lambda b: core_bank(g, b)
                buf = lambda name: core_buf(g, name)

                def qT(p):
                    return qkvT(2 * g + p // 2)[:, (p % 2) * P:(p % 2 + 1) * P]

                def chunk_of(kind, p):
                    return qkvT(kind * NHD + 2 * g + p // 2)[:, (p % 2) * P:(p % 2 + 1) * P]
                pairs = range(4)
                if step == "kvT":
                    for p in pairs:
                        nc.tensor.transpose(bank(0)[:, p, :], chunk_of(1, p), ident)
                    for p in pairs:
                        ins = nc.tensor.transpose(bank(1)[:, p, :], chunk_of(2, p), ident)
                elif step == "decay":
                    core_wait(pe, "pool", "gs", g)
                    if g >= 2:
                        core_wait(pe, "dve", "o", g - 2)
                    if g == 0:
                        pe.wait_ge(ba_act, 3)
                    for p in pairs:
                        ins = mm(bank(2)[:, p, :], buf("gs")[:, p, :], const[:, C_INCL:C_INCL + P], start=True, stop=True)
                elif step == "knT":
                    core_wait(pe, "dve", "kscale", g)
                    for p in pairs:
                        nc.tensor.transpose(bank(0)[:, p, :], buf("kn")[:, p, :], ident)
                    for p in pairs:
                        ins = nc.tensor.transpose(bank(1)[:, p, :], buf("kb")[:, p, :], ident)
                elif step == "scores":
                    core_wait(pe, "act", "knT_copy", g)
                    core_wait(pe, "act", "dec", g)
                    if g >= 2:
                        core_wait(pe, "dve", "y", g - 2)
                    for p in pairs:
                        mm(bank(2)[:, p, :], buf("knT")[:, p, :], qT(p), start=True, stop=True)
                        ins = mm(bank(3)[:, p, :], buf("knT")[:, p, :], buf("kbT")[:, p, :], start=True, stop=True)
                elif step == "xT":
                    if g % 2 == 0:
                        stay_busy(1, acc[:, 0, :])
                    core_wait(pe, "dve", "z0", g)
                    for p in pairs:
                        ins = nc.tensor.transpose(bank(0)[:, p, :], buf("Z")[:, p, :], ident)
                elif step[0] == "y":
                    n = int(step[1:])
                    if n == 1:
                        core_wait(pe, "act", "x_copy", g)
                    else:
                        core_wait(pe, "dve", f"x{n - 1}", g)
                    for p in pairs:
                        ins = mm(bank(0)[:, p, :], buf("B")[:, p, :], buf("X")[:, p, :], start=True, stop=True)
                elif step.startswith("zT"):
                    core_wait(pe, "dve", f"x{int(step[2:])}", g)
                    for p in pairs:
                        ins = nc.tensor.transpose(bank(2)[:, p, :], buf("X")[:, p, :], ident)
                elif step[0] == "d" and step != "decay":
                    n = int(step[1:])
                    core_wait(pe, "act", f"y{n}_copy", g)
                    if n > 1:
                        core_wait(pe, "dve", f"zT{n - 1}_copy", g)
                    for p in pairs:
                        if n < LEVELS - 1:
                            ins = mm(bank(1)[:, p, :], buf("Z")[:, p, :], buf("Y")[:, p, :], start=True, stop=True)
                        else:
                            ins = mm(bank(1)[:, p, :], buf("Y")[:, p, :], buf("Z")[:, p, :], start=True, stop=True)
                elif step == "vn0":
                    core_wait(pe, "dve", "z_last", g)
                    for hd in range(2):
                        ins = mm(bank(0)[:, hd, :], buf("Z")[:, 2 * hd, :], buf("vb")[:, 2 * hd, :], start=True, stop=True)
                elif step == "state":
                    core_wait(pe, "act", "vn0_copy", g)
                    for hd in range(2):
                        ins = mm(bank(1)[:, hd, :], buf("kd")[:, 2 * hd, :], buf("vn")[:, 2 * hd, :], start=True, stop=True)
                elif step == "o0":
                    for hd in range(2):
                        ins = mm(bank(2)[:, 2 * hd, :], buf("attnT")[:, 2 * hd, :], buf("vn")[:, 2 * hd, :],
                                 start=True, stop=True)
                elif step == "kqs":
                    core_wait(pe, "act", "state_copy", g)
                    for hd in range(2):
                        mm(bank(3)[:, hd, :], buf("knT")[:, 2 * hd + 1, :], buf("SR")[:, hd, :], start=True, stop=True)
                        ins = mm(bank(3)[:, 2 + hd, :], qT(2 * hd + 1), buf("SR")[:, hd, :], start=True, stop=True)
                elif step == "vn1":
                    core_wait(pe, "dve", "rhs1", g)
                    for hd in range(2):
                        ins = mm(bank(0)[:, 2 + hd, :], buf("Z")[:, 2 * hd + 1, :], buf("SR")[:, 2 + hd, :],
                                 start=True, stop=True)
                elif step == "o1":
                    core_wait(pe, "act", "vn1_copy", g)
                    for hd in range(2):
                        ins = mm(bank(2)[:, 2 * hd + 1, :], buf("attnT")[:, 2 * hd + 1, :], buf("vn")[:, 2 * hd + 1, :],
                                 start=True, stop=True)
                else:
                    if g == 2:
                        core_wait(pe, "dve", "yl", 1)
                        for k in range(4):
                            take(U_DNO + k)
                            row_tile(U_DNO + k, 0, yh[:, k, :], yl[:, k, :], k == 0, False)
                    core_wait(pe, "dve", "on", g)
                    for p in pairs:
                        ins = nc.tensor.transpose(bank(3)[:, p, :], buf("o")[:, p, :], ident)
                ins.then_inc(core["pe"], 1)

            core_wait(pe, "dve", "yl", 2)
            for k in range(4):
                row_tile(U_DNO + k, 1, yh[:, k, :], yl[:, k, :], k == 0, False).then_inc(unit_used, 1)
            row_unit(U_DNO + 4, None, yh[:, 4, :], yl[:, 4, :], False, False)
            core_wait(pe, "dve", "yl", 3)
            finish(U_DNO + 5, [(yh[:, k, :], yl[:, k, :]) for k in range(5, KC)], None, acc_part)
            pre(5)
            relu2(0)
            def mb_chunk(js, i):
                if js >= 3 or i is not None:
                    pe.wait_ge(mb_copied, val(js - 2, i, BODY))
                feature_chunk(U_MB + js, i, small_psum(js % 3), xh, xl)
            def v_tile(k, t):
                if t == 0:
                    take(U_MBV + k)
                pe.wait_ge(xT_ready, pre.ready + 2 * t + k // 4 + 1)
                return row_tile(U_MBV + k, t, xh[:, k, :], xl[:, k, :], k == 0, k == KC - 1)
            stay_busy(3)
            pre_turn(6, 0)
            v_tile(0, 0)
            v_tile(1, 0)
            pre_turn(6, 1)
            v_tile(2, 0)
            for k in range(3):
                v_tile(k, 1).then_inc(unit_used, 1)
            for k in range(3, KC):
                v_tile(k, 0)
                v_tile(k, 1).then_inc(unit_used, 1)
            pre.ready += 4
            for js in range(3):
                mb_chunk(js, None)
            turns(pe, 3, 2 * NHD - 3, BODY, mb_chunk)
            pe.wait_ge(mb_copied, 2 * NHD)
            heads(NH // 2, NHD // 2, False)
            pre(7)
            relu2(1)


_INS = ["x", "a_pre_norm", "a_w_in", "a_conv_w", "a_w_out", "a_post_norm", "ffn_pre_norm", "ffn_w_gate_up",
        "ffn_w_down", "ffn_post_norm", "kv_norm", "w_kv", "b_pre_norm", "b_w_q", "b_sinks", "b_w_o", "b_post_norm",
        "mix_norm_g_2", "mlp_norm_g_2", "dn_w_in_2", "dn_conv_w_2", "dn_a_log_2", "dn_dt_bias_2",
        "dn_out_norm_g_2", "dn_w_out_2", "mb_w_in_2", "mb_w_out_2", "mlp_w_up_2", "mlp_w_down_2", "final_norm_g_2"]


def constants():
    import numpy as np
    j, i = np.arange(P)[:, None], np.arange(P)[None, :]
    q, k = j, np.arange(T)[None, :]
    c = np.zeros((P, N_CONST), np.float32)
    c[:, C_ID:C_ID + P] = j == i
    c[:, C_INCL:C_INCL + P] = j <= i
    c[:, C_STRICT:C_STRICT + P] = j > i
    c[:, C_NEG:C_NEG + P] = -1.0 * (i > j)
    c[:, C_ONE] = 1.0
    c[:, C_BAND:C_BAND + P] = np.where(i <= j, 0.0, -1e30)
    c[:, C_BAND + P:C_BAND + 3 * P] = np.where((k <= q + P) & (k > q + P - 128), 0.0, -1e30)
    c[:, C_DIST:C_DIST + P] = np.where(i <= j, i - j, -1e30)
    c[:, C_DIST + P:C_DIST + 3 * P] = np.where(k <= q + P, k - q - P, -1e30)
    inv_freq = np.float32(500000.0) ** (-np.arange(0, 2 * ROT, 2, dtype=np.float32) / np.float32(2 * ROT))
    angle = (np.arange(T, dtype=np.float32)[:, None] * inv_freq[None, :]).reshape(NT, P, ROT).transpose(1, 0, 2)
    c[:, C_COS:C_COS + NT * ROT] = np.cos(angle).reshape(P, -1)
    c[:, C_SIN:C_SIN + NT * ROT] = np.sin(angle).reshape(P, -1)
    masks = np.zeros((P, 2 * LEVELS, P), np.float32)
    for n in range(LEVELS):
        b = 2 ** n
        low = (j // (2 * b) == i // (2 * b)) & (j % (2 * b) >= b) & (i % (2 * b) < b)
        masks[:, 2 * n, :] = low
        masks[:, 2 * n + 1, :] = low.T
    return c, masks


def kernel(**inputs):
    import numpy as _np
    import concourse.bacc as _bacc
    from concourse import mybir as _mybir
    from concourse.bass_utils import run_bass_kernel_spmd as _run

    nc = _bacc.Bacc("TRN2", target_bir_lowering=False, num_devices=1)
    arrays, args = {}, {}
    consts, masks = constants()
    given = {name: _np.ascontiguousarray(inputs[name]) for name in _INS}
    given["consts"], given["masks"] = consts, masks
    for name, v in given.items():
        arrays[f"in_{name}_dram"] = v
        args[name] = nc.dram_tensor(f"in_{name}_dram", v.shape, _mybir.dt.from_np(v.dtype), kind="ExternalInput").ap()
    out = nc.dram_tensor("out_0_dram", (1, T, D), F32, kind="ExternalOutput").ap()
    build(nc, args, out)
    r = _run(nc, [arrays], core_ids=[0])
    return r.results[0]["out_0_dram"]
```
